# Optimizing a Trainium2 kernel written in Bass

```python
import math
import jax
import jax.numpy as jnp
from jax import lax
import numpy as np

D_MODEL = 1024
BATCH = 1
SEQ = 256
DEPTH = 2

GRID_W = 64
CTX_LEN = 256
N_BRANCH = 4
WA = 256
CONF_K = 31
NA_HEADS = 4
NA_HEAD_DIM = 64
WB = NA_HEADS * NA_HEAD_DIM
NA_WIN_ROWS = 8
NA_WIN_COLS = 16
ATTN_SCALE = NA_HEAD_DIM ** -0.5
WC = 256
SC_K = 3
WD = 256
HY_ORDER = 2
HY_SHORT_K = 3
HY_PE_BANDS = 16
HY_PE_DIM = 1 + 2 * HY_PE_BANDS
HY_FILT_HID = 64
HY_FAST_DECAY = 0.3
HY_SLOW_DECAY = 1.5
HY_DECAY_TARGET = 1e-2
D_FF = 2816
N_MOD = 9
LN_EPS = 1e-5
ALPHA = (2 * DEPTH) ** 0.25
BETA = (8 * DEPTH) ** -0.25

OFF_A = 0
OFF_Q = OFF_A + 2 * WA
OFF_K = OFF_Q + WB
OFF_V = OFF_K + WB
OFF_SB = OFF_V + WB
OFF_SC = OFF_SB + WC
OFF_SX = OFF_SC + WC
OFF_HV = OFF_SX + WC
OFF_G = OFF_HV + (1 + HY_ORDER) * WD
P_IN = OFF_G + N_BRANCH * D_MODEL

kernel_name = 'hybrid_conv_na_hyena_diffusion_block'

def layer_norm(x, g=None, b=None):
    xf = x.astype(jnp.float32)
    mu = jnp.mean(xf, -1, keepdims=True)
    var = jnp.mean(jnp.square(xf - mu), -1, keepdims=True)
    y = (xf - mu) * lax.rsqrt(var + LN_EPS)
    if g is not None:
        y = y * g.astype(jnp.float32) + b.astype(jnp.float32)
    return y.astype(x.dtype)

def modulate(x, shift, scale):
    return layer_norm(x) * (1.0 + scale) + shift

def post_norm(x, sub, g, b):
    return layer_norm(ALPHA * x + sub, g, b)

def swiglu(h, w_in, w_out):
    a, g = jnp.split(h @ w_in, 2, axis=-1)
    return (jax.nn.silu(g) * a) @ w_out

def depthwise_conv(u, w, b=None):
    k = w.shape[0]
    y = lax.conv_general_dilated(u, w[:, None, :].astype(u.dtype), window_strides=(1,),
                                 padding=[(k // 2, k // 2)],
                                 dimension_numbers=('NWC', 'WIO', 'NWC'),
                                 feature_group_count=u.shape[-1])
    if b is not None:
        y = y + b
    return y

def heads(t):
    return t.reshape(*t.shape[:-1], NA_HEADS, NA_HEAD_DIM)

def conformer_conv(u2, dw_w, dw_b, ln_g, ln_b, w_proj):
    a, g = jnp.split(u2, 2, axis=-1)
    u = depthwise_conv(a * jax.nn.sigmoid(g), dw_w, dw_b)
    return jax.nn.silu(layer_norm(u, ln_g, ln_b)) @ w_proj

def short_gated_conv(gate_b, gate_c, u, conv_w, w_proj):
    return (gate_b * depthwise_conv(gate_c * u, conv_w)) @ w_proj

def hyena_filters(length, w1, b1, w2, b2, freq, w3):
    t = jnp.arange(length, dtype=jnp.float32)
    t_norm = t / max(length - 1, 1)
    bands = jnp.linspace(1e-4, HY_PE_BANDS - 1, HY_PE_BANDS, dtype=jnp.float32)
    ang = (2.0 * math.pi / length) * t[:, None] * bands[None, :]
    z = jnp.concatenate([t_norm[:, None], jnp.cos(ang), -jnp.sin(ang)], axis=-1)
    h = jnp.sin(freq[0] * (z @ w1 + b1))
    h = jnp.sin(freq[1] * (h @ w2 + b2))
    h = (h @ w3).astype(jnp.float32).reshape(length, HY_ORDER, 2, WD)
    deltas = jnp.linspace(math.log(HY_DECAY_TARGET) / HY_SLOW_DECAY,
                          math.log(HY_DECAY_TARGET) / HY_FAST_DECAY, WD, dtype=jnp.float32)
    decay = jnp.exp(-t_norm[:, None] * jnp.abs(deltas)[None, :])
    return h * decay[:, None, None, :]

def bidirectional_fft_conv(u, h_fwd, h_bwd, bias):
    length = u.shape[1]
    n = 2 * length
    k = jnp.concatenate([h_fwd, jnp.zeros_like(h_fwd[:1]), h_bwd[1:][::-1]], axis=0)
    k = k * lax.rsqrt(jnp.sum(jnp.square(k), axis=0, keepdims=True) + 1e-6)
    uf = u.astype(jnp.float32)
    spec = jnp.fft.rfft(uf, n=n, axis=1) * jnp.fft.rfft(k, n=n, axis=0)[None]
    y = jnp.fft.irfft(spec, n=n, axis=1)[:, :length]
    return (y + uf * bias.astype(jnp.float32)).astype(u.dtype)

def hyena_mixer(u3, sconv_w, sconv_b, filt, bias, w_proj):
    parts = jnp.split(depthwise_conv(u3, sconv_w, sconv_b), 1 + HY_ORDER, axis=-1)
    z = parts[0]
    for o in range(HY_ORDER):
        z = parts[1 + o] * bidirectional_fft_conv(z, filt[:, o, 0], filt[:, o, 1], bias[o])
    return z @ w_proj

def neighbourhood_attention(q, k, v, kc, vc, rpb):
    bsz, n_tok, n_h, dh = q.shape
    rows = n_tok // GRID_W
    wr = min(NA_WIN_ROWS, rows)
    wc = NA_WIN_COLS
    qg = (q * ATTN_SCALE).reshape(bsz, rows, GRID_W, n_h, dh).transpose(1, 0, 2, 3, 4)
    kg = k.reshape(bsz, rows, GRID_W, n_h, dh)
    vg = v.reshape(bsz, rows, GRID_W, n_h, dh)
    cols = jnp.arange(GRID_W)
    c0 = jnp.clip(cols - wc // 2, 0, GRID_W - wc)
    col_idx = c0[:, None] + jnp.arange(wc)[None, :]
    dc = col_idx - cols[:, None] + (NA_WIN_COLS - 1)

    def row_fn(args):
        r, q_row = args
        r0 = jnp.clip(r - wr // 2, 0, rows - wr)
        k_nb = lax.dynamic_slice_in_dim(kg, r0, wr, axis=1)[:, :, col_idx]
        v_nb = lax.dynamic_slice_in_dim(vg, r0, wr, axis=1)[:, :, col_idx]
        dr = r0 + jnp.arange(wr) - r + (NA_WIN_ROWS - 1)
        bias = rpb[:, dr[None, :, None], dc[:, None, :]]
        s_nb = jnp.einsum('bqhd,brqjhd->bhqrj', q_row, k_nb).astype(jnp.float32) + bias.astype(jnp.float32)
        s_ctx = jnp.einsum('bqhd,bkhd->bhqk', q_row, kc).astype(jnp.float32)
        s = jnp.concatenate([s_nb.reshape(bsz, n_h, GRID_W, wr * wc), s_ctx], axis=-1)
        p = jax.nn.softmax(s, axis=-1).astype(v.dtype)
        p_nb = p[..., :wr * wc].reshape(bsz, n_h, GRID_W, wr, wc)
        p_ctx = p[..., wr * wc:]
        return (jnp.einsum('bhqrj,brqjhd->bqhd', p_nb, v_nb)
                + jnp.einsum('bhqk,bkhd->bqhd', p_ctx, vc))

    out = lax.map(row_fn, (jnp.arange(rows), qg))
    return out.transpose(1, 0, 2, 3, 4).reshape(bsz, n_tok, n_h * dh)

def context_attention(q, k, v):
    s = jnp.einsum('bqhd,bkhd->bhqk', q * ATTN_SCALE, k).astype(jnp.float32)
    p = jax.nn.softmax(s, axis=-1).astype(v.dtype)
    o = jnp.einsum('bhqk,bkhd->bqhd', p, v)
    return o.reshape(*o.shape[:2], WB)

def token_mixer(p, attn, filt, lw):
    ya = conformer_conv(p[..., OFF_A:OFF_Q], lw['conf_dw_w'], lw['conf_dw_b'],
                        lw['conf_ln_g'], lw['conf_ln_b'], lw['conf_w_proj'])
    yb = attn @ lw['na_w_proj']
    yc = short_gated_conv(p[..., OFF_SB:OFF_SC], p[..., OFF_SC:OFF_SX], p[..., OFF_SX:OFF_HV],
                          lw['sc_conv_w'], lw['sc_w_proj'])
    yd = hyena_mixer(p[..., OFF_HV:OFF_G], lw['hy_sconv_w'], lw['hy_sconv_b'], filt,
                     lw['hy_bias'], lw['hy_w_proj'])
    g = jax.nn.sigmoid(p[..., OFF_G:P_IN]).reshape(*p.shape[:-1], N_BRANCH, D_MODEL)
    m = g[..., 0, :] * ya + g[..., 1, :] * yb + g[..., 2, :] * yc + g[..., 3, :] * yd
    return m @ lw['w_out'] + lw['b_out']

def setup_inputs(seed: int = 0) -> dict:
    key = jax.random.key(seed)
    ks = iter(jax.random.split(key, 40))

    def nrm(shape, scale):
        return jax.random.normal(next(ks), shape, jnp.float32) * scale

    L = DEPTH
    return {
        'x': nrm((BATCH, SEQ, D_MODEL), 1.0),
        'c': nrm((BATCH, D_MODEL), 1.0),
        'ctx': nrm((BATCH, CTX_LEN, D_MODEL), 1.0),
        'c_ctx': nrm((D_MODEL,), 1.0),
        'w_mod': nrm((L, D_MODEL, N_MOD * D_MODEL), 0.5 * D_MODEL ** -0.5),
        'b_mod': nrm((L, N_MOD * D_MODEL), 0.01),
        'post_ln_g': 1.0 + nrm((L, 3, D_MODEL), 0.02),
        'post_ln_b': nrm((L, 3, D_MODEL), 0.02),
        'ffn_w_in': nrm((L, 2, D_MODEL, 2 * D_FF), D_MODEL ** -0.5),
        'ffn_w_out': nrm((L, 2, D_FF, D_MODEL), BETA * D_FF ** -0.5),
        'w_in': nrm((L, D_MODEL, P_IN), D_MODEL ** -0.5),
        'b_in': nrm((L, P_IN), 0.02),
        'conf_dw_w': nrm((L, CONF_K, WA), CONF_K ** -0.5),
        'conf_dw_b': nrm((L, WA), 0.02),
        'conf_ln_g': 1.0 + nrm((L, WA), 0.02),
        'conf_ln_b': nrm((L, WA), 0.02),
        'conf_w_proj': nrm((L, WA, D_MODEL), WA ** -0.5),
        'na_rpb': nrm((L, NA_HEADS, 2 * NA_WIN_ROWS - 1, 2 * NA_WIN_COLS - 1), 0.1),
        'na_w_proj': nrm((L, WB, D_MODEL), WB ** -0.5),
        'sc_conv_w': nrm((L, SC_K, WC), SC_K ** -0.5),
        'sc_w_proj': nrm((L, WC, D_MODEL), WC ** -0.5),
        'hy_sconv_w': nrm((L, HY_SHORT_K, (1 + HY_ORDER) * WD), HY_SHORT_K ** -0.5),
        'hy_sconv_b': nrm((L, (1 + HY_ORDER) * WD), 0.02),
        'hy_w1': nrm((L, HY_PE_DIM, HY_FILT_HID), HY_PE_DIM ** -0.5),
        'hy_b1': nrm((L, HY_FILT_HID), 0.02),
        'hy_w2': nrm((L, HY_FILT_HID, HY_FILT_HID), HY_FILT_HID ** -0.5),
        'hy_b2': nrm((L, HY_FILT_HID), 0.02),
        'hy_freq': 1.0 + nrm((L, 2, HY_FILT_HID), 0.1),
        'hy_w3': nrm((L, HY_FILT_HID, HY_ORDER * 2 * WD), HY_FILT_HID ** -0.5),
        'hy_bias': nrm((L, HY_ORDER, WD), 1.0),
        'hy_w_proj': nrm((L, WD, D_MODEL), WD ** -0.5),
        'w_out': nrm((L, D_MODEL, D_MODEL), BETA * D_MODEL ** -0.5),
        'b_out': nrm((L, D_MODEL), 0.02),
    }

def reference(x, c, ctx, c_ctx, w_mod, b_mod, post_ln_g, post_ln_b, ffn_w_in, ffn_w_out,
              w_in, b_in, conf_dw_w, conf_dw_b, conf_ln_g, conf_ln_b, conf_w_proj,
              na_rpb, na_w_proj, sc_conv_w, sc_w_proj, hy_sconv_w, hy_sconv_b,
              hy_w1, hy_b1, hy_w2, hy_b2, hy_freq, hy_w3, hy_bias, hy_w_proj, w_out, b_out):
    bsz, n_lat, _ = x.shape
    ctx_len = ctx.shape[1]
    s_lat = jax.nn.silu(c)
    s_ctx = jax.nn.silu(c_ctx)
    xc = ctx
    for l in range(DEPTH):
        last = l == DEPTH - 1
        lw = {
            'conf_dw_w': conf_dw_w[l], 'conf_dw_b': conf_dw_b[l], 'conf_ln_g': conf_ln_g[l],
            'conf_ln_b': conf_ln_b[l], 'conf_w_proj': conf_w_proj[l], 'na_w_proj': na_w_proj[l],
            'sc_conv_w': sc_conv_w[l], 'sc_w_proj': sc_w_proj[l], 'hy_sconv_w': hy_sconv_w[l],
            'hy_sconv_b': hy_sconv_b[l], 'hy_bias': hy_bias[l], 'hy_w_proj': hy_w_proj[l],
            'w_out': w_out[l], 'b_out': b_out[l],
        }
        mod_all = (s_lat @ w_mod[l] + b_mod[l]).reshape(bsz, N_MOD, 1, D_MODEL)
        mod = [mod_all[:, i] for i in range(N_MOD)]
        n_cm = 5 if last else N_MOD
        mod_c = (s_ctx @ w_mod[l][:, :n_cm * D_MODEL] + b_mod[l][:n_cm * D_MODEL]).reshape(n_cm, D_MODEL)

        x = post_norm(x, 0.5 * mod[2] * swiglu(modulate(x, mod[0], mod[1]), ffn_w_in[l, 0], ffn_w_out[l, 0]),
                      post_ln_g[l, 0], post_ln_b[l, 0])
        xc = post_norm(xc, 0.5 * mod_c[2] * swiglu(modulate(xc, mod_c[0], mod_c[1]), ffn_w_in[l, 0], ffn_w_out[l, 0]),
                       post_ln_g[l, 0], post_ln_b[l, 0])

        p = modulate(x, mod[3], mod[4]) @ w_in[l] + b_in[l]
        hc = modulate(xc, mod_c[3], mod_c[4])
        if last:
            kvc = hc @ w_in[l][:, OFF_K:OFF_SB] + b_in[l][OFF_K:OFF_SB]
        else:
            pc = hc @ w_in[l] + b_in[l]
            kvc = pc[..., OFF_K:OFF_SB]
        kc = heads(kvc[..., :WB])
        vc = heads(kvc[..., WB:])
        attn = neighbourhood_attention(heads(p[..., OFF_Q:OFF_K]), heads(p[..., OFF_K:OFF_V]),
                                       heads(p[..., OFF_V:OFF_SB]), kc, vc, na_rpb[l])
        filt = hyena_filters(n_lat, hy_w1[l], hy_b1[l], hy_w2[l], hy_b2[l], hy_freq[l], hy_w3[l])
        x = post_norm(x, mod[5] * token_mixer(p, attn, filt, lw), post_ln_g[l, 1], post_ln_b[l, 1])
        if not last:
            attn_c = context_attention(heads(pc[..., OFF_Q:OFF_K]), kc, vc)
            filt_c = hyena_filters(ctx_len, hy_w1[l], hy_b1[l], hy_w2[l], hy_b2[l], hy_freq[l], hy_w3[l])
            xc = post_norm(xc, mod_c[5] * token_mixer(pc, attn_c, filt_c, lw), post_ln_g[l, 1], post_ln_b[l, 1])

        x = post_norm(x, 0.5 * mod[8] * swiglu(modulate(x, mod[6], mod[7]), ffn_w_in[l, 1], ffn_w_out[l, 1]),
                      post_ln_g[l, 2], post_ln_b[l, 2])
        if not last:
            xc = post_norm(xc, 0.5 * mod_c[8] * swiglu(modulate(xc, mod_c[6], mod_c[7]), ffn_w_in[l, 1], ffn_w_out[l, 1]),
                           post_ln_g[l, 2], post_ln_b[l, 2])
    return x


_drawn_inputs = setup_inputs


def setup_inputs(seed=0):
    import zlib

    import numpy as np

    out = dict(_drawn_inputs(seed))
    spreads = {}
    factors = {'ctx': 200.0,
     'c_ctx': 22.216,
     'b_mod': 4.964,
     'b_in': 3.89,
     'conf_dw_b': 8.0,
     'conf_ln_g': 51.956,
     'conf_ln_b': 46.905,
     'na_rpb': 64.0,
     'hy_sconv_b': 4.316,
     'hy_b1': 4.389,
     'hy_b2': 3.963,
     'b_out': 21.385,
     'hy_freq': 3.146}
    for name, (base, spread) in spreads.items():
        noise = np.random.default_rng([zlib.crc32(name.encode()), seed]).standard_normal(out[name].shape)
        drawn = base * np.exp(spread * noise) if base else spread * noise
        out[name] = jnp.asarray(drawn.astype(out[name].dtype))
    for name, factor in factors.items():
        out[name] = (out[name] * factor).astype(out[name].dtype)
    return out
```

```python
import math
from contextlib import ExitStack

import numpy as np

import concourse.bass as bass
from concourse import mybir

F32 = mybir.dt.float32
F32R = mybir.dt.float32r
ACT = mybir.ActivationFunctionType
ALU = mybir.AluOpType
AX = mybir.AxisListType

P = 128
D = 1024
KD = D // P
SEQ = 256
TOK = 2 * SEQ
DEPTH = 2
D_FF = 2816
JF = D_FF // P
CHUNKS = (8, 8, 6)
N_MOD = 9
MODT = N_MOD * KD
WB = 256
BT = WB // P
CONF_K = 31
PADC = CONF_K // 2
HEADS = 4
DH = 64
SCALE = DH ** -0.5
GRID_W = 64
WIN_ROWS, WIN_COLS = 8, 16
RPB_R, RPB_C = 2 * WIN_ROWS - 1, 2 * WIN_COLS - 1
ROWS = SEQ // GRID_W
MASKED = -1e30
ORDER = 2
PE_DIM = 33
FH = 64
LN_EPS = 1e-5
ALPHA = (2 * DEPTH) ** 0.25
TWO_PI = 2.0 * math.pi
PI_HI = 6.28125
PI_LO = TWO_PI - PI_HI
PI_IN = 3.1415925
ROUND = 1.5 * 2.0 ** 23
P_IN = 6912
M_G = 22

VROW = {"b_mod": (0, 0), "b_in": (0, 72),
        "ln_g": (1, 0), "ln_b": (1, 24), "conf_w": (1, 48), "sc_w": (1, 110), "conf_b": (1, 116),
        "conf_g": (1, 118), "conf_be": (1, 120), "hy_bias": (1, 122),
        "hs_w": (2, 0), "hs_b": (2, 18), "b_out": (2, 24), "hy_b1": (2, 32), "hy_b2": (2, 33), "hy_f": (2, 34)}
NG = 3

WIN_ORDER = (0, 1, 2, 3, 16, 17, 18, 19, 20, 21, 4, 5, 6, 7, 8, 9, 10, 11, 12, 13, 14, 15)
N_WIN = len(WIN_ORDER)
N_SUB = 2 * DEPTH
MOD_IN = ((4, 4, 4), (4, 4, 4), (4, 0, 0), (0, 0, 0))
MOD_OUT = ((2, 2, 2), (2, 2, 2), (0, 0, 0), (0, 0, 0))
MOD_FIRST = 16


def plan():
    u, q = MOD_FIRST, MOD_FIRST
    at, modq, proj = {("pre",): 0}, {("pre",): 0}, set()

    def ffn(f):
        nonlocal u, q
        for c, n in enumerate(CHUNKS):
            at["in", f, c], modq["in", f, c] = u, q
            u += (n // 2) * (4 + MOD_IN[f][c])
            q += (n // 2) * MOD_IN[f][c]
            at["out", f, c], modq["out", f, c] = u, q
            u += 2 * (4 + MOD_OUT[f][c])
            q += 2 * MOD_OUT[f][c]

    for l in range(DEPTH):
        ffn(2 * l)
        at["win", l] = u
        u += N_WIN
        at["gate", l] = u
        for m in range(KD):
            proj.add(u + 5 * m + 2)
        u += 5 * KD
        at["wout", l] = u
        u += KD
        ffn(2 * l + 1)
    assert q == DEPTH * MODT
    return at, modq, proj, u


AT, MODQ, PROJ, UNITS = plan()


def landed(u):
    return 16 * (u // 2 + 1) + 48 * sum(1 for x in PROJ if x % 2 == u % 2 and x <= u)


def body_in(nmod):
    mains = [("a", 0), ("g", 0), ("a", 1), ("g", 1)]
    return [x for i, w in enumerate(mains) for x in ([("m", i)] if nmod else []) + [w]]


def body_out(nmod):
    return [("m", 0), ("o", 0), ("o", 1), ("m", 1), ("o", 2), ("o", 3)] if nmod else [("o", i) for i in range(4)]


def modbase(f, kind, c):
    n = MOD_FIRST // 4
    for ff in range(N_SUB):
        for cc, j in enumerate(CHUNKS):
            if (ff, "in", cc) == (f, kind, c):
                return n
            n += (j // 2) if MOD_IN[ff][cc] else 0
            if (ff, "out", cc) == (f, kind, c):
                return n
            n += 2 if MOD_OUT[ff][cc] else 0


def win_tokens(l, m):
    return TOK if l < DEPTH - 1 or 6 <= m < 10 else SEQ


def build(nc, a, out):
    ctx = ExitStack()
    with ctx:
        def sb(name, shape, dt=F32):
            return ctx.enter_context(nc.sbuf_tensor(name, shape, dt))

        def sem(name):
            return ctx.enter_context(nc.semaphore(name))

        X = sb("X", [P, KD, TOK])
        Y = sb("Y", [P, KD, TOK])
        Hh = sb("Hh", [P, KD, TOK], F32R)
        Hl = sb("Hl", [P, KD, TOK], F32R)
        with nc.sbuf_tensor("UWORK", [P, 2 * KD * TOK], F32) as Wk:
            pass
        Uh = sb("Uh", [P, KD, TOK], F32R)
        Ul = sb("Ul", [P, KD, TOK], F32R)
        Bh = sb("Bh", [P, 4, BT, TOK], F32R)
        Bl = sb("Bl", [P, 4, BT, TOK], F32R)
        raw = [sb(f"raw{s}", [P, KD, P]) for s in range(2)]
        wh = [sb(f"wh{s}", [P, KD, P], F32R) for s in range(2)]
        wl = [sb(f"wl{s}", [P, KD, P], F32R) for s in range(2)]
        spec = sb("spec", [P, DEPTH, 2, 2, ORDER, WB])
        dft = sb("dft", [P, 4, 2, SEQ])
        mats = sb("mats", [P, 4, P])
        flip = sb("flip", [P, P])
        vec = sb("vec", [P, DEPTH, NG, P])
        bmod2 = sb("bmod2", [P, DEPTH * MODT, 2])
        modv = sb("modv", [P, DEPTH * MODT, 2])
        S4 = sb("S4", [P, KD, 4], F32R)
        modrow = sb("modrow", [4, 4, P])
        sel = sb("sel", [4, 2])
        gate = sb("gate", [P, KD, 2])
        small = sb("small", [P, 64])
        E = sb("E", [P, 5248])

        mean = E[:, 0:512]
        var = E[:, 512:1024]
        rstd = E[:, 1024:1536]
        nmr = E[:, 1536:2048]
        tt = [E[:, 2048:2560], E[:, 2560:3072]]
        sq = [E[:, 3072:3584], E[:, 3584:4096]]
        acc1 = E[:, 4096:4608]
        acc2 = E[:, 4608:5120]
        Yf = Y[:].rearrange("p k t -> p (k t)")
        qk = Wk[:, 0:2048].rearrange("p (i t) -> p i t", i=4)
        vtok = Wk[:, 2048:3072].rearrange("p (i c) -> p i c", i=4)
        btab = Wk[:, 3072:5120].rearrange("p (q h r c) -> p q h r c", q=2, h=HEADS, r=ROWS)
        hvc = Wk[:, 5120:8192].rearrange("p (i t) -> p i t", i=6)
        rtab = Wk[:, 6144:8192].rearrange("p (q h r c) -> p q h r c", q=2, h=HEADS, r=ROWS)
        hvpad = Yf[:, 0:3096].rearrange("p (i s t) -> p i s t", i=6, s=2)
        ysp = Yf[:, 0:2048].rearrange("p (r f n) -> p r f n", r=2, f=2)
        uT = Yf[:, 2048:3072].rearrange("p (i n) -> p i n", i=2)
        cpad = E[:, 0:1144].rearrange("p (i s t) -> p i s t", i=2, s=2)
        cacc = E[:, 1144:2168].rearrange("p (i t) -> p i t", i=2)
        scpad = E[:, 2168:3200].rearrange("p (i s t) -> p i s t", i=2, s=2)
        sbb = E[:, 3200:4224].rearrange("p (i t) -> p i t", i=2)
        tmpa = E[:, 4224:5248].rearrange("p (i t) -> p i t", i=2)
        cmean, cvar, crstd, cnmr = (E[:, 2168 + 512 * i:2680 + 512 * i] for i in range(4))
        csq = tmpa
        sbuf_s = [E[:, 512 * i:512 * i + 512] for i in range(2)]
        sbuf_p = [E[:, 1024 + 512 * i:1536 + 512 * i] for i in range(2)]
        sbuf_pT = [E[:, 2048 + 512 * i:2560 + 512 * i].rearrange("p (k q) -> p k q", k=4) for i in range(2)]
        obuf = E[:, 3072:4096].rearrange("p (i t) -> p i t", i=2)
        hprod = [E[:, 4096 + 512 * i:4608 + 512 * i] for i in range(2)]
        xrow = Yf.rearrange("p (t n) -> p t n", t=4)
        vrow = Wk[:, 0:768].rearrange("p (l g c) -> p l g c", l=DEPTH, g=NG)
        crow = Wk[0:16, 768:896]
        decay = Wk[:, 1024:2048].rearrange("p (t r c) -> p t r c", t=2, r=2)
        zT = Wk[0:PE_DIM, 2048:2304]
        fw1 = Wk[0:PE_DIM, 2304:2304 + 2 * FH].rearrange("p (l c) -> p l c", l=2)
        fw2 = Wk[0:FH, 2432:2432 + 2 * FH].rearrange("p (l c) -> p l c", l=2)
        fw3 = Wk[0:FH, 2560:4608].rearrange("p (l c) -> p l c", l=2)
        farg = Wk[0:FH, 4608:4864]
        fk = Wk[0:FH, 4864:5120]
        fh = Wk[0:FH, 5120:5376]
        filt = Wk[:, 5376:6400].rearrange("p (o r c) -> p o r c", o=ORDER, r=2)
        hp = E[:, 0:1024].rearrange("p (t o c) -> p t o c", t=2, o=ORDER)
        hm = E[:, 1024:2048].rearrange("p (t o c) -> p t o c", t=2, o=ORDER)
        hsq = E[:, 2048:4096].rearrange("p (r t n) -> p r t n", r=2, t=2)
        fn = E[:, 4096:4608]
        cs = small[:, 0:16]
        nmax = small[:, 16:18]
        psumr = small[:, 18:20]
        prec = small[:, 20:22]

        ident, invD, invB, ones = (mats[:, i, :] for i in range(4))

        bank = [ctx.enter_context(nc.psum_tensor(f"bank{i}", [P, 512], F32)) for i in range(8)]

        def col(l, name, i=0, rows=slice(0, P)):
            g, r = VROW[name]
            return vec[rows, l, g, r + i:r + i + 1]

        s_c = sem("s_c")
        s_const = sem("s_const")
        s_xin = sem("s_xin")
        w_landed = [sem(f"w_landed{s}") for s in range(2)]
        hi_done = sem("hi_done")
        lo_done = sem("lo_done")
        unit_done = sem("unit_done")
        zero_done = sem("zero_done")
        turned = sem("turned")
        cols_done = sem("cols_done")
        s4hi = sem("s4hi")
        s4lo = sem("s4lo")
        cols_fix = sem("cols_fix")
        x_turned = sem("x_turned")
        x_tile = sem("x_tile")
        sq_tile = sem("sq_tile")
        acc_step = sem("acc_step")
        stat_mm = sem("stat_mm")
        stat_cp = sem("stat_cp")
        stat_v = sem("stat_v")
        stat_sd = sem("stat_sd")
        t_mul = sem("t_mul")
        t_sub = sem("t_sub")
        h_full = sem("h_full")
        h_hi = sem("h_hi")
        h_lo = sem("h_lo")
        mrow_done = sem("mrow_done")
        mcol_mm = sem("mcol_mm")
        mod_done = sem("mod_done")
        silu_done = sem("silu_done")
        prod_done = sem("prod_done")
        u_hi = sem("u_hi")
        u_lo = sem("u_lo")
        out_evac = sem("out_evac")
        resid = sem("resid")
        gate_rdy = sem("gate_rdy")
        f_mm = sem("f_mm")
        f_v = sem("f_v")
        f_a = sem("f_a")
        pads = sem("pads")
        s_rtab = sem("s_rtab")
        r_mask = sem("r_mask")
        flipped = sem("flipped")
        btab_cp = sem("btab_cp")
        win_evac = sem("win_evac")
        cglu = sem("cglu")
        ctap = sem("ctap")
        htap = sem("htap")
        stap = sem("stap")
        c_sq = sem("c_sq")
        c_mm = sem("c_mm")
        c_cp = sem("c_cp")
        c_v = sem("c_v")
        c_sd = sem("c_sd")
        c_silu = sem("c_silu")
        b_hi = sem("b_hi")
        b_lo = sem("b_lo")
        at_s = sem("at_s")
        at_v = sem("at_v")
        at_m = sem("at_m")
        at_e = sem("at_e")
        at_r = sem("at_r")
        at_n = sem("at_n")
        at_t = sem("at_t")
        at_tc = sem("at_tc")
        at_o = sem("at_o")
        at_oc = sem("at_oc")
        hy_t = sem("hy_t")
        hy_tc = sem("hy_tc")
        hy_f = sem("hy_f")
        hy_p = sem("hy_p")
        hy_i = sem("hy_i")
        hy_z = sem("hy_z")
        sig_done = sem("sig_done")
        mix_step = sem("mix_step")
        m_hi = sem("m_hi")
        m_lo = sem("m_lo")
        o_turn = sem("o_turn")
        o_copy = sem("o_copy")
        s_out = sem("s_out")

        def streams(l):
            return 2 if l < DEPTH - 1 else 1

        def blocks(l):
            return [(s, h, q) for s in range(streams(l)) for h in range(HEADS) for q in range(2)]

        NB0 = len([1 for s in range(2) for h in range(HEADS) for q in range(2)])

        def lnt(n):
            return TOK if n <= 8 else SEQ

        def ffn_tok(f):
            return TOK if f < 3 else SEQ

        NLN = 6 * DEPTH

        def hfull_at(n, k):
            return sum(8 * (lnt(x) // SEQ) for x in range(0, n, 2)) + (k + 1) * (lnt(n) // SEQ)

        FS = 6
        FV = 2 * FS + 12 + 2 + 4
        FM = 2 + 4 + 1 + 4
        NHT = 18
        NST = 2 + 6 + 2
        NCV = 8
        AV0 = 24
        FREE = 2
        FREE_MIX = 4

        def mix_at(l, d):
            return FREE_MIX + 56 * l + 7 * d

        block = ctx.enter_context(nc.Block())

        @block.sync
        def _(sp):
            def unit(u, k, it, per, srcs):
                if u >= 2:
                    sp.wait_ge(lo_done, u - 1 + it * per)
                    sp.nop(nofuse=True)
                for lo, n, src in srcs:
                    sp.dma_start(raw[u % 2][:, lo:lo + n, :], src).then_inc(w_landed[u % 2], 16)

            def rows(w, c0):
                return w.rearrange("(k p) n -> p k n", p=P)[:, :, bass.ds(c0, P)]

            def mod_src(q, it, step, i):
                l = q // MODT
                return rows(a["w_mod"][l], (q % MODT + i) * P + it * step * P)

            def xload():
                for t in range(2):
                    sp.dma_start(xrow[:, t, :], a["x"][0, t * P:(t + 1) * P, :]).then_inc(s_xin, 16)
                    sp.dma_start(xrow[:, 2 + t, :], a["ctx"][0, t * P:(t + 1) * P, :]).then_inc(s_xin, 16)

            for i in range(2):
                unit(i, KD, 0, 0, [(0, KD, mod_src(0, 0, 0, i))])
            xload()
            unit(2, KD, 0, 0, [(0, KD, mod_src(0, 0, 0, 2))])
            unit(3, KD, 0, 0, [(0, KD, mod_src(0, 0, 0, 3))])
            with sp.Fori(0, MOD_FIRST // 4 - 1) as it:
                for i in range(4):
                    unit(4 + i, KD, it, 4, [(0, KD, mod_src(4, it, 4, i))])

            def ffn(f):
                l, s = f // 2, f % 2
                j0 = 0
                for c, n in enumerate(CHUNKS):
                    u0, q0 = AT["in", f, c], MODQ["in", f, c]
                    body = body_in(MOD_IN[f][c])
                    with sp.Fori(0, n // 2) as it:
                        for i, (kind, x) in enumerate(body):
                            if kind == "m":
                                src = mod_src(q0, it, 4, x)
                            else:
                                src = rows(a["ffn_w_in"][l, s],
                                           (D_FF if kind == "g" else 0) + (j0 + x) * P + it * 2 * P)
                            unit(u0 + i, KD, it, len(body), [(0, KD, src)])
                    u0, q0 = AT["out", f, c], MODQ["out", f, c]
                    body = body_out(MOD_OUT[f][c])
                    with sp.Fori(0, 2) as it:
                        for i, (kind, x) in enumerate(body):
                            if kind == "m":
                                unit(u0 + i, KD, it, len(body), [(0, KD, mod_src(q0, it, 2, x))])
                            else:
                                w = a["ffn_w_out"][l, s, j0 * P:(j0 + n) * P, :]
                                unit(u0 + i, n, it, len(body), [(0, n, rows(w, x * P + it * 4 * P))])
                    j0 += n

            def mixer(l):
                sp.wait_ge(unit_done, AT["win", l])
                rpb = a["na_rpb"]
                for r in range(ROWS):
                    for h in range(HEADS):
                        off = ((l * HEADS + h) * RPB_R + WIN_ROWS - 1 - r) * RPB_C + WIN_COLS - 1 - (GRID_W - 1)
                        src = bass.AP(tensor=rpb.tensor, offset=rpb.offset + off,
                                      ap=[[1, GRID_W], [RPB_C, ROWS], [1, GRID_W]])
                        sp.dma_start(rtab[GRID_W * (r % 2):GRID_W * (r % 2 + 1), r // 2, h, :, :],
                                     src).then_inc(s_rtab, 16)
                u0 = AT["win", l]
                for i, m in enumerate(WIN_ORDER):
                    unit(u0 + i, KD, 0, 0, [(0, KD, rows(a["w_in"][l], m * P))])
                u0 = AT["gate", l]
                with sp.Fori(0, KD // 2) as it:
                    for d in range(2):
                        for i, b in enumerate((0, 1, None, 2, 3)):
                            if b is None:
                                srcs = [(2 * n, BT, rows(a[w][l], d * P + it * 2 * P)) for n, w in
                                        enumerate(("conf_w_proj", "na_w_proj", "sc_w_proj", "hy_w_proj"))]
                            else:
                                srcs = [(0, KD, rows(a["w_in"][l], (M_G + KD * b + d) * P + it * 2 * P))]
                            unit(u0 + 5 * d + i, KD, it, 10, srcs)
                u0 = AT["wout", l]
                with sp.Fori(0, KD // 4) as it:
                    for i in range(4):
                        unit(u0 + i, KD, it, 4, [(0, KD, rows(a["w_out"][l], i * P + it * 4 * P))])

            for l in range(DEPTH):
                ffn(2 * l)
                mixer(l)
                ffn(2 * l + 1)
            for t in range(2):
                sp.wait_ge(o_copy, 2 * (t + 1))
                sp.dma_start(out[0, t * P:(t + 1) * P, :], xrow[:, t, :]).then_inc(s_out, 16)
            sp.wait_ge(s_out, 32)

        @block.gpsimd
        def _(pool):
            pool.memset(Wk[:, 0:1024], 0.0).then_inc(zero_done, 1)
            pool.wait_ge(zero_done, 1)

            def vload(l, name, src):
                g, r = VROW[name]
                n, w = src.shape
                pool.dma_start(vrow[r:r + n, l, g, 0:w], src).then_inc(s_const, 16)

            pool.dma_start(crow[0:8, :], a["c"].rearrange("b (k p) -> (b k) p", p=P)).then_inc(s_c, 16)
            pool.dma_start(crow[8:16, :], a["c_ctx"].rearrange("(k p) -> k p", p=P)).then_inc(s_c, 16)
            pool.dma_start(mats[:], a["k_mats"]).then_inc(s_c, 16)
            pool.dma_start(sel[:], a["k_sel"]).then_inc(s_const, 16)
            pool.dma_start(flip[:], a["k_flip"]).then_inc(s_const, 16)
            pool.dma_start(dft[:], a["k_dft"]).then_inc(s_const, 16)
            pool.dma_start(decay, a["k_decay"]).then_inc(s_const, 16)
            pool.dma_start(zT, a["k_zT"]).then_inc(s_const, 16)
            for l in range(DEPTH):
                vload(l, "b_mod", a["b_mod"][l].rearrange("(k p) -> k p", p=P))
                vload(l, "b_in", a["b_in"][l].rearrange("(k p) -> k p", p=P))
                vload(l, "ln_g", a["post_ln_g"][l].rearrange("i (k p) -> (i k) p", p=P))
                vload(l, "ln_b", a["post_ln_b"][l].rearrange("i (k p) -> (i k) p", p=P))
                vload(l, "conf_w", a["conf_dw_w"][l].rearrange("i (k p) -> (i k) p", p=P))
                vload(l, "sc_w", a["sc_conv_w"][l].rearrange("i (k p) -> (i k) p", p=P))
                vload(l, "conf_b", a["conf_dw_b"][l].rearrange("(k p) -> k p", p=P))
                vload(l, "conf_g", a["conf_ln_g"][l].rearrange("(k p) -> k p", p=P))
                vload(l, "conf_be", a["conf_ln_b"][l].rearrange("(k p) -> k p", p=P))
                vload(l, "hy_bias", a["hy_bias"][l].rearrange("i (k p) -> (i k) p", p=P))
                vload(l, "hs_w", a["hy_sconv_w"][l].rearrange("i (k p) -> (i k) p", p=P))
                vload(l, "hs_b", a["hy_sconv_b"][l].rearrange("(k p) -> k p", p=P))
                vload(l, "b_out", a["b_out"][l].rearrange("(k p) -> k p", p=P))
                vload(l, "hy_b1", a["hy_b1"][l:l + 1])
                vload(l, "hy_b2", a["hy_b2"][l:l + 1])
                vload(l, "hy_f", a["hy_freq"][l])
                pool.dma_start(fw1[:, l, :], a["hy_w1"][l]).then_inc(s_const, 16)
                pool.dma_start(fw2[:, l, :], a["hy_w2"][l]).then_inc(s_const, 16)
                pool.dma_start(fw3[:, l, :], a["hy_w3"][l]).then_inc(s_const, 16)

            n_acc = 0
            n_sub = 0

            def sum_sq(n, with_x):
                nonlocal n_acc
                T = lnt(n)
                for k in range(KD):
                    base = n_acc
                    if with_x:
                        pool.wait_ge(resid, 8 * (n // 2) + k + 1)
                        if k == 0:
                            pool.tensor_copy(acc1[:, 0:T], X[:, k, 0:T]).then_inc(acc_step, 1)
                        else:
                            pool.wait_ge(acc_step, base - 1)
                            pool.tensor_tensor(acc1[:, 0:T], acc1[:, 0:T], X[:, k, 0:T],
                                               ALU.add).then_inc(acc_step, 1)
                        n_acc += 1
                    pool.wait_ge(sq_tile, 8 * n + k + 1)
                    if k == 0:
                        pool.tensor_copy(acc2[:, 0:T], sq[k % 2][:, 0:T]).then_inc(acc_step, 1)
                    else:
                        pool.wait_ge(acc_step, base)
                        pool.tensor_tensor(acc2[:, 0:T], acc2[:, 0:T], sq[k % 2][:, 0:T],
                                           ALU.add).then_inc(acc_step, 1)
                    n_acc += 1

            def masks(l):
                pool.wait_ge(s_rtab, 16 * 16 * (l + 1))
                pool.wait_ge(t_sub, 8 * (6 * l + 2) + KD)
                k = 8 * l
                for q in range(2):
                    for half in range(2):
                        rows = slice(GRID_W * half, GRID_W * half + GRID_W)
                        v = rtab[rows, q, :, :, 0:GRID_W - WIN_COLS].rearrange("p h r c -> p (h r) c")
                        pool.affine_select(out=v, in_=v, compare_op=ALU.is_ge, fill=MASKED,
                                           base=WIN_COLS // 2 - (GRID_W - 1),
                                           pattern=[[0, HEADS * ROWS], [1, GRID_W - WIN_COLS]],
                                           channel_multiplier=1).then_inc(r_mask, 1)
                        pool.wait_ge(r_mask, k + 1)
                        v = rtab[rows, q, :, :, WIN_COLS:GRID_W].rearrange("p h r c -> p (h r) c")
                        pool.affine_select(out=v, in_=v, compare_op=ALU.is_ge, fill=MASKED,
                                           base=GRID_W - 1 + WIN_COLS // 2 - 1 - WIN_COLS,
                                           pattern=[[0, HEADS * ROWS], [-1, GRID_W - WIN_COLS]],
                                           channel_multiplier=-1).then_inc(r_mask, 1)
                        k += 2
                        pool.wait_ge(r_mask, k)

            def apply_mod(n):
                nonlocal n_sub
                T = lnt(n)
                pool.wait_ge(stat_v, 4 * n + 4)
                for k in range(KD):
                    n_sub += 1
                    pool.wait_ge(t_mul, 8 * n + k + 1)
                    pool.tensor_tensor(tt[k % 2][:, 0:T], tt[k % 2][:, 0:T], nmr[:, 0:T],
                                       ALU.subtract).then_inc(t_sub, 1)

            sum_sq(0, False)
            apply_mod(0)
            for l in range(DEPTH):
                for sub in range(3):
                    n = 6 * l + 2 * sub + 1
                    sum_sq(n, True)
                    if n < NLN - 1:
                        sum_sq(n + 1, False)
                        apply_mod(n + 1)
                    if sub == 0:
                        masks(l)

        @block.scalar
        def _(act):
            def hi(u, it=0, per=0):
                step = landed(u + per) - landed(u) if per else 0
                act.wait_ge(w_landed[u % 2], landed(u) + it * step)
                if u >= 2:
                    act.wait_ge(unit_done, u - 1 + it * per)
                nc.scalar.activation(wh[u % 2][:], raw[u % 2][:], ACT.Copy).then_inc(hi_done, 1)

            def nxt(u, it=0, per=0):
                if per or u + 2 < UNITS:
                    hi(u + 2, it, per)

            def rows_out(u, n_prev, it, per, nm):
                act.wait_ge(unit_done, u + 1 + it * per)
                act.wait_ge(mcol_mm, n_prev + it)
                nc.scalar.activation(modrow[:, 0:nm, :],
                                     bank[6][0:4, 0:nm * P].rearrange("p (i c) -> p i c", i=nm),
                                     ACT.Copy).then_inc(mrow_done, 1)

            act.wait_ge(turned, 1)
            nc.scalar.activation(cs, bank[2][:, 0:16], ACT.Silu).then_inc(cols_done, 1)
            act.wait_ge(cols_done, 1)
            for s in range(2):
                nc.scalar.activation(S4[:, :, 2 * s], cs[:, 8 * s:8 * s + 8], ACT.Copy).then_inc(s4hi, 1)
            hi(0)
            hi(1)
            act.wait_ge(turned, 3)
            for l in range(DEPTH):
                nc.scalar.activation(vec[:, l, :, :], bank[l][:, 0:NG * P].rearrange("p (g c) -> p g c", g=NG),
                                     ACT.Copy).then_inc(cols_done, 1)

            for i in range(4):
                nxt(i)
            act.wait_ge(unit_done, 4)
            nc.scalar.activation(modrow[:, 0:4, :], bank[6][0:4, :].rearrange("p (i c) -> p i c", i=4),
                                 ACT.Copy).then_inc(mrow_done, 1)
            for k in range(KD):
                act.wait_ge(x_turned, k + 1)
                nc.scalar.activation(X[:, k, :], bank[4 + k % 2][:], ACT.Copy, scale=ALPHA).then_inc(x_tile, 1)
                act.wait_ge(x_tile, k + 1)
                if k >= 2:
                    act.wait_ge(acc_step, k - 1)
                nc.scalar.activation(sq[k % 2][:], X[:, k, :], ACT.Square).then_inc(sq_tile, 1)
            with act.Fori(0, MOD_FIRST // 4 - 1) as it:
                for i in range(4):
                    act.wait_ge(unit_done, 5 + i + it * 4)
                    nxt(4 + i, it, 4)
                rows_out(7, 1, it, 4, 4)

            n_x = KD
            n_h = 0
            n_acc = KD

            def stats(n):
                T = lnt(n)
                act.wait_ge(stat_mm, 2 * n + 1)
                nc.scalar.activation(mean[:, 0:T], bank[0][:, 0:T], ACT.Copy).then_inc(stat_cp, 1)
                nc.scalar.activation(var[:, 0:T], bank[0][:, 0:T], ACT.Square).then_inc(stat_cp, 1)
                act.wait_ge(stat_v, 4 * n + 2)
                nc.scalar.activation(var[:, 0:T], var[:, 0:T], ACT.Sqrt).then_inc(stat_sd, 1)

            def apply_post(n):
                nonlocal n_x, n_acc
                T, l, i = lnt(n), n // 6, (n % 6) // 2
                last = n == NLN - 1
                n_acc += 2 * KD
                for k in range(KD):
                    act.wait_ge(t_sub, 8 * n + k + 1)
                    nc.scalar.activation(X[:, k, 0:T], tt[k % 2][:, 0:T], ACT.Identity,
                                         bias=col(l, "ln_b", 8 * i + k), scale=col(l, "ln_g", 8 * i + k))\
                        .then_inc(x_tile, 1)
                    n_x += 1
                    if not last:
                        T2 = lnt(n + 1)
                        act.wait_ge(x_tile, n_x)
                        act.wait_ge(acc_step, n_acc if k < 2 else n_acc + k - 1)
                        nc.scalar.activation(sq[k % 2][:, 0:T2], X[:, k, 0:T2], ACT.Square).then_inc(sq_tile, 1)
                if not last:
                    n_acc += KD

            def apply_mod(n):
                nonlocal n_h
                T, l, i = lnt(n), n // 6, (n % 6) // 2
                act.wait_ge(mod_done, modbase((0, 1, 1, 2, 3, 3)[n // 2], "in", 0))
                for k in range(KD):
                    act.wait_ge(t_sub, 8 * n + k + 1)
                    if k >= 2:
                        act.wait_ge(h_lo, n_h - 1)
                    for s in range(T // SEQ):
                        t = slice(s * SEQ, (s + 1) * SEQ)
                        q = l * MODT + 24 * i + k
                        nc.scalar.activation(sq[k % 2][:, t], tt[k % 2][:, t], ACT.Identity,
                                             bias=modv[:, q, s:s + 1], scale=modv[:, q + 8, s:s + 1])\
                            .then_inc(h_full, 1)
                    n_h += 1
                    act.wait_ge(h_full, hfull_at(n, k))
                    nc.scalar.activation(Hh[:, k, 0:T], sq[k % 2][:, 0:T], ACT.Copy).then_inc(h_hi, 1)

            def post(kind, x, u, it, per, f, c, nbody, nm):
                if kind == "m" and x == nm - 1:
                    rows_out(u, nbody, it, per, nm)
                if kind == "g":
                    T = ffn_tok(f)
                    J = f * JF + sum(CHUNKS[:c]) + x
                    act.wait_ge(unit_done, u + 1 + it * per)
                    nc.scalar.activation(tt[x][:, 0:T], bank[2 * x + 1][:, 0:T], ACT.Silu).then_inc(silu_done, 1)
                    act.wait_ge(prod_done, FREE + J + 1 + it * 2)
                    nc.scalar.activation(Uh[:, bass.ds(it * 2 + x, 1), 0:T].rearrange("p o t -> p (o t)"),
                                         sq[x][:, 0:T], ACT.Copy).then_inc(u_hi, 1)

            def tail(n, m):
                T = lnt(n)
                act.wait_ge(resid, 8 * (n // 2) + m + 1)
                if m >= 2:
                    act.wait_ge(acc_step, n_acc + 2 * (m - 1))
                nc.scalar.activation(sq[m % 2][:, 0:T], X[:, m, 0:T], ACT.Square).then_inc(sq_tile, 1)

            def ffn(f):
                l, s = f // 2, f % 2
                n = 6 * l + (1 if s == 0 else 5)
                for c, nj in enumerate(CHUNKS):
                    u0 = AT["in", f, c]
                    nm = MOD_IN[f][c]
                    body = body_in(nm)
                    with act.Fori(0, nj // 2) as it:
                        for i, (kind, x) in enumerate(body):
                            act.wait_ge(unit_done, u0 + i + 1 + it * len(body))
                            nxt(u0 + i, it, len(body))
                            post(kind, x, u0 + i, it, len(body), f, c, modbase(f, "in", c), nm)
                    u0 = AT["out", f, c]
                    nm = MOD_OUT[f][c]
                    body = body_out(nm)
                    if c < len(CHUNKS) - 1:
                        with act.Fori(0, 2) as it:
                            for i, (kind, x) in enumerate(body):
                                act.wait_ge(unit_done, u0 + i + 1 + it * len(body))
                                nxt(u0 + i, it, len(body))
                                post(kind, x, u0 + i, it, len(body), f, c, modbase(f, "out", c), nm)
                    else:
                        for it in range(2):
                            for i, (kind, x) in enumerate(body):
                                u = u0 + it * len(body) + i
                                act.wait_ge(unit_done, u + 1)
                                nxt(u)
                                if kind == "m":
                                    post(kind, x, u, 0, 0, f, c, modbase(f, "out", c) + it, nm)
                                else:
                                    tail(n, 4 * it + x)

            def filters():
                act.wait_ge(acc_step, KD)
                for l in range(DEPTH):
                    for i in range(2):
                        act.wait_ge(f_v, FV * l + FS * (i + 1))
                        nc.scalar.activation(fh, farg, ACT.Sin).then_inc(f_a, 1)
                    act.wait_ge(f_v, FV * l + 2 * FS + 12)
                    nc.scalar.activation(hsq[:, 0, :, :], hp.rearrange("p t o c -> p t (o c)"), ACT.Square)\
                        .then_inc(f_a, 1)
                    nc.scalar.activation(hsq[:, 1, :, :], hm.rearrange("p t o c -> p t (o c)"), ACT.Square)\
                        .then_inc(f_a, 1)
                    act.wait_ge(f_v, FV * l + 2 * FS + 13)
                    nc.scalar.activation(fn, fn, ACT.Sqrt).then_inc(f_a, 1)

            def branch_hi(l, b, src, S):
                nc.scalar.activation(Bh[:, b, :, 0:S * SEQ], src[:, :, 0:S * SEQ], ACT.Copy).then_inc(b_hi, 1)

            def mixer(l):
                S = streams(l)
                T = S * SEQ
                u0 = AT["win", l]
                for i, m in enumerate(WIN_ORDER):
                    u = u0 + i
                    act.wait_ge(unit_done, u + 1)
                    nxt(u)
                    b = col(l, "b_in", m)
                    src = bank[i % 4]
                    if i == 0:
                        act.wait_ge(pads, 6 * (l + 1))
                    if m in (0, 1):
                        o, f, v = tmpa[:, m, 0:T], ACT.Identity, src[:, 0:T]
                    elif m in (2, 3):
                        o, f, v = cacc[:, m - 2, 0:T], ACT.Sigmoid, src[:, 0:T]
                    elif m >= 16:
                        o, f, v = hvpad[:, m - 16, 0:S, 1:SEQ + 1], ACT.Identity, \
                            src[:, 0:T].rearrange("p (s t) -> p s t", s=S)
                    elif m < 8:
                        TT = win_tokens(l, m)
                        o, f, v = qk[:, m - 4, 0:TT], ACT.Identity, src[:, 0:TT]
                    elif m < 10:
                        o, f, v, b = vtok[:, :, (m - 8) * P:(m - 7) * P], ACT.Copy, \
                            src[:, :].rearrange("p (t c) -> p t c", t=4), 0.0
                    elif m < 12:
                        o, f, v = sbb[:, m - 10, 0:T], ACT.Identity, src[:, 0:T]
                    elif m < 14:
                        if m == 12:
                            act.wait_ge(cglu, 2 * (l + 1))
                        o, f, v = tmpa[:, m - 12, 0:T], ACT.Identity, src[:, 0:T]
                    else:
                        o, f, v = scpad[:, m - 14, 0:S, 1:SEQ + 1], ACT.Identity, \
                            src[:, 0:T].rearrange("p (s t) -> p s t", s=S)
                    nc.scalar.activation(o, v, f, bias=b).then_inc(win_evac, 1)
                    if i == 4:
                        for q in range(2):
                            for h2 in range(2):
                                act.wait_ge(flipped, 4 * l + 2 * q + h2 + 1)
                                nc.scalar.activation(
                                    btab[:, q, 2 * h2:2 * h2 + 2, :, :].rearrange("p h r c -> p (h r c)"),
                                    bank[4 + 2 * q + h2][:], ACT.Copy).then_inc(btab_cp, 1)
                act.wait_ge(stap, NST * (l + 1))
                branch_hi(l, 2, tmpa, S)
                act.wait_ge(b_lo, 4 * l + 1)
                act.wait_ge(ctap, 2 * CONF_K * (l + 1))
                nc.scalar.activation(csq[:, :, 0:T], cacc[:, :, 0:T], ACT.Square).then_inc(c_sq, 1)
                act.wait_ge(c_mm, 2 * l + 1)
                nc.scalar.activation(cmean[:, 0:T], bank[0][:, 0:T], ACT.Copy).then_inc(c_cp, 1)
                nc.scalar.activation(cvar[:, 0:T], bank[0][:, 0:T], ACT.Square).then_inc(c_cp, 1)
                act.wait_ge(c_v, 8 * l + 2)
                nc.scalar.activation(cvar[:, 0:T], cvar[:, 0:T], ACT.Sqrt).then_inc(c_sd, 1)
                for i in range(BT):
                    act.wait_ge(c_v, 8 * l + 6 + 2 * i)
                    nc.scalar.activation(cacc[:, i, 0:T], cacc[:, i, 0:T], ACT.Silu, bias=col(l, "conf_be", i),
                                         scale=col(l, "conf_g", i)).then_inc(c_silu, 1)
                act.wait_ge(c_silu, 2 * (l + 1))
                branch_hi(l, 0, cacc, S)
                bl = blocks(l)
                nb = len(bl)
                g0 = NB0 * l
                act.wait_ge(b_lo, 4 * l + 2)
                for n in range(nb + 3):
                    if n < nb:
                        K = TOK if bl[n][0] == 0 else SEQ
                        act.wait_ge(at_m, g0 + n + 1)
                        if n >= 2:
                            act.wait_ge(at_t, g0 + n - 1)
                        nc.scalar.activation(sbuf_p[n % 2][:, 0:K], sbuf_s[n % 2][:, 0:K], ACT.Exp,
                                             bias=nmax[:, n % 2:n % 2 + 1],
                                             accum_out=psumr[:, n % 2:n % 2 + 1]).then_inc(at_e, 1)
                    m = n - 2
                    if 0 <= m < nb:
                        kt = 4 if bl[m][0] == 0 else 2
                        act.wait_ge(at_t, g0 + m + 1)
                        if m >= 2:
                            act.wait_ge(at_o, g0 + m - 1)
                        nc.scalar.activation(sbuf_pT[m % 2][:, 0:kt, :],
                                             bank[6][:, 0:kt * P].rearrange("p (k q) -> p k q", k=kt),
                                             ACT.Copy).then_inc(at_tc, 1)
                    m = n - 3
                    if 0 <= m < nb:
                        s, h, q = bl[m]
                        rr = slice(DH * (h % 2), DH * (h % 2) + DH)
                        act.wait_ge(at_o, g0 + m + 1)
                        nc.scalar.activation(obuf[rr, h // 2, s * SEQ + q * P:s * SEQ + (q + 1) * P],
                                             bank[7 - 4 * (m % 2)][rr, 0:P], ACT.Identity,
                                             bias=col(l, "b_in", 8 + h // 2, rr)).then_inc(at_oc, 1)
                act.wait_ge(at_oc, g0 + nb)
                branch_hi(l, 1, obuf, S)
                for o in range(ORDER):
                    for i in range(2):
                        act.wait_ge(hy_t, 2 * (ORDER * l + o) + i + 1)
                        nc.scalar.activation(uT[:, i, 0:S * WB], bank[i][:, 0:S * WB], ACT.Copy)\
                            .then_inc(hy_tc, 1)
                act.wait_ge(hy_z, 4 * ORDER * (l + 1))
                branch_hi(l, 3, hvc[:, 0:BT, :], S)
                u0 = AT["gate", l]
                with act.Fori(0, KD // 2) as it:
                    for d in range(2):
                        for i, b in enumerate((0, 1, None, 2, 3)):
                            u = u0 + 5 * d + i
                            act.wait_ge(unit_done, u + 1 + it * 10)
                            nxt(u, it, 10)
                            if b is None:
                                continue
                            act.wait_ge(mix_step, mix_at(l, d) + (-3, -1, 1, 2)[b] + it * 14)
                            nc.scalar.activation(
                                tt[b % 2][:, 0:T], bank[4 + b][:, 0:T], ACT.Sigmoid,
                                bias=vec[:, l, 0, bass.ds(it * 2 + VROW["b_in"][1] + M_G + KD * b + d, 1)])\
                                .then_inc(sig_done, 1)
                        act.wait_ge(mix_step, mix_at(l, d) + 7 + it * 14)
                        nc.scalar.activation(Uh[:, bass.ds(it * 2 + d, 1), 0:T].rearrange("p o t -> p (o t)"),
                                             acc1[:, 0:T], ACT.Copy).then_inc(m_hi, 1)
                u0 = AT["wout", l]
                for m in range(KD):
                    act.wait_ge(unit_done, u0 + m + 1)
                    nxt(u0 + m)
                    tail(6 * l + 3, m)

            filters()
            stats(0)
            apply_mod(0)
            for l in range(DEPTH):
                for sub in range(3):
                    n = 6 * l + 2 * sub + 1
                    if sub == 1:
                        mixer(l)
                    else:
                        ffn(2 * l + sub // 2)
                    stats(n)
                    apply_post(n)
                    if n < NLN - 1:
                        stats(n + 1)
                        apply_mod(n + 1)
            for i in range(4):
                act.wait_ge(o_turn, i + 1)
                nc.scalar.activation(xrow[:, i // 2, (i % 2) * 512:(i % 2 + 1) * 512], bank[4 + i][:],
                                     ACT.Copy).then_inc(o_copy, 1)

        @block.vector
        def _(dve):
            V = nc.vector

            def lo(u, it=0, per=0):
                dve.wait_ge(hi_done, u + 1 + it * per)
                V.tensor_tensor(wl[u % 2][:], raw[u % 2][:], wh[u % 2][:].bitcast(F32),
                                ALU.subtract).then_inc(lo_done, 1)

            def nxt(u, it=0, per=0):
                if per or u + 2 < UNITS:
                    lo(u + 2, it, per)

            def mod_cols(q0, it, step, nbody, nm):
                dve.wait_ge(mcol_mm, nbody + 1 + it)
                V.tensor_tensor(modv[:, bass.ds(it * step + q0, nm), :],
                                bank[7][:, 0:2 * nm].rearrange("p (i s) -> p i s", s=2),
                                bmod2[:, bass.ds(it * step + q0, nm), :], ALU.add).then_inc(mod_done, 1)

            V.memset(gate[:], 0.0).then_inc(gate_rdy, 1)
            V.memset(small[:, 32:33], 0.0).then_inc(prod_done, FREE)
            V.memset(small[:, 33:34], 0.0).then_inc(out_evac, FREE)
            V.memset(small[:, 34:35], 0.0).then_inc(mix_step, FREE_MIX)
            V.memset(small[:, 35:36], 0.0).then_inc(sig_done, FREE_MIX)
            dve.wait_ge(s4hi, 2)
            for s in range(2):
                V.tensor_tensor(S4[:, :, 2 * s + 1], cs[:, 8 * s:8 * s + 8], S4[:, :, 2 * s].bitcast(F32),
                                ALU.subtract).then_inc(s4lo, 1)
            lo(0)
            lo(1)
            dve.wait_ge(cols_done, 3)
            nfix = 0
            for l in range(DEPTH):
                for s in range(2):
                    V.tensor_copy(bmod2[:, l * MODT:(l + 1) * MODT, s], vec[:, l, 0, 0:MODT]).then_inc(cols_fix, 1)
                    nfix += 1
            dve.wait_ge(cols_fix, nfix)
            for l in range(DEPTH):
                v = bmod2[:, l * MODT:(l + 1) * MODT, :].rearrange("p (i k) s -> p i (k s)", i=3)
                V.tensor_scalar(v[:, :, 16:32], v[:, :, 16:32], 1.0, None, ALU.add).then_inc(cols_fix, 1)
                for r in (0, 24):
                    w = vec[:, l, 1, r:r + (24 if l < DEPTH - 1 else 16)]
                    V.tensor_scalar(w, w, ALPHA, None, ALU.mult).then_inc(cols_fix, 1)
                nfix += 3
            for i in range(4):
                nxt(i)
            dve.wait_ge(cols_fix, nfix)
            mod_cols(0, 0, 0, 0, 4)
            with dve.Fori(0, MOD_FIRST // 4 - 1) as it:
                for i in range(4):
                    nxt(4 + i, it, 4)
                mod_cols(4, it, 4, 1, 4)

            def filters():
                for l in range(DEPTH):
                    B = FV * l

                    def sine_arg(i):
                        b = col(l, ("hy_b1", "hy_b2")[i], 0, slice(0, FH))
                        fr = col(l, "hy_f", i, slice(0, FH))
                        dve.wait_ge(f_mm, FM * l + i + 1)
                        c = B + FS * i
                        V.tensor_scalar(farg, bank[i][0:FH, 0:SEQ], b, fr, ALU.add, ALU.mult).then_inc(f_v, 1)
                        dve.wait_ge(f_v, c + 1)
                        V.tensor_scalar(fk, farg, 1.0 / TWO_PI, ROUND, ALU.mult, ALU.add).then_inc(f_v, 1)
                        dve.wait_ge(f_v, c + 2)
                        V.tensor_scalar(fk, fk, ROUND, -PI_HI, ALU.subtract, ALU.mult).then_inc(f_v, 1)
                        dve.wait_ge(f_v, c + 3)
                        V.tensor_tensor(farg, farg, fk, ALU.add).then_inc(f_v, 1)
                        dve.wait_ge(f_v, c + 4)
                        V.scalar_tensor_tensor(out=farg, in0=fk, scalar=PI_LO / PI_HI, in1=farg, op0=ALU.mult,
                                               op1=ALU.add).then_inc(f_v, 1)
                        dve.wait_ge(f_v, c + 5)
                        V.tensor_scalar(farg, farg, PI_IN, -PI_IN, ALU.min, ALU.max).then_inc(f_v, 1)

                    sine_arg(0)
                    sine_arg(1)
                    c = B + 2 * FS
                    for t in range(2):
                        for o in range(ORDER):
                            dve.wait_ge(f_mm, FM * l + 2 + 2 * t + o + 1)
                            dve.wait_ge(f_v, c)
                            V.tensor_tensor(filt[:, o, :, :], bank[2 + o][:].rearrange("p (r c) -> p r c", r=2),
                                            decay[:, t, :, :], ALU.mult).then_inc(f_v, 1)
                            c += 1
                            dve.wait_ge(f_v, c)
                            V.tensor_tensor(hp[:, t, o, :], filt[:, o, 0, :], filt[:, o, 1, :],
                                            ALU.add).then_inc(f_v, 1)
                            V.tensor_tensor(hm[:, t, o, :], filt[:, o, 0, :], filt[:, o, 1, :],
                                            ALU.subtract).then_inc(f_v, 1)
                            c += 2
                    dve.wait_ge(f_mm, FM * l + 7)
                    V.tensor_scalar(fn, bank[4][:], 0.5, 1e-6, ALU.mult, ALU.add).then_inc(f_v, 1)
                    dve.wait_ge(f_a, 5 * (l + 1))
                    V.reciprocal(fn, fn).then_inc(f_v, 1)
                    dve.wait_ge(f_v, B + 2 * FS + 14)
                    for r in range(2):
                        for f in range(2):
                            dve.wait_ge(f_mm, FM * l + 8 + 2 * r + f)
                            V.tensor_tensor(spec[:, l, r, f, :, :].rearrange("p o c -> p (o c)"),
                                            bank[2 * r + f][:], fn, ALU.mult).then_inc(f_v, 1)

            def stats(n):
                T = lnt(n)
                eps = LN_EPS if n % 2 else LN_EPS * ALPHA * ALPHA
                dve.wait_ge(stat_mm, 2 * n + 2)
                dve.wait_ge(stat_cp, 2 * n + 2)
                V.tensor_tensor(var[:, 0:T], bank[1][:, 0:T], var[:, 0:T], ALU.subtract).then_inc(stat_v, 1)
                dve.wait_ge(stat_v, 4 * n + 1)
                V.tensor_scalar(var[:, 0:T], var[:, 0:T], 0.0, eps, ALU.max, ALU.add).then_inc(stat_v, 1)
                dve.wait_ge(stat_sd, n + 1)
                V.reciprocal(rstd[:, 0:T], var[:, 0:T]).then_inc(stat_v, 1)
                dve.wait_ge(stat_v, 4 * n + 3)
                V.tensor_tensor(nmr[:, 0:T], mean[:, 0:T], rstd[:, 0:T], ALU.mult).then_inc(stat_v, 1)

            def apply_post(n):
                T = lnt(n)
                dve.wait_ge(stat_v, 4 * n + 4)
                for k in range(KD):
                    if k >= 2:
                        dve.wait_ge(x_tile, 8 * ((n + 1) // 2) + k - 1)
                    V.tensor_tensor(tt[k % 2][:, 0:T], X[:, k, 0:T], rstd[:, 0:T], ALU.mult).then_inc(t_mul, 1)
                    dve.wait_ge(t_mul, 8 * n + k + 1)
                    V.tensor_tensor(tt[k % 2][:, 0:T], tt[k % 2][:, 0:T], nmr[:, 0:T],
                                    ALU.subtract).then_inc(t_sub, 1)

            def apply_mod(n):
                T = lnt(n)

                def low(k):
                    dve.wait_ge(h_hi, 4 * n + k + 1)
                    V.tensor_tensor(Hl[:, k, 0:T], sq[k % 2][:, 0:T], Hh[:, k, 0:T].bitcast(F32),
                                    ALU.subtract).then_inc(h_lo, 1)

                for k in range(KD):
                    if k >= 2:
                        low(k - 2)
                    V.tensor_tensor(tt[k % 2][:, 0:T], X[:, k, 0:T], rstd[:, 0:T], ALU.mult).then_inc(t_mul, 1)
                low(KD - 2)
                low(KD - 1)

            def post(kind, x, u, it, per, f, c, nbody, nm, q0, last):
                T = ffn_tok(f)
                if kind == "g":
                    J = f * JF + sum(CHUNKS[:c]) + x
                    dve.wait_ge(silu_done, J + 1 + it * 2)
                    V.tensor_tensor(sq[x][:, 0:T], tt[x][:, 0:T], bank[2 * x][:, 0:T],
                                    ALU.mult).then_inc(prod_done, 1)
                    dve.wait_ge(u_hi, J + 1 + it * 2)
                    V.tensor_tensor(Ul[:, bass.ds(it * 2 + x, 1), 0:T].rearrange("p o t -> p (o t)"),
                                    sq[x][:, 0:T],
                                    Uh[:, bass.ds(it * 2 + x, 1), 0:T].rearrange("p o t -> p (o t)").bitcast(F32),
                                    ALU.subtract).then_inc(u_lo, 1)
                if kind == "o":
                    dve.wait_ge(unit_done, u + 1 + it * per)
                    y = Y[:, bass.ds(it * 4 + x, 1), 0:T].rearrange("p o t -> p (o t)")
                    if c == 0:
                        V.tensor_copy(y, bank[4 + x % 2][:, 0:T]).then_inc(out_evac, 1)
                    else:
                        V.tensor_tensor(y, bank[4 + x % 2][:, 0:T], y, ALU.add).then_inc(out_evac, 1)

            def n_evac(n):
                l, sub = n // 6, (n % 6) // 2
                return 56 * l + (16, 24, 48)[sub]

            def tail(n, m, u, y):
                T = lnt(n)
                l = n // 6
                dve.wait_ge(unit_done, u + 1)
                if y is None:
                    V.tensor_scalar(tt[m % 2][:, 0:T], bank[4 + m % 2][:, 0:T], col(l, "b_out", m), None,
                                    ALU.add).then_inc(out_evac, 1)
                else:
                    V.tensor_tensor(tt[m % 2][:, 0:T], bank[4 + m % 2][:, 0:T], y, ALU.add).then_inc(out_evac, 1)
                dve.wait_ge(out_evac, FREE + n_evac(n) + m + 1)
                for s in range(T // SEQ):
                    t = slice(s * SEQ, (s + 1) * SEQ)
                    i = V.scalar_tensor_tensor(out=X[:, m, t], in0=tt[m % 2][:, t], scalar=gate[:, m, s:s + 1],
                                               in1=X[:, m, t], op0=ALU.mult, op1=ALU.add)
                i.then_inc(resid, 1)

            def set_gate(n, mod_bodies):
                l, sub = n // 6, (n % 6) // 2
                q = l * MODT + 24 * sub + 16
                dve.wait_ge(mod_done, mod_bodies)
                if n > 1:
                    dve.wait_ge(resid, 8 * (n // 2))
                V.tensor_scalar(gate[:], modv[:, q:q + 8, :], 1.0 if sub == 1 else 0.5, None,
                                ALU.mult).then_inc(gate_rdy, 1)
                dve.wait_ge(gate_rdy, n // 2 + 2)

            def ffn(f):
                l, s = f // 2, f % 2
                n = 6 * l + (1 if s == 0 else 5)
                for c, nj in enumerate(CHUNKS):
                    u0, q0 = AT["in", f, c], MODQ["in", f, c]
                    nm = MOD_IN[f][c]
                    body = body_in(nm)
                    nb_ = modbase(f, "in", c)
                    with dve.Fori(0, nj // 2) as it:
                        for i, (kind, x) in enumerate(body):
                            nxt(u0 + i, it, len(body))
                            post(kind, x, u0 + i, it, len(body), f, c, 0, 0, 0, False)
                        if nm:
                            mod_cols(q0, it, 4, nb_, nm)
                    u0, q0 = AT["out", f, c], MODQ["out", f, c]
                    nm = MOD_OUT[f][c]
                    body = body_out(nm)
                    nb_ = modbase(f, "out", c)
                    if c < len(CHUNKS) - 1:
                        with dve.Fori(0, 2) as it:
                            for i, (kind, x) in enumerate(body):
                                nxt(u0 + i, it, len(body))
                                post(kind, x, u0 + i, it, len(body), f, c, 0, 0, 0, False)
                            if nm:
                                mod_cols(q0, it, 2, nb_, nm)
                    else:
                        set_gate(n, nb_)
                        for it in range(2):
                            for i, (kind, x) in enumerate(body):
                                u = u0 + it * len(body) + i
                                nxt(u)
                                if kind == "o":
                                    m = 4 * it + x
                                    tail(n, m, u, Y[:, m, 0:ffn_tok(f)])
                            if nm:
                                mod_cols(q0 + 2 * it, 0, 0, nb_ + it, nm)

            def mixer(l):
                S = streams(l)
                T = S * SEQ
                n = 6 * l + 3
                ct, ht, st = 2 * CONF_K * l, 24 * l * 0 + NHT * l, NST * l
                nw = N_WIN * l
                dve.wait_ge(h_lo, 24 * l + 16)
                for v, w, L in ((cpad, PADC, 2 * PADC + SEQ), (scpad, 1, SEQ + 2), (hvpad, 1, SEQ + 2)):
                    V.memset(v[:, :, :, 0:w], 0.0).then_inc(pads, 1)
                    V.memset(v[:, :, :, L - w:L], 0.0).then_inc(pads, 1)
                dve.wait_ge(pads, 6 * (l + 1))

                def conf_tap(j):
                    nonlocal ct
                    for i in range(BT):
                        src = cpad[:, i, 0:S, j:j + SEQ]
                        dst = cacc[:, i, 0:T].rearrange("p (s t) -> p s t", s=S)
                        w = col(l, "conf_w", BT * j + i)
                        if j == 0:
                            dve.wait_ge(cglu, 2 * (l + 1))
                            V.tensor_scalar(dst, src, w, col(l, "conf_b", i), ALU.mult, ALU.add).then_inc(ctap, 1)
                        else:
                            dve.wait_ge(ctap, ct - 1)
                            V.scalar_tensor_tensor(out=dst, in0=src, scalar=w, in1=dst, op0=ALU.mult,
                                                   op1=ALU.add).then_inc(ctap, 1)
                        ct += 1

                def hy_short(i):
                    nonlocal ht
                    dst = hvc[:, i, 0:T].rearrange("p (s t) -> p s t", s=S)
                    dve.wait_ge(win_evac, nw + 5 + i)
                    for j in range(3):
                        src = hvpad[:, i, 0:S, j:j + SEQ]
                        w = col(l, "hs_w", 6 * j + i)
                        if j == 0:
                            V.tensor_scalar(dst, src, w, col(l, "hs_b", i), ALU.mult, ALU.add).then_inc(htap, 1)
                        else:
                            dve.wait_ge(htap, ht)
                            V.scalar_tensor_tensor(out=dst, in0=src, scalar=w, in1=dst, op0=ALU.mult,
                                                   op1=ALU.add).then_inc(htap, 1)
                        ht += 1

                u0 = AT["win", l]
                tap = 0
                for i, m in enumerate(WIN_ORDER):
                    nxt(u0 + i)
                    if m in (2, 3):
                        dve.wait_ge(win_evac, nw + i + 1)
                        V.tensor_tensor(cpad[:, m - 2, 0:S, PADC:PADC + SEQ],
                                        tmpa[:, m - 2, 0:T].rearrange("p (s t) -> p s t", s=S),
                                        cacc[:, m - 2, 0:T].rearrange("p (s t) -> p s t", s=S),
                                        ALU.mult).then_inc(cglu, 1)
                    for _ in range(2):
                        if i >= 4 and tap < CONF_K:
                            conf_tap(tap)
                            tap += 1
                    if i == 5:
                        dve.wait_ge(btab_cp, 4 * (l + 1))
                    if 5 <= i < 11:
                        hy_short(i - 5)
                    if m >= 14 and m < 16:
                        j = m - 14
                        dve.wait_ge(win_evac, nw + i + 1)
                        v = scpad[:, j, 0:S, 1:SEQ + 1]
                        V.tensor_tensor(v, v, tmpa[:, j, 0:T].rearrange("p (s t) -> p s t", s=S),
                                        ALU.mult).then_inc(stap, 1)
                        st += 1
                while tap < CONF_K:
                    conf_tap(tap)
                    tap += 1
                for j in range(3):
                    for i in range(BT):
                        dst = tmpa[:, i, 0:T].rearrange("p (s t) -> p s t", s=S)
                        src = scpad[:, i, 0:S, j:j + SEQ]
                        w = col(l, "sc_w", BT * j + i)
                        dve.wait_ge(stap, st - 1)
                        if j == 0:
                            V.tensor_scalar(dst, src, w, None, ALU.mult).then_inc(stap, 1)
                        else:
                            V.scalar_tensor_tensor(out=dst, in0=src, scalar=w, in1=dst, op0=ALU.mult,
                                                   op1=ALU.add).then_inc(stap, 1)
                        st += 1
                for i in range(BT):
                    dve.wait_ge(stap, st - 1)
                    V.tensor_tensor(tmpa[:, i, 0:T], tmpa[:, i, 0:T], sbb[:, i, 0:T], ALU.mult).then_inc(stap, 1)
                    st += 1

                def branch_lo(b, src, k):
                    dve.wait_ge(b_hi, 4 * l + k)
                    V.tensor_tensor(Bl[:, b, :, 0:T], src[:, :, 0:T], Bh[:, b, :, 0:T].bitcast(F32),
                                    ALU.subtract).then_inc(b_lo, 1)

                branch_lo(2, tmpa, 1)
                c0 = NCV * l
                dve.wait_ge(c_mm, 2 * l + 2)
                dve.wait_ge(c_cp, 2 * l + 2)
                V.tensor_tensor(cvar[:, 0:T], bank[1][:, 0:T], cvar[:, 0:T], ALU.subtract).then_inc(c_v, 1)
                dve.wait_ge(c_v, c0 + 1)
                V.tensor_scalar(cvar[:, 0:T], cvar[:, 0:T], 0.0, LN_EPS, ALU.max, ALU.add).then_inc(c_v, 1)
                dve.wait_ge(c_sd, l + 1)
                V.reciprocal(crstd[:, 0:T], cvar[:, 0:T]).then_inc(c_v, 1)
                dve.wait_ge(c_v, c0 + 3)
                V.tensor_tensor(cnmr[:, 0:T], cmean[:, 0:T], crstd[:, 0:T], ALU.mult).then_inc(c_v, 1)
                dve.wait_ge(c_v, c0 + 4)
                for i in range(BT):
                    V.tensor_tensor(cacc[:, i, 0:T], cacc[:, i, 0:T], crstd[:, 0:T], ALU.mult).then_inc(c_v, 1)
                    dve.wait_ge(c_v, c0 + 5 + 2 * i)
                    V.tensor_tensor(cacc[:, i, 0:T], cacc[:, i, 0:T], cnmr[:, 0:T],
                                    ALU.subtract).then_inc(c_v, 1)
                branch_lo(0, cacc, 2)
                bl = blocks(l)
                nb = len(bl)
                g0 = NB0 * l
                gv = AV0 * l
                for n_ in range(nb + 1):
                    if n_ < nb:
                        s, h, q = bl[n_]
                        r = n_ % 2
                        dve.wait_ge(at_s, g0 + n_ + 1)
                        if s == 0:
                            V.scalar_tensor_tensor(out=sbuf_s[r][:, 0:SEQ], in0=bank[4 + r][:, 0:SEQ], scalar=SCALE,
                                                   in1=btab[:, q, h, :, :].rearrange("p r c -> p (r c)"),
                                                   op0=ALU.mult, op1=ALU.add).then_inc(at_v, 1)
                            V.tensor_scalar(sbuf_s[r][:, SEQ:TOK], bank[4 + r][:, SEQ:TOK], SCALE, None,
                                            ALU.mult).then_inc(at_v, 1)
                            gv += 2
                            K = TOK
                        else:
                            V.tensor_scalar(sbuf_s[r][:, 0:SEQ], bank[4 + r][:, 0:SEQ], SCALE, None,
                                            ALU.mult).then_inc(at_v, 1)
                            gv += 1
                            K = SEQ
                        dve.wait_ge(at_v, gv)
                        V.tensor_reduce(out=nmax[:, r:r + 1], in_=sbuf_s[r][:, 0:K], axis=AX.X, op=ALU.max,
                                        negate=True).then_inc(at_m, 1)
                    m = n_ - 1
                    if 0 <= m:
                        r = m % 2
                        K = TOK if bl[m][0] == 0 else SEQ
                        dve.wait_ge(at_e, g0 + m + 1)
                        V.reciprocal(prec[:, r:r + 1], psumr[:, r:r + 1]).then_inc(at_r, 1)
                        dve.wait_ge(at_r, g0 + m + 1)
                        V.tensor_scalar(sbuf_p[r][:, 0:K], sbuf_p[r][:, 0:K], prec[:, r:r + 1], None,
                                        ALU.mult).then_inc(at_n, 1)
                branch_lo(1, obuf, 3)
                pc = 12 * ORDER * l
                zc = 4 * ORDER * l
                dve.wait_ge(htap, NHT * (l + 1))
                for o in range(ORDER):
                    N = S * WB
                    for f in range(2):
                        kr = spec[:, l, 0, f, o, :].unsqueeze(1).to_broadcast([P, S, WB])
                        ks = spec[:, l, 1, f, o, :].unsqueeze(1).to_broadcast([P, S, WB])

                        def v3(x):
                            return x[:, 0:N].rearrange("p (s c) -> p s c", s=S)

                        dve.wait_ge(hy_f, 4 * (ORDER * l + o) + 2 * f + 2)
                        for out_, x0, k0, x1, k1, op in ((0, f, kr, 2 + f, ks, ALU.subtract),
                                                         (1, f, ks, 2 + f, kr, ALU.add)):
                            if pc:
                                dve.wait_ge(hy_p, pc)
                            V.tensor_tensor(v3(hprod[0]), v3(bank[x0][:, :]), k0, ALU.mult).then_inc(hy_p, 1)
                            V.tensor_tensor(v3(hprod[1]), v3(bank[x1][:, :]), k1, ALU.mult).then_inc(hy_p, 1)
                            pc += 2
                            dve.wait_ge(hy_p, pc)
                            V.tensor_tensor(ysp[:, out_, f, 0:N], hprod[0][:, 0:N], hprod[1][:, 0:N],
                                            op).then_inc(hy_p, 1)
                            pc += 1
                    for i in range(BT):
                        dve.wait_ge(hy_i, 2 * (ORDER * l + o) + i + 1)
                        V.scalar_tensor_tensor(out=hvc[:, i, 0:T], in0=hvc[:, i, 0:T],
                                               scalar=col(l, "hy_bias", BT * o + i), in1=bank[i][:, 0:T],
                                               op0=ALU.mult, op1=ALU.add).then_inc(hy_z, 1)
                        zc += 1
                        dve.wait_ge(hy_z, zc)
                        V.tensor_tensor(hvc[:, i, 0:T], hvc[:, i, 0:T], hvc[:, BT * (1 + o) + i, 0:T],
                                        ALU.mult).then_inc(hy_z, 1)
                        zc += 1
                branch_lo(3, hvc[:, 0:2, :], 4)
                u0 = AT["gate", l]
                with dve.Fori(0, KD // 2) as it:
                    for d in range(2):
                        base = mix_at(l, d)
                        for i, b in enumerate((0, 1, None, 2, 3)):
                            u = u0 + 5 * d + i
                            nxt(u, it, 10)
                            for b in {2: (0, 1), 3: (2,), 4: (3,)}.get(i, ()):
                                dve.wait_ge(sig_done, FREE_MIX + 32 * l + 4 * d + b + 1 + it * 8)
                                if b == 0:
                                    dve.wait_ge(unit_done, u0 + 5 * d + 3 + it * 10)
                                    V.tensor_tensor(acc1[:, 0:T], tt[0][:, 0:T], bank[0][:, 0:T],
                                                    ALU.mult).then_inc(mix_step, 1)
                                    continue
                                dve.wait_ge(mix_step, base + 2 * b - 1 + it * 14)
                                V.tensor_tensor(acc2[:, 0:T], tt[b % 2][:, 0:T], bank[b][:, 0:T],
                                                ALU.mult).then_inc(mix_step, 1)
                                dve.wait_ge(mix_step, base + 2 * b + it * 14)
                                V.tensor_tensor(acc1[:, 0:T], acc1[:, 0:T], acc2[:, 0:T],
                                                ALU.add).then_inc(mix_step, 1)
                        dve.wait_ge(m_hi, 8 * l + d + 1 + it * 2)
                        V.tensor_tensor(Ul[:, bass.ds(it * 2 + d, 1), 0:T].rearrange("p o t -> p (o t)"),
                                        acc1[:, 0:T],
                                        Uh[:, bass.ds(it * 2 + d, 1), 0:T].rearrange("p o t -> p (o t)").bitcast(F32),
                                        ALU.subtract).then_inc(m_lo, 1)
                set_gate(n, modbase(2 * l + 1, "in", 0))
                u0 = AT["wout", l]
                for m in range(KD):
                    nxt(u0 + m)
                    tail(n, m, u0 + m, None)

            filters()
            stats(0)
            apply_mod(0)
            for l in range(DEPTH):
                for sub in range(3):
                    n = 6 * l + 2 * sub + 1
                    if sub == 1:
                        mixer(l)
                    else:
                        ffn(2 * l + sub // 2)
                    stats(n)
                    apply_post(n)
                    if n < NLN - 1:
                        stats(n + 1)
                        apply_mod(n + 1)

        @block.tensor
        def _(pe):
            T_ = nc.tensor

            def split3(o, k, s, xh, xl, first, last):
                T_.matmul(o, wh[s][:, k, :], xh, start=first, stop=False)
                T_.matmul(o, wh[s][:, k, :], xl, start=False, stop=False)
                return T_.matmul(o, wl[s][:, k, :], xh, start=False, stop=last)

            def split_in(u, it=0, per=0):
                pe.wait_ge(lo_done, u + 1 + it * per)

            def mod_unit(u, x, it=0, per=0):
                split_in(u, it, per)
                s = u % 2
                for k in range(KD):
                    T_.matmul(bank[6][0:4, x * P:(x + 1) * P], S4[:, k, :], wh[s][:, k, :], start=(k == 0), stop=False)
                    i = T_.matmul(bank[6][0:4, x * P:(x + 1) * P], S4[:, k, :], wl[s][:, k, :], start=False,
                                  stop=(k == KD - 1))
                i.then_inc(unit_done, 1)

            def mod_turn(nbody, nm, it=0):
                pe.wait_ge(mrow_done, nbody + 1 + it)
                if nbody:
                    pe.wait_ge(mod_done, nbody + it)
                for x in range(nm):
                    i = T_.matmul(bank[7][:, 2 * x:2 * x + 2], modrow[:, x, :], sel[:], start=True, stop=True)
                i.then_inc(mcol_mm, 1)

            pe.wait_ge(s_c, 48)
            T_.transpose(bank[2][:, 0:16], crow, ident[0:16, 0:16]).then_inc(turned, 1)
            pe.wait_ge(s_const, 16 * (5 + DEPTH * 19))
            for l in range(DEPTH):
                for g in range(NG):
                    i = T_.transpose(bank[l][:, g * P:(g + 1) * P], vrow[:, l, g, :], ident)
                i.then_inc(turned, 1)
            pe.wait_ge(s4hi, 2)
            pe.wait_ge(s4lo, 2)
            for x in range(4):
                mod_unit(x, x)
            pe.wait_ge(s_xin, 64)
            for k in range(KD):
                if k >= 2:
                    pe.wait_ge(x_tile, k - 1)
                for t in range(4):
                    i = T_.transpose(bank[4 + k % 2][:, t * P:(t + 1) * P], xrow[:, t, k * P:(k + 1) * P], ident)
                i.then_inc(x_turned, 1)
            mod_turn(0, 4)
            with pe.Fori(0, MOD_FIRST // 4 - 1) as it:
                for x in range(4):
                    mod_unit(4 + x, x, it, 4)
                mod_turn(1, 4, it)

            def filters():
                for l in range(DEPTH):
                    pe.wait_ge(cols_fix, 10)
                    if l:
                        pe.wait_ge(f_v, FV * l)
                    T_.matmul(bank[0][0:FH, 0:SEQ], fw1[:, l, :], zT, start=True, stop=True).then_inc(f_mm, 1)
                    pe.wait_ge(f_a, 5 * l + 1)
                    T_.matmul(bank[1][0:FH, 0:SEQ], fw2[:, l, :], fh, start=True, stop=True).then_inc(f_mm, 1)
                    pe.wait_ge(f_a, 5 * l + 2)
                    for t in range(2):
                        for o in range(ORDER):
                            if t:
                                pe.wait_ge(f_v, FV * l + 2 * FS + 3 * o + 1)
                            T_.matmul(bank[2 + o][:], fh[:, t * P:(t + 1) * P], fw3[:, l, o * 512:(o + 1) * 512],
                                      start=True, stop=True).then_inc(f_mm, 1)
                    pe.wait_ge(f_a, 5 * l + 4)
                    for i in range(4):
                        m = T_.matmul(bank[4][:], ones, hsq[:, i // 2, i % 2, :], start=(i == 0), stop=(i == 3))
                    m.then_inc(f_mm, 1)
                    for r, h in ((0, hp), (1, hm)):
                        for f in range(2):
                            for t in range(2):
                                m = T_.matmul(bank[2 * r + f][:], dft[:, r, t, f * P:(f + 1) * P],
                                              h[:, t, :, :].rearrange("p o c -> p (o c)"),
                                              start=(t == 0), stop=(t == 1))
                            m.then_inc(f_mm, 1)

            def stats_direct(n):
                T = lnt(n)
                if n == 0:
                    pe.wait_ge(f_v, FV * DEPTH)
                for k in range(KD):
                    pe.wait_ge(x_tile, 8 * (n // 2) + k + 1)
                    m = T_.matmul(bank[0][:, 0:T], invD, X[:, k, 0:T], start=(k == 0), stop=(k == KD - 1))
                m.then_inc(stat_mm, 1)
                pe.wait_ge(acc_step, 24 * (n // 2) + 8)
                T_.matmul(bank[1][:, 0:T], invD, acc2[:, 0:T], start=True, stop=True).then_inc(stat_mm, 1)

            def stats_sums(n):
                T = lnt(n)
                pe.wait_ge(acc_step, 24 * (n // 2) + 8 + 15)
                T_.matmul(bank[0][:, 0:T], invD, acc1[:, 0:T], start=True, stop=True).then_inc(stat_mm, 1)
                pe.wait_ge(acc_step, 24 * (n // 2) + 8 + 16)
                T_.matmul(bank[1][:, 0:T], invD, acc2[:, 0:T], start=True, stop=True).then_inc(stat_mm, 1)

            def ffn(f):
                T = ffn_tok(f)
                l, s = f // 2, f % 2
                n = 6 * l + (0 if s == 0 else 4)
                for c, nj in enumerate(CHUNKS):
                    J0 = f * JF + sum(CHUNKS[:c])
                    u0 = AT["in", f, c]
                    nm = MOD_IN[f][c]
                    body = body_in(nm)
                    nb_ = modbase(f, "in", c)
                    with pe.Fori(0, nj // 2) as it:
                        first_main = True
                        for i, (kind, x) in enumerate(body):
                            u = u0 + i
                            if kind == "m":
                                mod_unit(u, x, it, len(body))
                                continue
                            if kind == "a":
                                pe.wait_ge(prod_done, FREE + J0 + x - 1 + it * 2)
                            split_in(u, it, len(body))
                            o = bank[2 * x + (kind == "g")][:, 0:T]
                            for k in range(KD):
                                if c == 0 and first_main:
                                    pe.wait_ge(h_lo, 4 * n + k + 1)
                                m = split3(o, k, u % 2, Hh[:, k, 0:T], Hl[:, k, 0:T], k == 0, k == KD - 1)
                            first_main = False
                            m.then_inc(unit_done, 1)
                        if nm:
                            mod_turn(nb_, nm, it)
                    u0 = AT["out", f, c]
                    nm = MOD_OUT[f][c]
                    body = body_out(nm)
                    nb_ = modbase(f, "out", c)
                    pe.wait_ge(u_lo, J0 + nj)
                    ev = n_evac_pe(f, c)

                    with pe.Fori(0, 2) as it:
                        for i, (kind, x) in enumerate(body):
                            u = u0 + i
                            if kind == "m":
                                mod_unit(u, x, it, len(body))
                                continue
                            pe.wait_ge(out_evac, FREE + ev + x - 1 + it * 4)
                            split_in(u, it, len(body))
                            for k in range(nj):
                                m = split3(bank[4 + x % 2][:, 0:T], k, u % 2, Uh[:, k, 0:T], Ul[:, k, 0:T],
                                           k == 0, k == nj - 1)
                            m.then_inc(unit_done, 1)
                        if nm:
                            mod_turn(nb_, nm, it)

            def n_evac_pe(f, c):
                return 56 * (f // 2) + (32 if f % 2 else 0) + 8 * c

            def mixer(l):
                S = streams(l)
                T = S * SEQ
                n = 6 * l + 2
                u0 = AT["win", l]
                nw = N_WIN * l
                for i, m in enumerate(WIN_ORDER):
                    u = u0 + i
                    split_in(u)
                    if i >= 4:
                        pe.wait_ge(win_evac, nw + i - 3)
                    TT = win_tokens(l, m)
                    if 8 <= m < 10:
                        for t in range(4):
                            o = bank[i % 4][:, t * P:(t + 1) * P]
                            tk = slice(t * P, (t + 1) * P)
                            for k in range(KD):
                                T_.matmul(o, Hh[:, k, tk], wh[u % 2][:, k, :], start=(k == 0), stop=False)
                                T_.matmul(o, Hh[:, k, tk], wl[u % 2][:, k, :], start=False, stop=False)
                                mm = T_.matmul(o, Hl[:, k, tk], wh[u % 2][:, k, :], start=False, stop=(k == KD - 1))
                    else:
                        for k in range(KD):
                            if i == 0:
                                pe.wait_ge(h_lo, 4 * n + k + 1)
                            mm = split3(bank[i % 4][:, 0:TT], k, u % 2, Hh[:, k, 0:TT], Hl[:, k, 0:TT], k == 0,
                                        k == KD - 1)
                    mm.then_inc(unit_done, 1)
                    if i == 2:
                        pe.wait_ge(r_mask, 8 * (l + 1))
                        for q in range(2):
                            for h2 in range(2):
                                T_.matmul(bank[4 + 2 * q + h2][:], flip[:],
                                          rtab[:, q, 2 * h2:2 * h2 + 2, :, :].rearrange("p h r c -> p (h r c)"),
                                          start=True, stop=True).then_inc(flipped, 1)
                pe.wait_ge(ctap, 2 * CONF_K * (l + 1))
                pe.wait_ge(win_evac, N_WIN * (l + 1))
                for i in range(BT):
                    mm = T_.matmul(bank[0][:, 0:T], invB, cacc[:, i, 0:T], start=(i == 0), stop=(i == BT - 1))
                mm.then_inc(c_mm, 1)
                pe.wait_ge(c_sq, l + 1)
                for i in range(BT):
                    mm = T_.matmul(bank[1][:, 0:T], invB, csq[:, i, 0:T], start=(i == 0), stop=(i == BT - 1))
                mm.then_inc(c_mm, 1)
                bl = blocks(l)
                nb = len(bl)
                g0 = NB0 * l
                nv = 0
                gv = [AV0 * l]
                for s, h, q in bl:
                    gv.append(gv[-1] + (2 if s == 0 else 1))
                pe.wait_ge(btab_cp, 4 * (l + 1))
                for n_ in range(nb + 3):
                    if n_ < nb:
                        s, h, q = bl[n_]
                        rr = slice(DH * (h % 2), DH * (h % 2) + DH)
                        qs = qk[rr, h // 2, s * SEQ + q * P:s * SEQ + (q + 1) * P]
                        if s == 0:
                            ks, K = qk[rr, 2 + h // 2, 0:TOK], TOK
                        else:
                            ks, K = qk[rr, 2 + h // 2, SEQ:TOK], SEQ
                        if n_ >= 2:
                            pe.wait_ge(at_v, gv[n_ - 1])
                        T_.matmul(bank[4 + n_ % 2][:, 0:K], qs, ks, start=True, stop=True).then_inc(at_s, 1)
                    m = n_ - 2
                    if 0 <= m < nb:
                        kt = 4 if bl[m][0] == 0 else 2
                        pe.wait_ge(at_n, g0 + m + 1)
                        if m:
                            pe.wait_ge(at_tc, g0 + m)
                        for k in range(kt):
                            mm = T_.transpose(bank[6][:, k * P:(k + 1) * P], sbuf_p[m % 2][:, k * P:(k + 1) * P], ident)
                        mm.then_inc(at_t, 1)
                    m = n_ - 3
                    if 0 <= m < nb:
                        s, h, q = bl[m]
                        kt = 4 if s == 0 else 2
                        rr = slice(DH * (h % 2), DH * (h % 2) + DH)
                        pe.wait_ge(at_tc, g0 + m + 1)
                        if m >= 2:
                            pe.wait_ge(at_oc, g0 + m - 1)
                        for k in range(kt):
                            mm = T_.matmul(bank[7 - 4 * (m % 2)][rr, 0:P],
                                           vtok[:, 2 * s + k, h * DH:(h + 1) * DH], sbuf_pT[m % 2][:, k, :],
                                           start=(k == 0), stop=(k == kt - 1))
                        mm.then_inc(at_o, 1)
                N = S * WB
                pe.wait_ge(htap, NHT * (l + 1))
                pe.wait_ge(c_v, NCV * l + 1)
                pe.wait_ge(at_oc, g0 + nb)
                for o in range(ORDER):
                    e = ORDER * l + o
                    if o:
                        pe.wait_ge(hy_z, 4 * e)
                    for t in range(2):
                        for s in range(S):
                            for i in range(BT):
                                mm = T_.transpose(bank[t][:, s * WB + i * P:s * WB + (i + 1) * P],
                                                  hvc[:, i, s * SEQ + t * P:s * SEQ + (t + 1) * P], ident)
                        mm.then_inc(hy_t, 1)
                    pe.wait_ge(hy_tc, 2 * e + 2)
                    for f in range(2):
                        for r in range(2):
                            for t in range(2):
                                mm = T_.matmul(bank[2 * r + f][:, 0:N], dft[:, r, t, f * P:(f + 1) * P],
                                               uT[:, t, 0:N], start=(t == 0), stop=(t == 1))
                            mm.then_inc(hy_f, 1)
                    pe.wait_ge(hy_p, 12 * (e + 1))
                    for i in range(BT):
                        for s in range(S):
                            for f in range(2):
                                for r in range(2):
                                    mm = T_.matmul(bank[i][:, s * SEQ:(s + 1) * SEQ],
                                                   ysp[:, r, f, s * WB + i * P:s * WB + (i + 1) * P],
                                                   dft[:, 2 + r, f, :], start=(f == 0 and r == 0),
                                                   stop=(f == 1 and r == 1))
                        mm.then_inc(hy_i, 1)
                pe.wait_ge(b_lo, 4 * (l + 1))
                u0 = AT["gate", l]
                pe.wait_ge(at_oc, g0 + nb)

                def gate_unit(u, b, it, per):
                    split_in(u, it, per)
                    for k in range(KD):
                        mm = split3(bank[4 + b][:, 0:T], k, u % 2, Hh[:, k, 0:T], Hl[:, k, 0:T], k == 0, k == KD - 1)
                    mm.then_inc(unit_done, 1)

                with pe.Fori(0, KD // 2) as it:
                    for d in range(2):
                        for i, b in enumerate((0, 1, None, 2, 3)):
                            u = u0 + 5 * d + i
                            if b is not None:
                                pe.wait_ge(sig_done, FREE_MIX + 32 * l + 4 * d + b - 3 + it * 8)
                                gate_unit(u, b, it, 10)
                                continue
                            split_in(u, it, 10)
                            pe.wait_ge(mix_step, mix_at(l, d) + it * 14)
                            for b4 in range(4):
                                for k in range(BT):
                                    mm = split3(bank[b4][:, 0:T], 2 * b4 + k, u % 2, Bh[:, b4, k, 0:T],
                                                Bl[:, b4, k, 0:T], k == 0, k == BT - 1)
                            mm.then_inc(unit_done, 1)
                u0 = AT["wout", l]
                pe.wait_ge(m_lo, 8 * (l + 1))
                ev = 56 * l + 24
                for m in range(KD):
                    pe.wait_ge(out_evac, FREE + ev + m - 1)
                    split_in(u0 + m)
                    for k in range(KD):
                        mm = split3(bank[4 + m % 2][:, 0:T], k, (u0 + m) % 2, Uh[:, k, 0:T], Ul[:, k, 0:T],
                                    k == 0, k == KD - 1)
                    mm.then_inc(unit_done, 1)

            filters()
            stats_direct(0)
            for l in range(DEPTH):
                for sub in range(3):
                    n = 6 * l + 2 * sub + 1
                    if sub == 1:
                        mixer(l)
                    else:
                        ffn(2 * l + sub // 2)
                    stats_sums(n)
                    if n < NLN - 1:
                        stats_direct(n + 1)
            for i in range(4):
                t, half = i // 2, i % 2
                for k in range(4):
                    pe.wait_ge(x_tile, 8 * (NLN // 2) + 4 * half + k + 1)
                    mm = T_.transpose(bank[4 + i][:, k * P:(k + 1) * P], X[:, 4 * half + k, t * P:(t + 1) * P], ident)
                mm.then_inc(o_turn, 1)


def _tables():
    f32 = np.float32
    eye = np.eye(P, dtype=f32)
    mats = np.stack([eye, np.full((P, P), 1.0 / D, f32), np.full((P, P), 1.0 / WB, f32), np.ones((P, P), f32)], 1)
    sel = np.array([[1, 0], [1, 0], [0, 1], [0, 1]], f32)
    flip = np.zeros((P, P), f32)
    for p in range(P):
        flip[p, (p // GRID_W) * GRID_W + GRID_W - 1 - p % GRID_W] = 1.0
    t = np.arange(SEQ, dtype=np.float64)
    ang = np.outer(t, (t + 0.5) * 2 * np.pi / (2 * SEQ))
    dft = np.stack([np.cos(ang), np.sin(ang), np.cos(ang).T / SEQ, np.sin(ang).T / SEQ])
    dft = dft.reshape(4, 2, P, SEQ).transpose(2, 0, 1, 3).astype(f32)
    tf = np.arange(SEQ, dtype=f32)
    t_norm = tf / f32(SEQ - 1)
    deltas = np.linspace(math.log(1e-2) / 1.5, math.log(1e-2) / 0.3, WB, dtype=f32)
    dec = np.exp(-t_norm[:, None] * np.abs(deltas)[None, :]).astype(f32)
    back = dec.copy()
    back[0] = 0.0
    decay = np.stack([dec, back], 1).reshape(2, P, 2, WB).transpose(1, 0, 2, 3)
    bands = np.linspace(1e-4, 15, 16, dtype=f32)
    a = (f32(2.0 * math.pi / SEQ) * tf[:, None]) * bands[None, :]
    zT = np.concatenate([t_norm[:, None], np.cos(a), -np.sin(a)], -1).astype(f32).T
    return {"k_mats": mats, "k_sel": sel, "k_flip": flip, "k_dft": dft, "k_decay": decay, "k_zT": zT}


_INS = ("x", "c", "ctx", "c_ctx", "w_mod", "b_mod", "post_ln_g", "post_ln_b", "ffn_w_in", "ffn_w_out", "w_in", "b_in",
        "conf_dw_w", "conf_dw_b", "conf_ln_g", "conf_ln_b", "conf_w_proj", "na_rpb", "na_w_proj", "sc_conv_w",
        "sc_w_proj", "hy_sconv_w", "hy_sconv_b", "hy_w1", "hy_b1", "hy_w2", "hy_b2", "hy_freq", "hy_w3", "hy_bias",
        "hy_w_proj", "w_out", "b_out")


def kernel(**inputs):
    import concourse.bacc as bacc
    from concourse.bass_utils import run_bass_kernel_spmd as run

    nc = bacc.Bacc("TRN2", target_bir_lowering=False, num_devices=1)
    arrays, aps = {}, {}
    for name, arr in [(n, inputs[n]) for n in _INS] + list(_tables().items()):
        arr = np.ascontiguousarray(arr)
        arrays["in_" + name] = arr
        aps[name] = nc.dram_tensor("in_" + name, arr.shape, mybir.dt.from_np(arr.dtype), kind="ExternalInput").ap()
    out = nc.dram_tensor("out", (1, SEQ, D), F32, kind="ExternalOutput").ap()
    build(nc, aps, out)
    return run(nc, [arrays], core_ids=[0]).results[0]["out"]
```

```python
import math
from contextlib import ExitStack

import numpy as np

import concourse.bass as bass
from concourse import mybir

F32 = mybir.dt.float32
F32R = mybir.dt.float32r
ACT = mybir.ActivationFunctionType
ALU = mybir.AluOpType
AX = mybir.AxisListType

P = 128
D = 1024
KD = D // P
SEQ = 256
TOK = 2 * SEQ
DEPTH = 2
D_FF = 2816
JF = D_FF // P
CHUNKS = (8, 8, 6)
N_MOD = 9
MODT = N_MOD * KD
WB = 256
BT = WB // P
CONF_K = 31
PADC = CONF_K // 2
HEADS = 4
DH = 64
SCALE = DH ** -0.5
GRID_W = 64
WIN_ROWS, WIN_COLS = 8, 16
RPB_R, RPB_C = 2 * WIN_ROWS - 1, 2 * WIN_COLS - 1
ROWS = SEQ // GRID_W
MASKED = -1e30
ORDER = 2
PE_DIM = 33
FH = 64
LN_EPS = 1e-5
ALPHA = (2 * DEPTH) ** 0.25
TWO_PI = 2.0 * math.pi
PI_HI = 6.28125
PI_LO = TWO_PI - PI_HI
PI_IN = 3.1415925
ROUND = 1.5 * 2.0 ** 23
P_IN = 6912
M_G = 22

VROW = {"b_mod": (0, 0), "b_in": (0, 72),
        "ln_g": (1, 0), "ln_b": (1, 24), "conf_w": (1, 48), "sc_w": (1, 110), "conf_b": (1, 116),
        "conf_g": (1, 118), "conf_be": (1, 120), "hy_bias": (1, 122),
        "hs_w": (2, 0), "hs_b": (2, 18), "b_out": (2, 24), "hy_b1": (2, 32), "hy_b2": (2, 33), "hy_f": (2, 34)}
NG = 3

WIN_ORDER = (0, 1, 2, 3, 16, 17, 18, 19, 20, 21, 4, 5, 6, 7, 8, 9, 10, 11, 12, 13, 14, 15)
N_WIN = len(WIN_ORDER)
N_SUB = 2 * DEPTH
MOD_IN = ((4, 4, 4), (4, 4, 4), (4, 0, 0), (0, 0, 0))
MOD_OUT = ((2, 2, 2), (2, 2, 2), (0, 0, 0), (0, 0, 0))
MOD_FIRST = 16


def plan():
    u, q = 0, MOD_FIRST
    at, modq, proj = {}, {}, set()

    def ffn(f):
        nonlocal u, q
        for c, n in enumerate(CHUNKS):
            at["in", f, c], modq["in", f, c] = u, q
            u += (n // 2) * 4
            q += (n // 2) * MOD_IN[f][c]
            at["out", f, c], modq["out", f, c] = u, q
            u += KD
            q += 2 * MOD_OUT[f][c]

    for l in range(DEPTH):
        ffn(2 * l)
        at["win", l] = u
        u += N_WIN
        at["gate", l] = u
        for m in range(KD):
            proj.add(u + 5 * m + 2)
        u += 5 * KD
        at["wout", l] = u
        u += KD
        ffn(2 * l + 1)
    assert q == DEPTH * MODT
    return at, modq, proj, u


AT, MODQ, PROJ, UNITS = plan()


def landed(u):
    return 16 * (u // 2 + 1) + 48 * sum(1 for x in PROJ if x % 2 == u % 2 and x <= u)


def body_in(nmod):
    mains = [("a", 0, 0), ("g", 0, 1), ("a", 1, 2), ("g", 1, 3)]
    return [x for i, w in enumerate(mains) for x in ([("m", i, i)] if nmod else []) + [w]]


def body_out(nmod):
    mains = [("o", i, i) for i in range(4)]
    return [("m", 0, 0)] + mains[:2] + [("m", 1, 1)] + mains[2:] if nmod else mains


def mod_last(f, kind, c):
    later = [(k, cc) for cc in range(len(CHUNKS)) for k in ("in", "out") if (MOD_IN if k == "in" else MOD_OUT)[f][cc]]
    return bool(later) and later[-1] == (kind, c)


def mod_end(f):
    return MODQ["in", f + 1, 0] if f + 1 < N_SUB else DEPTH * MODT


def modbase(f, kind, c):
    n = MOD_FIRST // 4
    for ff in range(N_SUB):
        for cc, j in enumerate(CHUNKS):
            if (ff, "in", cc) == (f, kind, c):
                return n
            n += (j // 2) if MOD_IN[ff][cc] else 0
            if (ff, "out", cc) == (f, kind, c):
                return n
            n += 2 if MOD_OUT[ff][cc] else 0


def win_tokens(l, m):
    return TOK if l < DEPTH - 1 or 6 <= m < 10 else SEQ


def build(nc, a, out):
    ctx = ExitStack()
    with ctx:
        def sb(name, shape, dt=F32):
            return ctx.enter_context(nc.sbuf_tensor(name, shape, dt))

        def sem(name):
            return ctx.enter_context(nc.semaphore(name))

        X = sb("X", [P, KD, TOK])
        Y = sb("Y", [P, KD, TOK])
        Hh = sb("Hh", [P, KD, TOK], F32R)
        Hl = sb("Hl", [P, KD, TOK], F32R)
        with nc.sbuf_tensor("UWORK", [P, 2 * KD * TOK], F32) as Wk:
            pass
        Uh = sb("Uh", [P, KD, TOK], F32R)
        Ul = sb("Ul", [P, KD, TOK], F32R)
        with nc.sbuf_tensor("MWORK", [P, 2, KD, P], F32) as mraw:
            pass
        Bh = sb("Bh", [P, 4, BT, TOK], F32R)
        Bl = sb("Bl", [P, 4, BT, TOK], F32R)
        mwh = [Bh[:, 2 + s, :, :].rearrange("p i (k c) -> p (i k) c", c=P) for s in range(2)]
        mwl = [Bl[:, s, :, :].rearrange("p i (k c) -> p (i k) c", c=P) for s in range(2)]
        raw = [sb(f"raw{s}", [P, KD, P]) for s in range(2)]
        wh = [sb(f"wh{s}", [P, KD, P], F32R) for s in range(2)]
        wl = [sb(f"wl{s}", [P, KD, P], F32R) for s in range(2)]
        spec = sb("spec", [P, DEPTH, 2, 2, ORDER, WB])
        dft = sb("dft", [P, 4, 2, SEQ])
        mats = sb("mats", [P, 4, P])
        flip = sb("flip", [P, P])
        vec = sb("vec", [P, DEPTH, NG, P])
        bmod2 = sb("bmod2", [P, DEPTH * MODT, 2])
        modv = sb("modv", [P, DEPTH * MODT, 2])
        S4 = sb("S4", [P, KD, 4], F32R)
        modrow = sb("modrow", [4, 4, P])
        sel = sb("sel", [4, 2])
        gate = sb("gate", [P, KD, 2])
        small = sb("small", [P, 64])
        E = sb("E", [P, 5248])

        var = E[:, 0:P]
        rstd = E[:, P:2 * P]
        rows_of = E[:, 512:1536].rearrange("p (v t) -> p v t", v=2)
        nmr_all = E[:, 1536:2048]
        tt = [E[:, 2048:2560], E[:, 2560:3072]]
        sq = [E[:, 3072:3584], E[:, 3584:4096]]
        acc1 = E[:, 4096:4608]
        acc2 = E[:, 4608:5120]
        Yf = Y[:].rearrange("p k t -> p (k t)")
        qk = Wk[:, 0:2048].rearrange("p (i t) -> p i t", i=4)
        vtok = Wk[:, 2048:3072].rearrange("p (i c) -> p i c", i=4)
        btab = Wk[:, 3072:5120].rearrange("p (q h r c) -> p q h r c", q=2, h=HEADS, r=ROWS)
        hvc = Wk[:, 5120:8192].rearrange("p (i t) -> p i t", i=6)
        rtab = Wk[:, 6144:8192].rearrange("p (q h r c) -> p q h r c", q=2, h=HEADS, r=ROWS)
        hvpad = Yf[:, 0:3096].rearrange("p (i s t) -> p i s t", i=6, s=2)
        ysp = Yf[:, 0:2048].rearrange("p (r f n) -> p r f n", r=2, f=2)
        uT = Yf[:, 2048:3072].rearrange("p (i n) -> p i n", i=2)
        cpad = E[:, 0:1144].rearrange("p (i s t) -> p i s t", i=2, s=2)
        cacc = E[:, 1144:2168].rearrange("p (i t) -> p i t", i=2)
        scpad = E[:, 2168:3200].rearrange("p (i s t) -> p i s t", i=2, s=2)
        sbb = E[:, 3200:4224].rearrange("p (i t) -> p i t", i=2)
        tmpa = E[:, 4224:5248].rearrange("p (i t) -> p i t", i=2)
        cmean, cvar, crstd, cnmr = (E[:, 2168 + 512 * i:2680 + 512 * i] for i in range(4))
        csq = tmpa
        sbuf_s = [E[:, 512 * i:512 * i + 512] for i in range(2)]
        sbuf_p = [E[:, 1024 + 512 * i:1536 + 512 * i] for i in range(2)]
        sbuf_pT = [E[:, 2048 + 512 * i:2560 + 512 * i].rearrange("p (k q) -> p k q", k=4) for i in range(2)]
        obuf = E[:, 3072:4096].rearrange("p (i t) -> p i t", i=2)
        hprod = [E[:, 4096 + 512 * i:4608 + 512 * i] for i in range(2)]
        xrow = Yf.rearrange("p (t n) -> p t n", t=4)
        vrow = Wk[:, 0:768].rearrange("p (l g c) -> p l g c", l=DEPTH, g=NG)
        crow = Wk[0:16, 768:896]
        decay = Wk[:, 1024:2048].rearrange("p (t r c) -> p t r c", t=2, r=2)
        zT = Wk[0:PE_DIM, 2048:2304]
        fw1 = Wk[0:PE_DIM, 2304:2304 + 2 * FH].rearrange("p (l c) -> p l c", l=2)
        fw2 = Wk[0:FH, 2432:2432 + 2 * FH].rearrange("p (l c) -> p l c", l=2)
        fw3 = Wk[0:FH, 2560:4608].rearrange("p (l c) -> p l c", l=2)
        farg = Wk[0:FH, 4608:4864]
        fk = Wk[0:FH, 4864:5120]
        fh = Wk[0:FH, 5120:5376]
        filt = Wk[:, 5376:6400].rearrange("p (o r c) -> p o r c", o=ORDER, r=2)
        hp = E[:, 0:1024].rearrange("p (t o c) -> p t o c", t=2, o=ORDER)
        hm = E[:, 1024:2048].rearrange("p (t o c) -> p t o c", t=2, o=ORDER)
        hsq = E[:, 2048:4096].rearrange("p (r t n) -> p r t n", r=2, t=2)
        fn = E[:, 4096:4608]
        cs = small[:, 0:16]
        nmax = small[:, 16:18]
        psumr = small[:, 18:20]
        prec = small[:, 20:22]

        ident, invD, invB, ones = (mats[:, i, :] for i in range(4))

        bank = [ctx.enter_context(nc.psum_tensor(f"bank{i}", [P, 512], F32)) for i in range(8)]

        def col(l, name, i=0, rows=slice(0, P)):
            g, r = VROW[name]
            return vec[rows, l, g, r + i:r + i + 1]

        s_c = sem("s_c")
        s_const = sem("s_const")
        s_xin = sem("s_xin")
        w_landed = [sem(f"w_landed{s}") for s in range(2)]
        hi_done = sem("hi_done")
        lo_done = sem("lo_done")
        m_landed = [sem(f"m_landed{s}") for s in range(2)]
        mhi_done = sem("mhi_done")
        mlo_done = sem("mlo_done")
        munit_done = sem("munit_done")
        unit_done = sem("unit_done")
        zero_done = sem("zero_done")
        turned = sem("turned")
        cols_done = sem("cols_done")
        s4hi = sem("s4hi")
        s4lo = sem("s4lo")
        cols_fix = sem("cols_fix")
        x_turned = sem("x_turned")
        x_tile = sem("x_tile")
        sq_tile = sem("sq_tile")
        acc_step = sem("acc_step")
        stat_mm = sem("stat_mm")
        stat_cp = sem("stat_cp")
        stat_v = sem("stat_v")
        rows_zero = sem("rows_zero")
        stat_all = sem("stat_all")
        nmr_cp = sem("nmr_cp")
        stat_sd = sem("stat_sd")
        t_mul = sem("t_mul")
        t_sub = sem("t_sub")
        h_full = sem("h_full")
        h_fullv = sem("h_fullv")
        h_hi = sem("h_hi")
        h_lo = sem("h_lo")
        mrow_done = sem("mrow_done")
        mcol_mm = sem("mcol_mm")
        mod_done = sem("mod_done")
        silu_done = sem("silu_done")
        prod_done = sem("prod_done")
        u_hi = sem("u_hi")
        u_lo = sem("u_lo")
        out_evac = sem("out_evac")
        resid = sem("resid")
        gate_rdy = sem("gate_rdy")
        f_mm = sem("f_mm")
        f_v = sem("f_v")
        f_a = sem("f_a")
        pads = sem("pads")
        s_rtab = sem("s_rtab")
        r_mask = sem("r_mask")
        flipped = sem("flipped")
        btab_cp = sem("btab_cp")
        win_evac = sem("win_evac")
        cglu = sem("cglu")
        ctap = sem("ctap")
        htap = sem("htap")
        stap = sem("stap")
        c_sq = sem("c_sq")
        c_mm = sem("c_mm")
        c_cp = sem("c_cp")
        c_v = sem("c_v")
        c_sd = sem("c_sd")
        c_silu = sem("c_silu")
        b_hi = sem("b_hi")
        b_lo = sem("b_lo")
        at_s = sem("at_s")
        at_v = sem("at_v")
        at_m = sem("at_m")
        at_e = sem("at_e")
        at_r = sem("at_r")
        at_n = sem("at_n")
        at_t = sem("at_t")
        at_tc = sem("at_tc")
        at_o = sem("at_o")
        at_oc = sem("at_oc")
        hy_t = sem("hy_t")
        hy_tc = sem("hy_tc")
        hy_f = sem("hy_f")
        hy_p = sem("hy_p")
        hy_i = sem("hy_i")
        hy_z = sem("hy_z")
        sig_done = sem("sig_done")
        mix_step = sem("mix_step")
        m_hi = sem("m_hi")
        m_lo = sem("m_lo")
        o_turn = sem("o_turn")
        o_copy = sem("o_copy")
        s_out = sem("s_out")

        def streams(l):
            return 2 if l < DEPTH - 1 else 1

        def blocks(l):
            return [(s, h, q) for s in range(streams(l)) for h in range(HEADS) for q in range(2)]

        NB0 = len([1 for s in range(2) for h in range(HEADS) for q in range(2)])

        def lnt(n):
            return TOK if n <= 8 else SEQ

        def ffn_tok(f):
            return TOK if f < 3 else SEQ

        NLN = 6 * DEPTH

        V_TILES = (2, 5)

        def hfull_at(n, k):
            return sum((KD - len(V_TILES)) * (lnt(x) // SEQ) for x in range(0, n, 2)) + \
                sum(lnt(n) // SEQ for x in range(k + 1) if x not in V_TILES)

        KSUM = KD - 2

        def acc_at(i):
            return KD + i * (2 * KD + KSUM)

        FS = 6
        FV = 2 * FS + 12 + 2 + 4
        FM = 2 + 4 + 1 + 4
        NHT = 18
        NST = 2 + 6 + 2
        NCV = 8
        AV0 = 24
        FREE = 2
        FREE_MIX = 4
        FREE_LO = 4

        def mix_at(l, d):
            return FREE_MIX + 56 * l + 7 * d

        block = ctx.enter_context(nc.Block())

        @block.sync
        def _(sp):
            def unit(u, k, it, per, srcs):
                sp.wait_ge(lo_done, FREE_LO + 2 * (u - 1) + it * (2 * per))
                sp.nop(nofuse=True)
                for lo, n, src in srcs:
                    sp.dma_start(raw[u % 2][:, lo:lo + n, :], src).then_inc(w_landed[u % 2], 16)

            def mod_unit(q, it, step, i):
                n = q + i
                if n >= 2:
                    sp.wait_ge(mlo_done, n - 1 + it * step)
                    sp.nop(nofuse=True)
                sp.dma_start(mraw[:, n % 2, :, :], mod_src(q, it, step, i)).then_inc(m_landed[n % 2], 16)

            def rows(w, c0):
                return w.rearrange("(k p) n -> p k n", p=P)[:, :, bass.ds(c0, P)]

            def mod_src(q, it, step, i):
                l = q // MODT
                return rows(a["w_mod"][l], (q % MODT + i) * P + it * step * P)

            def xload():
                for t in range(2):
                    sp.dma_start(xrow[:, t, :], a["x"][0, t * P:(t + 1) * P, :]).then_inc(s_xin, 16)
                    sp.dma_start(xrow[:, 2 + t, :], a["ctx"][0, t * P:(t + 1) * P, :]).then_inc(s_xin, 16)

            for i in range(4):
                mod_unit(0, 0, 0, i)
                if i == 1:
                    xload()
            with sp.Fori(0, MOD_FIRST // 4 - 1) as it:
                for i in range(4):
                    mod_unit(4, it, 4, i)

            def ffn(f):
                l, s = f // 2, f % 2
                if f in (1, 2):
                    sp.wait_ge(unit_done, AT["wout", 0])
                j0 = 0
                for c, n in enumerate(CHUNKS):
                    u0, q0 = AT["in", f, c], MODQ["in", f, c]
                    body = body_in(MOD_IN[f][c])
                    with sp.Fori(0, n // 2) as it:
                        for kind, x, i in body:
                            if kind == "m":
                                mod_unit(q0, it, 4, x)
                            else:
                                src = rows(a["ffn_w_in"][l, s],
                                           (D_FF if kind == "g" else 0) + (j0 + x) * P + it * 2 * P)
                                unit(u0 + i, KD, it, 4, [(0, KD, src)])
                    u0, q0 = AT["out", f, c], MODQ["out", f, c]
                    body = body_out(MOD_OUT[f][c])
                    with sp.Fori(0, 2) as it:
                        for kind, x, i in body:
                            if kind == "m":
                                mod_unit(q0, it, 2, x)
                            else:
                                w = a["ffn_w_out"][l, s, j0 * P:(j0 + n) * P, :]
                                unit(u0 + i, n, it, 4, [(0, n, rows(w, x * P + it * 4 * P))])
                    j0 += n

            def mixer(l):
                def win_units(first, last):
                    for i in range(first, last):
                        unit(AT["win", l] + i, KD, 0, 0, [(0, KD, rows(a["w_in"][l], WIN_ORDER[i] * P))])

                win_units(0, 2)
                sp.wait_ge(unit_done, AT["win", l])
                rpb = a["na_rpb"]
                for r in range(ROWS):
                    for h in range(HEADS):
                        off = ((l * HEADS + h) * RPB_R + WIN_ROWS - 1 - r) * RPB_C + WIN_COLS - 1 - (GRID_W - 1)
                        src = bass.AP(tensor=rpb.tensor, offset=rpb.offset + off,
                                      ap=[[1, GRID_W], [RPB_C, ROWS], [1, GRID_W]])
                        sp.dma_start(rtab[GRID_W * (r % 2):GRID_W * (r % 2 + 1), r // 2, h, :, :],
                                     src).then_inc(s_rtab, 16)
                win_units(2, N_WIN)
                u0 = AT["gate", l]
                with sp.Fori(0, KD // 2) as it:
                    for d in range(2):
                        for i, b in enumerate((0, 1, None, 2, 3)):
                            if b is None:
                                srcs = [(2 * n, BT, rows(a[w][l], d * P + it * 2 * P)) for n, w in
                                        enumerate(("conf_w_proj", "na_w_proj", "sc_w_proj", "hy_w_proj"))]
                            else:
                                srcs = [(0, KD, rows(a["w_in"][l], (M_G + KD * b + d) * P + it * 2 * P))]
                            unit(u0 + 5 * d + i, KD, it, 10, srcs)
                u0 = AT["wout", l]
                with sp.Fori(0, KD // 4) as it:
                    for i in range(4):
                        unit(u0 + i, KD, it, 4, [(0, KD, rows(a["w_out"][l], i * P + it * 4 * P))])

            for l in range(DEPTH):
                ffn(2 * l)
                mixer(l)
                ffn(2 * l + 1)
            for t in range(2):
                sp.wait_ge(o_copy, 2 * (t + 1))
                sp.dma_start(out[0, t * P:(t + 1) * P, :], xrow[:, t, :]).then_inc(s_out, 16)
            sp.wait_ge(s_out, 32)

        @block.gpsimd
        def _(pool):
            pool.memset(Wk[:, 0:1024], 0.0).then_inc(zero_done, 1)
            pool.wait_ge(zero_done, 1)

            def vload(l, name, src):
                g, r = VROW[name]
                n, w = src.shape
                pool.dma_start(vrow[r:r + n, l, g, 0:w], src).then_inc(s_const, 16)

            pool.dma_start(crow[0:8, :], a["c"].rearrange("b (k p) -> (b k) p", p=P)).then_inc(s_c, 16)
            pool.dma_start(crow[8:16, :], a["c_ctx"].rearrange("(k p) -> k p", p=P)).then_inc(s_c, 16)
            pool.dma_start(mats[:], a["k_mats"]).then_inc(s_c, 16)
            pool.dma_start(sel[:], a["k_sel"]).then_inc(s_const, 16)
            pool.dma_start(flip[:], a["k_flip"]).then_inc(s_const, 16)
            pool.dma_start(dft[:], a["k_dft"]).then_inc(s_const, 16)
            pool.dma_start(decay, a["k_decay"]).then_inc(s_const, 16)
            pool.dma_start(zT, a["k_zT"]).then_inc(s_const, 16)
            for l in range(DEPTH):
                vload(l, "b_mod", a["b_mod"][l].rearrange("(k p) -> k p", p=P))
                vload(l, "b_in", a["b_in"][l].rearrange("(k p) -> k p", p=P))
                vload(l, "ln_g", a["post_ln_g"][l].rearrange("i (k p) -> (i k) p", p=P))
                vload(l, "ln_b", a["post_ln_b"][l].rearrange("i (k p) -> (i k) p", p=P))
                vload(l, "conf_w", a["conf_dw_w"][l].rearrange("i (k p) -> (i k) p", p=P))
                vload(l, "sc_w", a["sc_conv_w"][l].rearrange("i (k p) -> (i k) p", p=P))
                vload(l, "conf_b", a["conf_dw_b"][l].rearrange("(k p) -> k p", p=P))
                vload(l, "conf_g", a["conf_ln_g"][l].rearrange("(k p) -> k p", p=P))
                vload(l, "conf_be", a["conf_ln_b"][l].rearrange("(k p) -> k p", p=P))
                vload(l, "hy_bias", a["hy_bias"][l].rearrange("i (k p) -> (i k) p", p=P))
                vload(l, "hs_w", a["hy_sconv_w"][l].rearrange("i (k p) -> (i k) p", p=P))
                vload(l, "hs_b", a["hy_sconv_b"][l].rearrange("(k p) -> k p", p=P))
                vload(l, "b_out", a["b_out"][l].rearrange("(k p) -> k p", p=P))
                vload(l, "hy_b1", a["hy_b1"][l:l + 1])
                vload(l, "hy_b2", a["hy_b2"][l:l + 1])
                vload(l, "hy_f", a["hy_freq"][l])
                pool.dma_start(fw1[:, l, :], a["hy_w1"][l]).then_inc(s_const, 16)
                pool.dma_start(fw2[:, l, :], a["hy_w2"][l]).then_inc(s_const, 16)
                pool.dma_start(fw3[:, l, :], a["hy_w3"][l]).then_inc(s_const, 16)

            n_acc = 0

            def sum_sq(n, with_x):
                nonlocal n_acc
                T = lnt(n)
                for k in range(KD if with_x or n == 0 else KSUM):
                    src = sq[k % 2] if with_x or n == 0 else Y[:, k, :]
                    base = n_acc
                    if with_x:
                        pool.wait_ge(resid, 8 * (n // 2) + k + 1)
                        if k == 0:
                            pool.tensor_copy(acc1[:, 0:T], X[:, k, 0:T]).then_inc(acc_step, 1)
                        else:
                            pool.wait_ge(acc_step, base - 1)
                            pool.tensor_tensor(acc1[:, 0:T], acc1[:, 0:T], X[:, k, 0:T],
                                               ALU.add).then_inc(acc_step, 1)
                        n_acc += 1
                    pool.wait_ge(sq_tile, 8 * n + k + 1)
                    if k == 0:
                        pool.tensor_copy(acc2[:, 0:T], src[:, 0:T]).then_inc(acc_step, 1)
                    else:
                        pool.wait_ge(acc_step, base)
                        pool.tensor_tensor(acc2[:, 0:T], acc2[:, 0:T], src[:, 0:T],
                                           ALU.add).then_inc(acc_step, 1)
                    n_acc += 1

            def masks(l):
                pool.wait_ge(s_rtab, 16 * 16 * (l + 1))
                pool.wait_ge(t_sub, 8 * (6 * l + 2) + KD)
                k = 8 * l
                for q in range(2):
                    for half in range(2):
                        rows = slice(GRID_W * half, GRID_W * half + GRID_W)
                        v = rtab[rows, q, :, :, 0:GRID_W - WIN_COLS].rearrange("p h r c -> p (h r) c")
                        pool.affine_select(out=v, in_=v, compare_op=ALU.is_ge, fill=MASKED,
                                           base=WIN_COLS // 2 - (GRID_W - 1),
                                           pattern=[[0, HEADS * ROWS], [1, GRID_W - WIN_COLS]],
                                           channel_multiplier=1).then_inc(r_mask, 1)
                        pool.wait_ge(r_mask, k + 1)
                        v = rtab[rows, q, :, :, WIN_COLS:GRID_W].rearrange("p h r c -> p (h r) c")
                        pool.affine_select(out=v, in_=v, compare_op=ALU.is_ge, fill=MASKED,
                                           base=GRID_W - 1 + WIN_COLS // 2 - 1 - WIN_COLS,
                                           pattern=[[0, HEADS * ROWS], [-1, GRID_W - WIN_COLS]],
                                           channel_multiplier=-1).then_inc(r_mask, 1)
                        k += 2
                        pool.wait_ge(r_mask, k)

            def apply_mod(n):
                T = lnt(n)
                pool.wait_ge(nmr_cp, n // 2 + 1)
                for k in range(KD):
                    pool.wait_ge(t_mul, 8 * n + k + 1)
                    pool.tensor_tensor(Y[:, k, 0:T], Y[:, k, 0:T], nmr_all[:, 0:T],
                                       ALU.subtract).then_inc(t_sub, 1)

            sum_sq(0, False)
            apply_mod(0)
            for l in range(DEPTH):
                for sub in range(3):
                    n = 6 * l + 2 * sub + 1
                    sum_sq(n, True)
                    if n < NLN - 1:
                        sum_sq(n + 1, False)
                        apply_mod(n + 1)
                    if sub == 0:
                        masks(l)

        @block.scalar
        def _(act):
            def hi(u, it=0, per=0):
                step = landed(u + per) - landed(u) if per else 0
                act.wait_ge(w_landed[u % 2], landed(u) + it * step)
                if u >= 2:
                    act.wait_ge(unit_done, u - 1 + it * per)
                for h in range(2):
                    k = slice(h * KD // 2, (h + 1) * KD // 2)
                    nc.scalar.activation(wh[u % 2][:, k, :], raw[u % 2][:, k, :], ACT.Copy).then_inc(hi_done, 1)

            def nxt(u, it=0, per=0):
                if per or u + 2 < UNITS:
                    hi(u + 2, it, per)

            def mhi(q, it=0, step=0):
                act.wait_ge(m_landed[q % 2], 16 * (q // 2 + 1) + it * (8 * step))
                if q >= 2:
                    act.wait_ge(munit_done, q - 1 + it * step)
                nc.scalar.activation(mwh[q % 2], mraw[:, q % 2, :, :], ACT.Copy).then_inc(mhi_done, 1)

            def rows_out(q, n_prev, it, step, nm):
                act.wait_ge(munit_done, q + 1 + it * step)
                act.wait_ge(mcol_mm, n_prev + it)
                nc.scalar.activation(modrow[:, 0:nm, :],
                                     bank[6][0:4, 0:nm * P].rearrange("p (i c) -> p i c", i=nm),
                                     ACT.Copy).then_inc(mrow_done, 1)

            act.wait_ge(turned, 1)
            nc.scalar.activation(cs, bank[2][:, 0:16], ACT.Silu).then_inc(cols_done, 1)
            act.wait_ge(cols_done, 1)
            for s in range(2):
                nc.scalar.activation(S4[:, :, 2 * s], cs[:, 8 * s:8 * s + 8], ACT.Copy).then_inc(s4hi, 1)
            mhi(0)
            mhi(1)
            act.wait_ge(turned, 3)
            for l in range(DEPTH):
                nc.scalar.activation(vec[:, l, :, :], bank[l][:, 0:NG * P].rearrange("p (g c) -> p g c", g=NG),
                                     ACT.Copy).then_inc(cols_done, 1)

            for i in range(4):
                mhi(i + 2)
            act.wait_ge(munit_done, 4)
            nc.scalar.activation(modrow[:, 0:4, :], bank[6][0:4, :].rearrange("p (i c) -> p i c", i=4),
                                 ACT.Copy).then_inc(mrow_done, 1)
            for k in range(KD):
                act.wait_ge(x_turned, k + 1)
                nc.scalar.activation(X[:, k, :], bank[4 + k % 2][:], ACT.Copy, scale=ALPHA).then_inc(x_tile, 1)
                act.wait_ge(x_tile, k + 1)
                if k >= 2:
                    act.wait_ge(acc_step, k - 1)
                nc.scalar.activation(sq[k % 2][:], X[:, k, :], ACT.Square).then_inc(sq_tile, 1)
            with act.Fori(0, MOD_FIRST // 4 - 1) as it:
                for i in range(4):
                    mhi(6 + i, it, 4)
                rows_out(7, 1, it, 4, 4)
            hi(0)
            hi(1)

            n_x = KD
            n_acc = KD

            def stats(n):
                T = lnt(n)
                rows = slice(0, T // 4)
                act.wait_ge(stat_mm, 2 * n + 1)
                nc.scalar.activation(var[rows], bank[0][rows, 0:P], ACT.Square).then_inc(stat_cp, 1)
                act.wait_ge(stat_v, 5 * n + 2)
                nc.scalar.activation(var[rows], var[rows], ACT.Sqrt).then_inc(stat_sd, 1)
                if n % 2 == 0:
                    act.wait_ge(stat_all, 2 * n + 2)
                    nc.scalar.activation(nmr_all[:, 0:T], bank[3][:, 0:T], ACT.Copy).then_inc(nmr_cp, 1)

            def apply_post(n):
                nonlocal n_x, n_acc
                T, l, i = lnt(n), n // 6, (n % 6) // 2
                for k in range(KD):
                    act.wait_ge(t_sub, 8 * n + k + 1)
                    nc.scalar.activation(X[:, k, 0:T], Y[:, k, 0:T], ACT.Identity,
                                         bias=col(l, "ln_b", 8 * i + k), scale=col(l, "ln_g", 8 * i + k))\
                        .then_inc(x_tile, 1)
                    n_x += 1
                    if n < NLN - 1:
                        act.wait_ge(x_tile, n_x)
                        nc.scalar.activation(Y[:, k, 0:T], X[:, k, 0:T], ACT.Square).then_inc(sq_tile, 1)
                n_acc += 2 * KD + KSUM

            def apply_mod(n):
                T, l, i = lnt(n), n // 6, (n % 6) // 2
                act.wait_ge(mod_done, modbase((0, 1, 1, 2, 3, 3)[n // 2], "in", 0))
                for k in range(KD):
                    if k in V_TILES:
                        act.wait_ge(h_fullv, len(V_TILES) * (n // 2) + V_TILES.index(k) + 1)
                    else:
                        act.wait_ge(t_sub, 8 * n + k + 1)
                        for s in range(T // SEQ):
                            t = slice(s * SEQ, (s + 1) * SEQ)
                            q = l * MODT + 24 * i + k
                            nc.scalar.activation(Y[:, k, t], Y[:, k, t], ACT.Identity,
                                                 bias=modv[:, q, s:s + 1], scale=modv[:, q + 8, s:s + 1])\
                                .then_inc(h_full, 1)
                        act.wait_ge(h_full, hfull_at(n, k))
                    nc.scalar.activation(Hh[:, k, 0:T], Y[:, k, 0:T], ACT.Copy).then_inc(h_hi, 1)

            def mod_step(q, it, step, x, nbody, nm, ahead):
                if ahead:
                    mhi(q + x + 2, it, step)
                if x == nm - 1:
                    rows_out(q + x, nbody, it, step, nm)

            def hidden(f, c, x, u, it):
                T = ffn_tok(f)
                J = f * JF + sum(CHUNKS[:c]) + x
                nc.scalar.activation(tt[x][:, 0:T], bank[2 * x + 1][:, 0:T], ACT.Silu).then_inc(silu_done, 1)
                act.wait_ge(prod_done, FREE + J + 1 + it * 2)
                nc.scalar.activation(Uh[:, bass.ds(it * 2 + x, 1), 0:T].rearrange("p o t -> p (o t)"),
                                     sq[x][:, 0:T], ACT.Copy).then_inc(u_hi, 1)

            def tail(n, m):
                T = lnt(n)
                act.wait_ge(resid, 8 * (n // 2) + m + 1)
                if m >= 2:
                    act.wait_ge(acc_step, n_acc + 2 * (m - 1))
                nc.scalar.activation(sq[m % 2][:, 0:T], X[:, m, 0:T], ACT.Square).then_inc(sq_tile, 1)

            def ffn(f):
                l, s = f // 2, f % 2
                n = 6 * l + (1 if s == 0 else 5)
                for c, nj in enumerate(CHUNKS):
                    u0, q0, nm = AT["in", f, c], MODQ["in", f, c], MOD_IN[f][c]
                    nb_ = modbase(f, "in", c)

                    def in_body(it, ahead):
                        for kind, x, i in body_in(nm):
                            if kind == "m":
                                act.wait_ge(munit_done, q0 + x + 1 + it * 4)
                                mod_step(q0, it, 4, x, nb_, nm, ahead or x < 2)
                                continue
                            act.wait_ge(unit_done, u0 + i + 1 + it * 4)
                            nxt(u0 + i, it, 4)
                            if kind == "g":
                                hidden(f, c, x, u0 + i, it)

                    peel = mod_last(f, "in", c)
                    with act.Fori(0, nj // 2 - peel) as it:
                        in_body(it, True)
                    if peel:
                        in_body(nj // 2 - 1, False)
                    u0, q0, nm = AT["out", f, c], MODQ["out", f, c], MOD_OUT[f][c]
                    nb_ = modbase(f, "out", c)

                    def out_body(it, last):
                        for kind, x, i in body_out(nm):
                            if kind == "m":
                                act.wait_ge(munit_done, q0 + x + 1 + it * 2)
                                mod_step(q0, it, 2, x, nb_, nm, not (last and it == 1))
                                continue
                            act.wait_ge(unit_done, u0 + i + 1 + it * 4)
                            if last:
                                nxt(u0 + 4 * it + i)
                                tail(n, 4 * it + x)
                            else:
                                nxt(u0 + i, it, 4)

                    if c < len(CHUNKS) - 1:
                        with act.Fori(0, 2) as it:
                            out_body(it, False)
                    else:
                        for it in range(2):
                            out_body(it, True)

            def filters():
                act.wait_ge(acc_step, KD)
                for l in range(DEPTH):
                    for i in range(2):
                        act.wait_ge(f_v, FV * l + FS * (i + 1))
                        nc.scalar.activation(fh, farg, ACT.Sin).then_inc(f_a, 1)
                    act.wait_ge(f_v, FV * l + 2 * FS + 12)
                    nc.scalar.activation(hsq[:, 0, :, :], hp.rearrange("p t o c -> p t (o c)"), ACT.Square)\
                        .then_inc(f_a, 1)
                    nc.scalar.activation(hsq[:, 1, :, :], hm.rearrange("p t o c -> p t (o c)"), ACT.Square)\
                        .then_inc(f_a, 1)
                    act.wait_ge(f_v, FV * l + 2 * FS + 13)
                    nc.scalar.activation(fn, fn, ACT.Sqrt).then_inc(f_a, 1)

            def branch_hi(l, b, src, S):
                nc.scalar.activation(Bh[:, b, :, 0:S * SEQ], src[:, :, 0:S * SEQ], ACT.Copy).then_inc(b_hi, 1)

            def mixer(l):
                S = streams(l)
                T = S * SEQ
                u0 = AT["win", l]
                for i, m in enumerate(WIN_ORDER):
                    u = u0 + i
                    act.wait_ge(unit_done, u + 1)
                    nxt(u)
                    b = col(l, "b_in", m)
                    src = bank[i % 4]
                    if i == 0:
                        act.wait_ge(pads, 6 * (l + 1))
                    if m in (0, 1):
                        o, f, v = tmpa[:, m, 0:T], ACT.Identity, src[:, 0:T]
                    elif m in (2, 3):
                        o, f, v = cacc[:, m - 2, 0:T], ACT.Sigmoid, src[:, 0:T]
                    elif m >= 16:
                        o, f, v = hvpad[:, m - 16, 0:S, 1:SEQ + 1], ACT.Identity, \
                            src[:, 0:T].rearrange("p (s t) -> p s t", s=S)
                    elif m < 8:
                        TT = win_tokens(l, m)
                        o, f, v = qk[:, m - 4, 0:TT], ACT.Identity, src[:, 0:TT]
                    elif m < 10:
                        o, f, v, b = vtok[:, :, (m - 8) * P:(m - 7) * P], ACT.Copy, \
                            src[:, :].rearrange("p (t c) -> p t c", t=4), 0.0
                    elif m < 12:
                        o, f, v = sbb[:, m - 10, 0:T], ACT.Identity, src[:, 0:T]
                    elif m < 14:
                        if m == 12:
                            act.wait_ge(cglu, 2 * (l + 1))
                        o, f, v = tmpa[:, m - 12, 0:T], ACT.Identity, src[:, 0:T]
                    else:
                        o, f, v = scpad[:, m - 14, 0:S, 1:SEQ + 1], ACT.Identity, \
                            src[:, 0:T].rearrange("p (s t) -> p s t", s=S)
                    nc.scalar.activation(o, v, f, bias=b).then_inc(win_evac, 1)
                    if i == 4:
                        for q in range(2):
                            for h2 in range(2):
                                act.wait_ge(flipped, 4 * l + 2 * q + h2 + 1)
                                nc.scalar.activation(
                                    btab[:, q, 2 * h2:2 * h2 + 2, :, :].rearrange("p h r c -> p (h r c)"),
                                    bank[4 + 2 * q + h2][:], ACT.Copy).then_inc(btab_cp, 1)
                act.wait_ge(stap, NST * (l + 1))
                branch_hi(l, 2, tmpa, S)
                act.wait_ge(b_lo, 4 * l + 1)
                act.wait_ge(ctap, 2 * CONF_K * (l + 1))
                nc.scalar.activation(csq[:, :, 0:T], cacc[:, :, 0:T], ACT.Square).then_inc(c_sq, 1)
                act.wait_ge(c_mm, 2 * l + 1)
                nc.scalar.activation(cmean[:, 0:T], bank[0][:, 0:T], ACT.Copy).then_inc(c_cp, 1)
                nc.scalar.activation(cvar[:, 0:T], bank[0][:, 0:T], ACT.Square).then_inc(c_cp, 1)
                act.wait_ge(c_v, 8 * l + 2)
                nc.scalar.activation(cvar[:, 0:T], cvar[:, 0:T], ACT.Sqrt).then_inc(c_sd, 1)
                for i in range(BT):
                    act.wait_ge(c_v, 8 * l + 6 + 2 * i)
                    nc.scalar.activation(cacc[:, i, 0:T], cacc[:, i, 0:T], ACT.Silu, bias=col(l, "conf_be", i),
                                         scale=col(l, "conf_g", i)).then_inc(c_silu, 1)
                act.wait_ge(c_silu, 2 * (l + 1))
                branch_hi(l, 0, cacc, S)
                bl = blocks(l)
                nb = len(bl)
                g0 = NB0 * l
                act.wait_ge(b_lo, 4 * l + 2)
                for n in range(nb + 3):
                    if n < nb:
                        K = TOK if bl[n][0] == 0 else SEQ
                        act.wait_ge(at_m, g0 + n + 1)
                        if n >= 2:
                            act.wait_ge(at_t, g0 + n - 1)
                        nc.scalar.activation(sbuf_p[n % 2][:, 0:K], sbuf_s[n % 2][:, 0:K], ACT.Exp,
                                             bias=nmax[:, n % 2:n % 2 + 1],
                                             accum_out=psumr[:, n % 2:n % 2 + 1]).then_inc(at_e, 1)
                    m = n - 2
                    if 0 <= m < nb:
                        kt = 4 if bl[m][0] == 0 else 2
                        act.wait_ge(at_t, g0 + m + 1)
                        if m >= 2:
                            act.wait_ge(at_o, g0 + m - 1)
                        nc.scalar.activation(sbuf_pT[m % 2][:, 0:kt, :],
                                             bank[6][:, 0:kt * P].rearrange("p (k q) -> p k q", k=kt),
                                             ACT.Copy).then_inc(at_tc, 1)
                    m = n - 3
                    if 0 <= m < nb:
                        s, h, q = bl[m]
                        rr = slice(DH * (h % 2), DH * (h % 2) + DH)
                        act.wait_ge(at_o, g0 + m + 1)
                        nc.scalar.activation(obuf[rr, h // 2, s * SEQ + q * P:s * SEQ + (q + 1) * P],
                                             bank[7 - 4 * (m % 2)][rr, 0:P], ACT.Identity,
                                             bias=col(l, "b_in", 8 + h // 2, rr)).then_inc(at_oc, 1)
                act.wait_ge(at_oc, g0 + nb)
                branch_hi(l, 1, obuf, S)
                for o in range(ORDER):
                    for i in range(2):
                        act.wait_ge(hy_t, 2 * (ORDER * l + o) + i + 1)
                        nc.scalar.activation(uT[:, i, 0:S * WB], bank[i][:, 0:S * WB], ACT.Copy)\
                            .then_inc(hy_tc, 1)
                act.wait_ge(hy_z, 4 * ORDER * (l + 1))
                branch_hi(l, 3, hvc[:, 0:BT, :], S)
                u0 = AT["gate", l]
                with act.Fori(0, KD // 2) as it:
                    for d in range(2):
                        for i, b in enumerate((0, 1, None, 2, 3)):
                            u = u0 + 5 * d + i
                            act.wait_ge(unit_done, u + 1 + it * 10)
                            nxt(u, it, 10)
                            if b is None:
                                continue
                            act.wait_ge(mix_step, mix_at(l, d) + (-3, -1, 1, 2)[b] + it * 14)
                            nc.scalar.activation(
                                tt[b % 2][:, 0:T], bank[4 + b][:, 0:T], ACT.Sigmoid,
                                bias=vec[:, l, 0, bass.ds(it * 2 + VROW["b_in"][1] + M_G + KD * b + d, 1)])\
                                .then_inc(sig_done, 1)
                        act.wait_ge(mix_step, mix_at(l, d) + 7 + it * 14)
                        nc.scalar.activation(Uh[:, bass.ds(it * 2 + d, 1), 0:T].rearrange("p o t -> p (o t)"),
                                             acc1[:, 0:T], ACT.Copy).then_inc(m_hi, 1)
                u0 = AT["wout", l]
                for m in range(KD):
                    act.wait_ge(unit_done, u0 + m + 1)
                    nxt(u0 + m)
                    tail(6 * l + 3, m)

            filters()
            stats(0)
            apply_mod(0)
            for l in range(DEPTH):
                for sub in range(3):
                    n = 6 * l + 2 * sub + 1
                    if sub == 1:
                        mixer(l)
                    else:
                        ffn(2 * l + sub // 2)
                    if n in (3, 5):
                        for i in range(2):
                            mhi(MODQ["in", n // 2, 0] + i)
                    stats(n)
                    apply_post(n)
                    if n < NLN - 1:
                        stats(n + 1)
                        apply_mod(n + 1)
            for i in range(4):
                act.wait_ge(o_turn, i + 1)
                nc.scalar.activation(xrow[:, i // 2, (i % 2) * 512:(i % 2 + 1) * 512], bank[4 + i][:],
                                     ACT.Copy).then_inc(o_copy, 1)

        @block.vector
        def _(dve):
            V = nc.vector

            def lo(u, it=0, per=0):
                for h in range(2):
                    k = slice(h * KD // 2, (h + 1) * KD // 2)
                    dve.wait_ge(hi_done, 2 * u + 1 + h + it * (2 * per))
                    V.tensor_tensor(wl[u % 2][:, k, :], raw[u % 2][:, k, :], wh[u % 2][:, k, :].bitcast(F32),
                                    ALU.subtract).then_inc(lo_done, 1)

            def mlo(q, it=0, step=0):
                dve.wait_ge(mhi_done, q + 1 + it * step)
                V.tensor_tensor(mwl[q % 2], mraw[:, q % 2, :, :], mwh[q % 2].bitcast(F32),
                                ALU.subtract).then_inc(mlo_done, 1)

            def nxt(u, it=0, per=0):
                if per or u + 2 < UNITS:
                    lo(u + 2, it, per)

            def mod_cols(q0, it, step, nbody, nm):
                dve.wait_ge(mcol_mm, nbody + 1 + it)
                V.tensor_tensor(modv[:, bass.ds(it * step + q0, nm), :],
                                bank[7][:, 0:2 * nm].rearrange("p (i s) -> p i s", s=2),
                                bmod2[:, bass.ds(it * step + q0, nm), :], ALU.add).then_inc(mod_done, 1)

            V.memset(gate[:], 0.0).then_inc(gate_rdy, 1)
            V.memset(small[:, 32:33], 0.0).then_inc(prod_done, FREE)
            V.memset(small[:, 33:34], 0.0).then_inc(out_evac, FREE)
            V.memset(small[:, 34:35], 0.0).then_inc(mix_step, FREE_MIX)
            V.memset(small[:, 35:36], 0.0).then_inc(sig_done, FREE_MIX)
            V.memset(small[:, 36:37], 0.0).then_inc(lo_done, FREE_LO)
            dve.wait_ge(s4hi, 2)
            for s in range(2):
                V.tensor_tensor(S4[:, :, 2 * s + 1], cs[:, 8 * s:8 * s + 8], S4[:, :, 2 * s].bitcast(F32),
                                ALU.subtract).then_inc(s4lo, 1)
            mlo(0)
            mlo(1)
            dve.wait_ge(cols_done, 3)
            nfix = 0
            for l in range(DEPTH):
                for s in range(2):
                    V.tensor_copy(bmod2[:, l * MODT:(l + 1) * MODT, s], vec[:, l, 0, 0:MODT]).then_inc(cols_fix, 1)
                    nfix += 1
            dve.wait_ge(cols_fix, nfix)
            for l in range(DEPTH):
                v = bmod2[:, l * MODT:(l + 1) * MODT, :].rearrange("p (i k) s -> p i (k s)", i=3)
                V.tensor_scalar(v[:, :, 16:32], v[:, :, 16:32], 1.0, None, ALU.add).then_inc(cols_fix, 1)
                for r in (0, 24):
                    w = vec[:, l, 1, r:r + (24 if l < DEPTH - 1 else 16)]
                    V.tensor_scalar(w, w, ALPHA, None, ALU.mult).then_inc(cols_fix, 1)
                nfix += 3
            for i in range(4):
                mlo(i + 2)
            dve.wait_ge(cols_fix, nfix)
            mod_cols(0, 0, 0, 0, 4)
            with dve.Fori(0, MOD_FIRST // 4 - 1) as it:
                for i in range(4):
                    mlo(6 + i, it, 4)
                mod_cols(4, it, 4, 1, 4)
            lo(0)
            lo(1)

            def filters():
                for l in range(DEPTH):
                    B = FV * l

                    def sine_arg(i):
                        b = col(l, ("hy_b1", "hy_b2")[i], 0, slice(0, FH))
                        fr = col(l, "hy_f", i, slice(0, FH))
                        dve.wait_ge(f_mm, FM * l + i + 1)
                        c = B + FS * i
                        V.tensor_scalar(farg, bank[i][0:FH, 0:SEQ], b, fr, ALU.add, ALU.mult).then_inc(f_v, 1)
                        dve.wait_ge(f_v, c + 1)
                        V.tensor_scalar(fk, farg, 1.0 / TWO_PI, ROUND, ALU.mult, ALU.add).then_inc(f_v, 1)
                        dve.wait_ge(f_v, c + 2)
                        V.tensor_scalar(fk, fk, ROUND, -PI_HI, ALU.subtract, ALU.mult).then_inc(f_v, 1)
                        dve.wait_ge(f_v, c + 3)
                        V.tensor_tensor(farg, farg, fk, ALU.add).then_inc(f_v, 1)
                        dve.wait_ge(f_v, c + 4)
                        V.scalar_tensor_tensor(out=farg, in0=fk, scalar=PI_LO / PI_HI, in1=farg, op0=ALU.mult,
                                               op1=ALU.add).then_inc(f_v, 1)
                        dve.wait_ge(f_v, c + 5)
                        V.tensor_scalar(farg, farg, PI_IN, -PI_IN, ALU.min, ALU.max).then_inc(f_v, 1)

                    sine_arg(0)
                    sine_arg(1)
                    c = B + 2 * FS
                    for t in range(2):
                        for o in range(ORDER):
                            dve.wait_ge(f_mm, FM * l + 2 + 2 * t + o + 1)
                            dve.wait_ge(f_v, c)
                            V.tensor_tensor(filt[:, o, :, :], bank[2 + o][:].rearrange("p (r c) -> p r c", r=2),
                                            decay[:, t, :, :], ALU.mult).then_inc(f_v, 1)
                            c += 1
                            dve.wait_ge(f_v, c)
                            V.tensor_tensor(hp[:, t, o, :], filt[:, o, 0, :], filt[:, o, 1, :],
                                            ALU.add).then_inc(f_v, 1)
                            V.tensor_tensor(hm[:, t, o, :], filt[:, o, 0, :], filt[:, o, 1, :],
                                            ALU.subtract).then_inc(f_v, 1)
                            c += 2
                    dve.wait_ge(f_mm, FM * l + 7)
                    V.tensor_scalar(fn, bank[4][:], 0.5, 1e-6, ALU.mult, ALU.add).then_inc(f_v, 1)
                    dve.wait_ge(f_a, 5 * (l + 1))
                    V.reciprocal(fn, fn).then_inc(f_v, 1)
                    dve.wait_ge(f_v, B + 2 * FS + 14)
                    for r in range(2):
                        for f in range(2):
                            dve.wait_ge(f_mm, FM * l + 8 + 2 * r + f)
                            V.tensor_tensor(spec[:, l, r, f, :, :].rearrange("p o c -> p (o c)"),
                                            bank[2 * r + f][:], fn, ALU.mult).then_inc(f_v, 1)

            def stats(n):
                part = slice(0, lnt(n) // 4)
                eps = LN_EPS if n % 2 else LN_EPS * ALPHA * ALPHA
                if n in (0, 3, 9):
                    if n:
                        dve.wait_ge(resid, 8 * (n // 2) + 1)
                    V.memset(rows_of, 0.0).then_inc(rows_zero, 1)
                    dve.wait_ge(rows_zero, (0, 3, 9).index(n) + 1)
                dve.wait_ge(stat_mm, 2 * n + 2)
                dve.wait_ge(stat_cp, n + 1)
                V.tensor_tensor(var[part], bank[1][part, 0:P], var[part], ALU.subtract).then_inc(stat_v, 1)
                dve.wait_ge(stat_v, 5 * n + 1)
                V.tensor_scalar(var[part], var[part], 0.0, eps, ALU.max, ALU.add).then_inc(stat_v, 1)
                dve.wait_ge(stat_sd, n + 1)
                V.reciprocal(rstd[part], var[part]).then_inc(stat_v, 1)
                dve.wait_ge(stat_v, 5 * n + 3)
                js = [(slice(32 * j, 32 * j + 1), slice(j * P, (j + 1) * P)) for j in range(lnt(n) // P)]
                for p, t in js:
                    i = V.tensor_copy(rows_of[p, 0, t], rstd[p])
                i.then_inc(stat_v, 1)
                for p, t in js:
                    i = V.tensor_tensor(rows_of[p, 1, t], bank[0][p, 0:P], rstd[p], ALU.mult)
                i.then_inc(stat_v, 1)

            def times_rstd(n, k):
                T = lnt(n)
                V.tensor_tensor(Y[:, k, 0:T], X[:, k, 0:T], bank[2][:, 0:T], ALU.mult).then_inc(t_mul, 1)

            def apply_post(n):
                T = lnt(n)
                dve.wait_ge(stat_all, 2 * n + 1)
                times_rstd(n, 0)
                dve.wait_ge(stat_all, 2 * n + 2)
                for k in range(KD):
                    if k + 1 < KD:
                        times_rstd(n, k + 1)
                    dve.wait_ge(t_mul, 8 * n + k + 1)
                    V.tensor_tensor(Y[:, k, 0:T], Y[:, k, 0:T], bank[3][:, 0:T],
                                    ALU.subtract).then_inc(t_sub, 1)

            def apply_mod(n):
                T, l, i = lnt(n), n // 6, (n % 6) // 2

                def low(k):
                    dve.wait_ge(h_hi, 4 * n + k + 1)
                    V.tensor_tensor(Hl[:, k, 0:T], Y[:, k, 0:T], Hh[:, k, 0:T].bitcast(F32),
                                    ALU.subtract).then_inc(h_lo, 1)

                dve.wait_ge(stat_all, 2 * n + 1)
                dve.wait_ge(mod_done, modbase((0, 1, 1, 2, 3, 3)[n // 2], "in", 0))
                for k in range(KD):
                    times_rstd(n, k)
                    if k >= 3:
                        low(k - 3)
                    if k - 1 in V_TILES:
                        dve.wait_ge(t_sub, 8 * n + k)
                        for s in range(T // SEQ):
                            t = slice(s * SEQ, (s + 1) * SEQ)
                            q = l * MODT + 24 * i + k - 1
                            h = V.tensor_scalar(Y[:, k - 1, t], Y[:, k - 1, t], modv[:, q + 8, s:s + 1],
                                                modv[:, q, s:s + 1], ALU.mult, ALU.add)
                        h.then_inc(h_fullv, 1)
                for k in range(KD - 3, KD):
                    low(k)

            def hidden(f, c, x, it):
                T = ffn_tok(f)
                J = f * JF + sum(CHUNKS[:c]) + x
                dve.wait_ge(silu_done, J + 1 + it * 2)
                V.tensor_tensor(sq[x][:, 0:T], tt[x][:, 0:T], bank[2 * x][:, 0:T],
                                ALU.mult).then_inc(prod_done, 1)
                dve.wait_ge(u_hi, J + 1 + it * 2)
                V.tensor_tensor(Ul[:, bass.ds(it * 2 + x, 1), 0:T].rearrange("p o t -> p (o t)"),
                                sq[x][:, 0:T],
                                Uh[:, bass.ds(it * 2 + x, 1), 0:T].rearrange("p o t -> p (o t)").bitcast(F32),
                                ALU.subtract).then_inc(u_lo, 1)

            def partial(f, c, x, u, it):
                T = ffn_tok(f)
                dve.wait_ge(unit_done, u + 1 + it * 4)
                y = Y[:, bass.ds(it * 4 + x, 1), 0:T].rearrange("p o t -> p (o t)")
                if c == 0:
                    V.tensor_copy(y, bank[4 + x % 2][:, 0:T]).then_inc(out_evac, 1)
                else:
                    V.tensor_tensor(y, bank[4 + x % 2][:, 0:T], y, ALU.add).then_inc(out_evac, 1)

            def n_evac(n):
                l, sub = n // 6, (n % 6) // 2
                return 56 * l + (16, 24, 48)[sub]

            def tail(n, m, u, y):
                T = lnt(n)
                l = n // 6
                dve.wait_ge(unit_done, u + 1)
                if y is None:
                    V.tensor_scalar(tt[m % 2][:, 0:T], bank[4 + m % 2][:, 0:T], col(l, "b_out", m), None,
                                    ALU.add).then_inc(out_evac, 1)
                else:
                    V.tensor_tensor(tt[m % 2][:, 0:T], bank[4 + m % 2][:, 0:T], y, ALU.add).then_inc(out_evac, 1)
                dve.wait_ge(out_evac, FREE + n_evac(n) + m + 1)
                for s in range(T // SEQ):
                    t = slice(s * SEQ, (s + 1) * SEQ)
                    i = V.scalar_tensor_tensor(out=X[:, m, t], in0=tt[m % 2][:, t], scalar=gate[:, m, s:s + 1],
                                               in1=X[:, m, t], op0=ALU.mult, op1=ALU.add)
                i.then_inc(resid, 1)

            def set_gate(n, mod_bodies):
                l, sub = n // 6, (n % 6) // 2
                q = l * MODT + 24 * sub + 16
                dve.wait_ge(mod_done, mod_bodies)
                if n > 1:
                    dve.wait_ge(resid, 8 * (n // 2))
                V.tensor_scalar(gate[:], modv[:, q:q + 8, :], 1.0 if sub == 1 else 0.5, None,
                                ALU.mult).then_inc(gate_rdy, 1)
                dve.wait_ge(gate_rdy, n // 2 + 2)

            def ffn(f):
                l, s = f // 2, f % 2
                n = 6 * l + (1 if s == 0 else 5)
                for c, nj in enumerate(CHUNKS):
                    u0, q0, nm = AT["in", f, c], MODQ["in", f, c], MOD_IN[f][c]
                    nb_ = modbase(f, "in", c)

                    def in_body(it, ahead):
                        for kind, x, i in body_in(nm):
                            if kind == "m":
                                if ahead or x < 2:
                                    mlo(q0 + x + 2, it, 4)
                                continue
                            nxt(u0 + i, it, 4)
                            if kind == "g":
                                hidden(f, c, x, it)
                        if nm:
                            mod_cols(q0, it, 4, nb_, nm)

                    peel = mod_last(f, "in", c)
                    with dve.Fori(0, nj // 2 - peel) as it:
                        in_body(it, True)
                    if peel:
                        in_body(nj // 2 - 1, False)
                    u0, q0, nm = AT["out", f, c], MODQ["out", f, c], MOD_OUT[f][c]
                    nb_ = modbase(f, "out", c)

                    def out_body(it, last):
                        for kind, x, i in body_out(nm):
                            if kind == "m":
                                if not (last and it == 1):
                                    mlo(q0 + x + 2, it, 2)
                                continue
                            if last:
                                m = 4 * it + x
                                nxt(u0 + m)
                                tail(n, m, u0 + m, Y[:, m, 0:ffn_tok(f)])
                            else:
                                nxt(u0 + i, it, 4)
                                partial(f, c, x, u0 + i, it)
                        if nm:
                            mod_cols(q0, it, 2, nb_, nm)

                    if c < len(CHUNKS) - 1:
                        with dve.Fori(0, 2) as it:
                            out_body(it, False)
                    else:
                        set_gate(n, nb_)
                        for it in range(2):
                            out_body(it, True)

            def mixer(l):
                S = streams(l)
                T = S * SEQ
                n = 6 * l + 3
                ct, ht, st = 2 * CONF_K * l, 24 * l * 0 + NHT * l, NST * l
                nw = N_WIN * l
                dve.wait_ge(h_lo, 24 * l + 16)
                for v, w, L in ((cpad, PADC, 2 * PADC + SEQ), (scpad, 1, SEQ + 2), (hvpad, 1, SEQ + 2)):
                    V.memset(v[:, :, :, 0:w], 0.0).then_inc(pads, 1)
                    V.memset(v[:, :, :, L - w:L], 0.0).then_inc(pads, 1)
                dve.wait_ge(pads, 6 * (l + 1))

                def conf_tap(j):
                    nonlocal ct
                    for i in range(BT):
                        src = cpad[:, i, 0:S, j:j + SEQ]
                        dst = cacc[:, i, 0:T].rearrange("p (s t) -> p s t", s=S)
                        w = col(l, "conf_w", BT * j + i)
                        if j == 0:
                            dve.wait_ge(cglu, 2 * (l + 1))
                            V.tensor_scalar(dst, src, w, col(l, "conf_b", i), ALU.mult, ALU.add).then_inc(ctap, 1)
                        else:
                            dve.wait_ge(ctap, ct - 1)
                            V.scalar_tensor_tensor(out=dst, in0=src, scalar=w, in1=dst, op0=ALU.mult,
                                                   op1=ALU.add).then_inc(ctap, 1)
                        ct += 1

                def hy_short(i):
                    nonlocal ht
                    dst = hvc[:, i, 0:T].rearrange("p (s t) -> p s t", s=S)
                    dve.wait_ge(win_evac, nw + 5 + i)
                    for j in range(3):
                        src = hvpad[:, i, 0:S, j:j + SEQ]
                        w = col(l, "hs_w", 6 * j + i)
                        if j == 0:
                            V.tensor_scalar(dst, src, w, col(l, "hs_b", i), ALU.mult, ALU.add).then_inc(htap, 1)
                        else:
                            dve.wait_ge(htap, ht)
                            V.scalar_tensor_tensor(out=dst, in0=src, scalar=w, in1=dst, op0=ALU.mult,
                                                   op1=ALU.add).then_inc(htap, 1)
                        ht += 1

                u0 = AT["win", l]
                tap = 0
                for i, m in enumerate(WIN_ORDER):
                    nxt(u0 + i)
                    if m in (2, 3):
                        dve.wait_ge(win_evac, nw + i + 1)
                        V.tensor_tensor(cpad[:, m - 2, 0:S, PADC:PADC + SEQ],
                                        tmpa[:, m - 2, 0:T].rearrange("p (s t) -> p s t", s=S),
                                        cacc[:, m - 2, 0:T].rearrange("p (s t) -> p s t", s=S),
                                        ALU.mult).then_inc(cglu, 1)
                    for _ in range(2):
                        if i >= 4 and tap < CONF_K:
                            conf_tap(tap)
                            tap += 1
                    if i == 5:
                        dve.wait_ge(btab_cp, 4 * (l + 1))
                    if 5 <= i < 11:
                        hy_short(i - 5)
                    if m >= 14 and m < 16:
                        j = m - 14
                        dve.wait_ge(win_evac, nw + i + 1)
                        v = scpad[:, j, 0:S, 1:SEQ + 1]
                        V.tensor_tensor(v, v, tmpa[:, j, 0:T].rearrange("p (s t) -> p s t", s=S),
                                        ALU.mult).then_inc(stap, 1)
                        st += 1
                while tap < CONF_K:
                    conf_tap(tap)
                    tap += 1
                for j in range(3):
                    for i in range(BT):
                        dst = tmpa[:, i, 0:T].rearrange("p (s t) -> p s t", s=S)
                        src = scpad[:, i, 0:S, j:j + SEQ]
                        w = col(l, "sc_w", BT * j + i)
                        dve.wait_ge(stap, st - 1)
                        if j == 0:
                            V.tensor_scalar(dst, src, w, None, ALU.mult).then_inc(stap, 1)
                        else:
                            V.scalar_tensor_tensor(out=dst, in0=src, scalar=w, in1=dst, op0=ALU.mult,
                                                   op1=ALU.add).then_inc(stap, 1)
                        st += 1
                for i in range(BT):
                    dve.wait_ge(stap, st - 1)
                    V.tensor_tensor(tmpa[:, i, 0:T], tmpa[:, i, 0:T], sbb[:, i, 0:T], ALU.mult).then_inc(stap, 1)
                    st += 1

                def branch_lo(b, src, k):
                    dve.wait_ge(b_hi, 4 * l + k)
                    V.tensor_tensor(Bl[:, b, :, 0:T], src[:, :, 0:T], Bh[:, b, :, 0:T].bitcast(F32),
                                    ALU.subtract).then_inc(b_lo, 1)

                branch_lo(2, tmpa, 1)
                c0 = NCV * l
                dve.wait_ge(c_mm, 2 * l + 2)
                dve.wait_ge(c_cp, 2 * l + 2)
                V.tensor_tensor(cvar[:, 0:T], bank[1][:, 0:T], cvar[:, 0:T], ALU.subtract).then_inc(c_v, 1)
                dve.wait_ge(c_v, c0 + 1)
                V.tensor_scalar(cvar[:, 0:T], cvar[:, 0:T], 0.0, LN_EPS, ALU.max, ALU.add).then_inc(c_v, 1)
                dve.wait_ge(c_sd, l + 1)
                V.reciprocal(crstd[:, 0:T], cvar[:, 0:T]).then_inc(c_v, 1)
                dve.wait_ge(c_v, c0 + 3)
                V.tensor_tensor(cnmr[:, 0:T], cmean[:, 0:T], crstd[:, 0:T], ALU.mult).then_inc(c_v, 1)
                dve.wait_ge(c_v, c0 + 4)
                for i in range(BT):
                    V.tensor_tensor(cacc[:, i, 0:T], cacc[:, i, 0:T], crstd[:, 0:T], ALU.mult).then_inc(c_v, 1)
                    dve.wait_ge(c_v, c0 + 5 + 2 * i)
                    V.tensor_tensor(cacc[:, i, 0:T], cacc[:, i, 0:T], cnmr[:, 0:T],
                                    ALU.subtract).then_inc(c_v, 1)
                branch_lo(0, cacc, 2)
                bl = blocks(l)
                nb = len(bl)
                g0 = NB0 * l
                gv = AV0 * l
                for n_ in range(nb + 1):
                    if n_ < nb:
                        s, h, q = bl[n_]
                        r = n_ % 2
                        dve.wait_ge(at_s, g0 + n_ + 1)
                        if s == 0:
                            V.scalar_tensor_tensor(out=sbuf_s[r][:, 0:SEQ], in0=bank[4 + r][:, 0:SEQ], scalar=SCALE,
                                                   in1=btab[:, q, h, :, :].rearrange("p r c -> p (r c)"),
                                                   op0=ALU.mult, op1=ALU.add).then_inc(at_v, 1)
                            V.tensor_scalar(sbuf_s[r][:, SEQ:TOK], bank[4 + r][:, SEQ:TOK], SCALE, None,
                                            ALU.mult).then_inc(at_v, 1)
                            gv += 2
                            K = TOK
                        else:
                            V.tensor_scalar(sbuf_s[r][:, 0:SEQ], bank[4 + r][:, 0:SEQ], SCALE, None,
                                            ALU.mult).then_inc(at_v, 1)
                            gv += 1
                            K = SEQ
                        dve.wait_ge(at_v, gv)
                        V.tensor_reduce(out=nmax[:, r:r + 1], in_=sbuf_s[r][:, 0:K], axis=AX.X, op=ALU.max,
                                        negate=True).then_inc(at_m, 1)
                    m = n_ - 1
                    if 0 <= m:
                        r = m % 2
                        K = TOK if bl[m][0] == 0 else SEQ
                        dve.wait_ge(at_e, g0 + m + 1)
                        V.reciprocal(prec[:, r:r + 1], psumr[:, r:r + 1]).then_inc(at_r, 1)
                        dve.wait_ge(at_r, g0 + m + 1)
                        V.tensor_scalar(sbuf_p[r][:, 0:K], sbuf_p[r][:, 0:K], prec[:, r:r + 1], None,
                                        ALU.mult).then_inc(at_n, 1)
                branch_lo(1, obuf, 3)
                pc = 12 * ORDER * l
                zc = 4 * ORDER * l
                dve.wait_ge(htap, NHT * (l + 1))
                for o in range(ORDER):
                    N = S * WB
                    for f in range(2):
                        kr = spec[:, l, 0, f, o, :].unsqueeze(1).to_broadcast([P, S, WB])
                        ks = spec[:, l, 1, f, o, :].unsqueeze(1).to_broadcast([P, S, WB])

                        def v3(x):
                            return x[:, 0:N].rearrange("p (s c) -> p s c", s=S)

                        dve.wait_ge(hy_f, 4 * (ORDER * l + o) + 2 * f + 2)
                        for out_, x0, k0, x1, k1, op in ((0, f, kr, 2 + f, ks, ALU.subtract),
                                                         (1, f, ks, 2 + f, kr, ALU.add)):
                            if pc:
                                dve.wait_ge(hy_p, pc)
                            V.tensor_tensor(v3(hprod[0]), v3(bank[x0][:, :]), k0, ALU.mult).then_inc(hy_p, 1)
                            V.tensor_tensor(v3(hprod[1]), v3(bank[x1][:, :]), k1, ALU.mult).then_inc(hy_p, 1)
                            pc += 2
                            dve.wait_ge(hy_p, pc)
                            V.tensor_tensor(ysp[:, out_, f, 0:N], hprod[0][:, 0:N], hprod[1][:, 0:N],
                                            op).then_inc(hy_p, 1)
                            pc += 1
                    for i in range(BT):
                        dve.wait_ge(hy_i, 2 * (ORDER * l + o) + i + 1)
                        V.scalar_tensor_tensor(out=hvc[:, i, 0:T], in0=hvc[:, i, 0:T],
                                               scalar=col(l, "hy_bias", BT * o + i), in1=bank[i][:, 0:T],
                                               op0=ALU.mult, op1=ALU.add).then_inc(hy_z, 1)
                        zc += 1
                        dve.wait_ge(hy_z, zc)
                        V.tensor_tensor(hvc[:, i, 0:T], hvc[:, i, 0:T], hvc[:, BT * (1 + o) + i, 0:T],
                                        ALU.mult).then_inc(hy_z, 1)
                        zc += 1
                branch_lo(3, hvc[:, 0:2, :], 4)
                u0 = AT["gate", l]
                with dve.Fori(0, KD // 2) as it:
                    for d in range(2):
                        base = mix_at(l, d)
                        for i, b in enumerate((0, 1, None, 2, 3)):
                            u = u0 + 5 * d + i
                            nxt(u, it, 10)
                            for b in {2: (0, 1), 3: (2,), 4: (3,)}.get(i, ()):
                                dve.wait_ge(sig_done, FREE_MIX + 32 * l + 4 * d + b + 1 + it * 8)
                                if b == 0:
                                    dve.wait_ge(unit_done, u0 + 5 * d + 3 + it * 10)
                                    V.tensor_tensor(acc1[:, 0:T], tt[0][:, 0:T], bank[0][:, 0:T],
                                                    ALU.mult).then_inc(mix_step, 1)
                                    continue
                                dve.wait_ge(mix_step, base + 2 * b - 1 + it * 14)
                                V.tensor_tensor(acc2[:, 0:T], tt[b % 2][:, 0:T], bank[b][:, 0:T],
                                                ALU.mult).then_inc(mix_step, 1)
                                dve.wait_ge(mix_step, base + 2 * b + it * 14)
                                V.tensor_tensor(acc1[:, 0:T], acc1[:, 0:T], acc2[:, 0:T],
                                                ALU.add).then_inc(mix_step, 1)
                        dve.wait_ge(m_hi, 8 * l + d + 1 + it * 2)
                        V.tensor_tensor(Ul[:, bass.ds(it * 2 + d, 1), 0:T].rearrange("p o t -> p (o t)"),
                                        acc1[:, 0:T],
                                        Uh[:, bass.ds(it * 2 + d, 1), 0:T].rearrange("p o t -> p (o t)").bitcast(F32),
                                        ALU.subtract).then_inc(m_lo, 1)
                set_gate(n, modbase(2 * l + 1, "in", 0))
                u0 = AT["wout", l]
                for m in range(KD):
                    nxt(u0 + m)
                    tail(n, m, u0 + m, None)

            filters()
            stats(0)
            apply_mod(0)
            for l in range(DEPTH):
                for sub in range(3):
                    n = 6 * l + 2 * sub + 1
                    if sub == 1:
                        mixer(l)
                    else:
                        ffn(2 * l + sub // 2)
                    if n in (3, 5):
                        for i in range(2):
                            mlo(MODQ["in", n // 2, 0] + i)
                    stats(n)
                    apply_post(n)
                    if n < NLN - 1:
                        stats(n + 1)
                        apply_mod(n + 1)

        @block.tensor
        def _(pe):
            T_ = nc.tensor

            def split3(o, k, s, xh, xl, first, last):
                T_.matmul(o, wh[s][:, k, :], xh, start=first, stop=False)
                T_.matmul(o, wh[s][:, k, :], xl, start=False, stop=False)
                return T_.matmul(o, wl[s][:, k, :], xh, start=False, stop=last)

            def split_in(u, k, it=0, per=0):
                if k in (0, KD // 2):
                    pe.wait_ge(lo_done, FREE_LO + 2 * u + 1 + k // (KD // 2) + it * (2 * per))

            def mod_unit(q, x, it=0, step=0):
                pe.wait_ge(mlo_done, q + 1 + it * step)
                o = bank[6][0:4, x * P:(x + 1) * P]
                for k in range(KD):
                    T_.matmul(o, S4[:, k, :], mwh[q % 2][:, k, :], start=(k == 0), stop=False)
                    i = T_.matmul(o, S4[:, k, :], mwl[q % 2][:, k, :], start=False, stop=(k == KD - 1))
                i.then_inc(munit_done, 1)

            def mod_turn(nbody, nm, it=0):
                pe.wait_ge(mrow_done, nbody + 1 + it)
                if nbody:
                    pe.wait_ge(mod_done, nbody + it)
                for x in range(nm):
                    i = T_.matmul(bank[7][:, 2 * x:2 * x + 2], modrow[:, x, :], sel[:], start=True, stop=True)
                i.then_inc(mcol_mm, 1)

            pe.wait_ge(s_c, 48)
            T_.transpose(bank[2][:, 0:16], crow, ident[0:16, 0:16]).then_inc(turned, 1)
            pe.wait_ge(s_const, 16 * (5 + DEPTH * 19))
            for l in range(DEPTH):
                for g in range(NG):
                    i = T_.transpose(bank[l][:, g * P:(g + 1) * P], vrow[:, l, g, :], ident)
                i.then_inc(turned, 1)
            pe.wait_ge(s4hi, 2)
            pe.wait_ge(s4lo, 2)
            for x in range(4):
                mod_unit(x, x)
            pe.wait_ge(s_xin, 64)
            for k in range(KD):
                if k >= 2:
                    pe.wait_ge(x_tile, k - 1)
                for t in range(4):
                    i = T_.transpose(bank[4 + k % 2][:, t * P:(t + 1) * P], xrow[:, t, k * P:(k + 1) * P], ident)
                i.then_inc(x_turned, 1)
            mod_turn(0, 4)
            with pe.Fori(0, MOD_FIRST // 4 - 1) as it:
                for x in range(4):
                    mod_unit(4 + x, x, it, 4)
                mod_turn(1, 4, it)

            def filters():
                for l in range(DEPTH):
                    pe.wait_ge(cols_fix, 10)
                    if l:
                        pe.wait_ge(f_v, FV * l)
                    T_.matmul(bank[0][0:FH, 0:SEQ], fw1[:, l, :], zT, start=True, stop=True).then_inc(f_mm, 1)
                    pe.wait_ge(f_a, 5 * l + 1)
                    T_.matmul(bank[1][0:FH, 0:SEQ], fw2[:, l, :], fh, start=True, stop=True).then_inc(f_mm, 1)
                    pe.wait_ge(f_a, 5 * l + 2)
                    for t in range(2):
                        for o in range(ORDER):
                            if t:
                                pe.wait_ge(f_v, FV * l + 2 * FS + 3 * o + 1)
                            T_.matmul(bank[2 + o][:], fh[:, t * P:(t + 1) * P], fw3[:, l, o * 512:(o + 1) * 512],
                                      start=True, stop=True).then_inc(f_mm, 1)
                    pe.wait_ge(f_a, 5 * l + 4)
                    for i in range(4):
                        m = T_.matmul(bank[4][:], ones, hsq[:, i // 2, i % 2, :], start=(i == 0), stop=(i == 3))
                    m.then_inc(f_mm, 1)
                    for r, h in ((0, hp), (1, hm)):
                        for f in range(2):
                            for t in range(2):
                                m = T_.matmul(bank[2 * r + f][:], dft[:, r, t, f * P:(f + 1) * P],
                                              h[:, t, :, :].rearrange("p o c -> p (o c)"),
                                              start=(t == 0), stop=(t == 1))
                            m.then_inc(f_mm, 1)

            def mean_of(b, x, T, first, last):
                for j in range(T // P):
                    m = T_.matmul(bank[b][32 * j:32 * j + 32, 0:P], invD[:, 0:32], x[:, j * P:(j + 1) * P],
                                  start=first, stop=last)
                return m

            def to_all(n):
                T = lnt(n)
                for i in range(2):
                    pe.wait_ge(stat_v, 5 * n + 4 + i)
                    T_.matmul(bank[2 + i][:, 0:T], ones, rows_of[:, i, 0:T], start=True, stop=True)\
                        .then_inc(stat_all, 1)

            def stats_direct(n):
                T = lnt(n)
                if n == 0:
                    pe.wait_ge(f_v, FV * DEPTH)
                for k in range(KD):
                    pe.wait_ge(x_tile, 8 * (n // 2) + k + 1)
                    m = mean_of(0, X[:, k, :], T, k == 0, k == KD - 1)
                m.then_inc(stat_mm, 1)
                if n:
                    for k in range(KSUM, KD):
                        pe.wait_ge(sq_tile, 8 * n + k + 1)
                        mean_of(1, Y[:, k, :], T, k == KSUM, False)
                pe.wait_ge(acc_step, acc_at(n // 2))
                mean_of(1, acc2, T, n == 0, True).then_inc(stat_mm, 1)
                to_all(n)

            def stats_sums(n):
                T = lnt(n)
                pe.wait_ge(acc_step, acc_at(n // 2) + 2 * KD - 1)
                mean_of(0, acc1, T, True, True).then_inc(stat_mm, 1)
                pe.wait_ge(acc_step, acc_at(n // 2) + 2 * KD)
                mean_of(1, acc2, T, True, True).then_inc(stat_mm, 1)
                to_all(n)

            def ffn(f):
                T = ffn_tok(f)
                l, s = f // 2, f % 2
                n = 6 * l + (0 if s == 0 else 4)
                for c, nj in enumerate(CHUNKS):
                    J0 = f * JF + sum(CHUNKS[:c])
                    u0, q0, nm = AT["in", f, c], MODQ["in", f, c], MOD_IN[f][c]
                    body = body_in(nm)
                    nb_ = modbase(f, "in", c)
                    with pe.Fori(0, nj // 2) as it:
                        first_main = True
                        for kind, x, i in body:
                            u = u0 + i
                            if kind == "m":
                                mod_unit(q0 + x, x, it, 4)
                                continue
                            if kind == "a":
                                pe.wait_ge(prod_done, FREE + J0 + x - 1 + it * 2)
                            o = bank[2 * x + (kind == "g")][:, 0:T]
                            for k in range(KD):
                                split_in(u, k, it, 4)
                                if c == 0 and first_main:
                                    pe.wait_ge(h_lo, 4 * n + k + 1)
                                m = split3(o, k, u % 2, Hh[:, k, 0:T], Hl[:, k, 0:T], k == 0, k == KD - 1)
                            first_main = False
                            m.then_inc(unit_done, 1)
                        if nm:
                            mod_turn(nb_, nm, it)
                    u0, q0, nm = AT["out", f, c], MODQ["out", f, c], MOD_OUT[f][c]
                    body = body_out(nm)
                    nb_ = modbase(f, "out", c)
                    ev = n_evac_pe(f, c)

                    with pe.Fori(0, 2) as it:
                        for kind, x, i in body:
                            u = u0 + i
                            if kind == "m":
                                mod_unit(q0 + x, x, it, 2)
                                continue
                            pe.wait_ge(out_evac, FREE + ev + x - 1 + it * 4)
                            for k in range(nj):
                                split_in(u, k, it, 4)
                                if x == 0:
                                    pe.wait_ge(u_lo, J0 + k + 1)
                                m = split3(bank[4 + x % 2][:, 0:T], k, u % 2, Uh[:, k, 0:T], Ul[:, k, 0:T],
                                           k == 0, k == nj - 1)
                            m.then_inc(unit_done, 1)
                        if nm:
                            mod_turn(nb_, nm, it)

            def n_evac_pe(f, c):
                return 56 * (f // 2) + (32 if f % 2 else 0) + 8 * c

            def mixer(l):
                S = streams(l)
                T = S * SEQ
                n = 6 * l + 2
                u0 = AT["win", l]
                nw = N_WIN * l
                for i, m in enumerate(WIN_ORDER):
                    u = u0 + i
                    if i >= 4:
                        pe.wait_ge(win_evac, nw + i - 3)
                    TT = win_tokens(l, m)
                    if 8 <= m < 10:
                        split_in(u, KD // 2)
                        for t in range(4):
                            o = bank[i % 4][:, t * P:(t + 1) * P]
                            tk = slice(t * P, (t + 1) * P)
                            for k in range(KD):
                                T_.matmul(o, Hh[:, k, tk], wh[u % 2][:, k, :], start=(k == 0), stop=False)
                                T_.matmul(o, Hh[:, k, tk], wl[u % 2][:, k, :], start=False, stop=False)
                                mm = T_.matmul(o, Hl[:, k, tk], wh[u % 2][:, k, :], start=False, stop=(k == KD - 1))
                    else:
                        for k in range(KD):
                            split_in(u, k)
                            if i == 0:
                                pe.wait_ge(h_lo, 4 * n + k + 1)
                            mm = split3(bank[i % 4][:, 0:TT], k, u % 2, Hh[:, k, 0:TT], Hl[:, k, 0:TT], k == 0,
                                        k == KD - 1)
                    mm.then_inc(unit_done, 1)
                    if i == 2:
                        pe.wait_ge(r_mask, 8 * (l + 1))
                        for q in range(2):
                            for h2 in range(2):
                                T_.matmul(bank[4 + 2 * q + h2][:], flip[:],
                                          rtab[:, q, 2 * h2:2 * h2 + 2, :, :].rearrange("p h r c -> p (h r c)"),
                                          start=True, stop=True).then_inc(flipped, 1)
                pe.wait_ge(ctap, 2 * CONF_K * (l + 1))
                pe.wait_ge(win_evac, N_WIN * (l + 1))
                for i in range(BT):
                    mm = T_.matmul(bank[0][:, 0:T], invB, cacc[:, i, 0:T], start=(i == 0), stop=(i == BT - 1))
                mm.then_inc(c_mm, 1)
                pe.wait_ge(c_sq, l + 1)
                for i in range(BT):
                    mm = T_.matmul(bank[1][:, 0:T], invB, csq[:, i, 0:T], start=(i == 0), stop=(i == BT - 1))
                mm.then_inc(c_mm, 1)
                bl = blocks(l)
                nb = len(bl)
                g0 = NB0 * l
                nv = 0
                gv = [AV0 * l]
                for s, h, q in bl:
                    gv.append(gv[-1] + (2 if s == 0 else 1))
                pe.wait_ge(btab_cp, 4 * (l + 1))
                for n_ in range(nb + 3):
                    if n_ < nb:
                        s, h, q = bl[n_]
                        rr = slice(DH * (h % 2), DH * (h % 2) + DH)
                        qs = qk[rr, h // 2, s * SEQ + q * P:s * SEQ + (q + 1) * P]
                        if s == 0:
                            ks, K = qk[rr, 2 + h // 2, 0:TOK], TOK
                        else:
                            ks, K = qk[rr, 2 + h // 2, SEQ:TOK], SEQ
                        if n_ >= 2:
                            pe.wait_ge(at_v, gv[n_ - 1])
                        T_.matmul(bank[4 + n_ % 2][:, 0:K], qs, ks, start=True, stop=True).then_inc(at_s, 1)
                    m = n_ - 2
                    if 0 <= m < nb:
                        kt = 4 if bl[m][0] == 0 else 2
                        pe.wait_ge(at_n, g0 + m + 1)
                        if m:
                            pe.wait_ge(at_tc, g0 + m)
                        for k in range(kt):
                            mm = T_.transpose(bank[6][:, k * P:(k + 1) * P], sbuf_p[m % 2][:, k * P:(k + 1) * P], ident)
                        mm.then_inc(at_t, 1)
                    m = n_ - 3
                    if 0 <= m < nb:
                        s, h, q = bl[m]
                        kt = 4 if s == 0 else 2
                        rr = slice(DH * (h % 2), DH * (h % 2) + DH)
                        pe.wait_ge(at_tc, g0 + m + 1)
                        if m >= 2:
                            pe.wait_ge(at_oc, g0 + m - 1)
                        for k in range(kt):
                            mm = T_.matmul(bank[7 - 4 * (m % 2)][rr, 0:P],
                                           vtok[:, 2 * s + k, h * DH:(h + 1) * DH], sbuf_pT[m % 2][:, k, :],
                                           start=(k == 0), stop=(k == kt - 1))
                        mm.then_inc(at_o, 1)
                N = S * WB
                pe.wait_ge(htap, NHT * (l + 1))
                pe.wait_ge(c_v, NCV * l + 1)
                pe.wait_ge(at_oc, g0 + nb)
                for o in range(ORDER):
                    e = ORDER * l + o
                    if o:
                        pe.wait_ge(hy_z, 4 * e)
                    for t in range(2):
                        for s in range(S):
                            for i in range(BT):
                                mm = T_.transpose(bank[t][:, s * WB + i * P:s * WB + (i + 1) * P],
                                                  hvc[:, i, s * SEQ + t * P:s * SEQ + (t + 1) * P], ident)
                        mm.then_inc(hy_t, 1)
                    pe.wait_ge(hy_tc, 2 * e + 2)
                    for f in range(2):
                        for r in range(2):
                            for t in range(2):
                                mm = T_.matmul(bank[2 * r + f][:, 0:N], dft[:, r, t, f * P:(f + 1) * P],
                                               uT[:, t, 0:N], start=(t == 0), stop=(t == 1))
                            mm.then_inc(hy_f, 1)
                    pe.wait_ge(hy_p, 12 * (e + 1))
                    for i in range(BT):
                        for s in range(S):
                            for f in range(2):
                                for r in range(2):
                                    mm = T_.matmul(bank[i][:, s * SEQ:(s + 1) * SEQ],
                                                   ysp[:, r, f, s * WB + i * P:s * WB + (i + 1) * P],
                                                   dft[:, 2 + r, f, :], start=(f == 0 and r == 0),
                                                   stop=(f == 1 and r == 1))
                        mm.then_inc(hy_i, 1)
                pe.wait_ge(b_lo, 4 * (l + 1))
                u0 = AT["gate", l]
                pe.wait_ge(at_oc, g0 + nb)

                def gate_unit(u, b, it, per):
                    for k in range(KD):
                        split_in(u, k, it, per)
                        mm = split3(bank[4 + b][:, 0:T], k, u % 2, Hh[:, k, 0:T], Hl[:, k, 0:T], k == 0, k == KD - 1)
                    mm.then_inc(unit_done, 1)

                with pe.Fori(0, KD // 2) as it:
                    for d in range(2):
                        for i, b in enumerate((0, 1, None, 2, 3)):
                            u = u0 + 5 * d + i
                            if b is not None:
                                pe.wait_ge(sig_done, FREE_MIX + 32 * l + 4 * d + b - 3 + it * 8)
                                gate_unit(u, b, it, 10)
                                continue
                            split_in(u, KD // 2, it, 10)
                            pe.wait_ge(mix_step, mix_at(l, d) + it * 14)
                            for b4 in range(4):
                                for k in range(BT):
                                    mm = split3(bank[b4][:, 0:T], 2 * b4 + k, u % 2, Bh[:, b4, k, 0:T],
                                                Bl[:, b4, k, 0:T], k == 0, k == BT - 1)
                            mm.then_inc(unit_done, 1)
                u0 = AT["wout", l]
                pe.wait_ge(m_lo, 8 * (l + 1))
                ev = 56 * l + 24
                for m in range(KD):
                    pe.wait_ge(out_evac, FREE + ev + m - 1)
                    for k in range(KD):
                        split_in(u0 + m, k)
                        mm = split3(bank[4 + m % 2][:, 0:T], k, (u0 + m) % 2, Uh[:, k, 0:T], Ul[:, k, 0:T],
                                    k == 0, k == KD - 1)
                    mm.then_inc(unit_done, 1)

            filters()
            stats_direct(0)
            for l in range(DEPTH):
                for sub in range(3):
                    n = 6 * l + 2 * sub + 1
                    if sub == 1:
                        mixer(l)
                    else:
                        ffn(2 * l + sub // 2)
                    stats_sums(n)
                    if n < NLN - 1:
                        stats_direct(n + 1)
            for i in range(4):
                t, half = i // 2, i % 2
                for k in range(4):
                    pe.wait_ge(x_tile, 8 * (NLN // 2) + 4 * half + k + 1)
                    mm = T_.transpose(bank[4 + i][:, k * P:(k + 1) * P], X[:, 4 * half + k, t * P:(t + 1) * P], ident)
                mm.then_inc(o_turn, 1)


def _tables():
    f32 = np.float32
    eye = np.eye(P, dtype=f32)
    mats = np.stack([eye, np.full((P, P), 1.0 / D, f32), np.full((P, P), 1.0 / WB, f32), np.ones((P, P), f32)], 1)
    sel = np.array([[1, 0], [1, 0], [0, 1], [0, 1]], f32)
    flip = np.zeros((P, P), f32)
    for p in range(P):
        flip[p, (p // GRID_W) * GRID_W + GRID_W - 1 - p % GRID_W] = 1.0
    t = np.arange(SEQ, dtype=np.float64)
    ang = np.outer(t, (t + 0.5) * 2 * np.pi / (2 * SEQ))
    dft = np.stack([np.cos(ang), np.sin(ang), np.cos(ang).T / SEQ, np.sin(ang).T / SEQ])
    dft = dft.reshape(4, 2, P, SEQ).transpose(2, 0, 1, 3).astype(f32)
    tf = np.arange(SEQ, dtype=f32)
    t_norm = tf / f32(SEQ - 1)
    deltas = np.linspace(math.log(1e-2) / 1.5, math.log(1e-2) / 0.3, WB, dtype=f32)
    dec = np.exp(-t_norm[:, None] * np.abs(deltas)[None, :]).astype(f32)
    back = dec.copy()
    back[0] = 0.0
    decay = np.stack([dec, back], 1).reshape(2, P, 2, WB).transpose(1, 0, 2, 3)
    bands = np.linspace(1e-4, 15, 16, dtype=f32)
    a = (f32(2.0 * math.pi / SEQ) * tf[:, None]) * bands[None, :]
    zT = np.concatenate([t_norm[:, None], np.cos(a), -np.sin(a)], -1).astype(f32).T
    return {"k_mats": mats, "k_sel": sel, "k_flip": flip, "k_dft": dft, "k_decay": decay, "k_zT": zT}


_INS = ("x", "c", "ctx", "c_ctx", "w_mod", "b_mod", "post_ln_g", "post_ln_b", "ffn_w_in", "ffn_w_out", "w_in", "b_in",
        "conf_dw_w", "conf_dw_b", "conf_ln_g", "conf_ln_b", "conf_w_proj", "na_rpb", "na_w_proj", "sc_conv_w",
        "sc_w_proj", "hy_sconv_w", "hy_sconv_b", "hy_w1", "hy_b1", "hy_w2", "hy_b2", "hy_freq", "hy_w3", "hy_bias",
        "hy_w_proj", "w_out", "b_out")


def kernel(**inputs):
    import concourse.bacc as bacc
    from concourse.bass_utils import run_bass_kernel_spmd as run

    nc = bacc.Bacc("TRN2", target_bir_lowering=False, num_devices=1)
    arrays, aps = {}, {}
    for name, arr in [(n, inputs[n]) for n in _INS] + list(_tables().items()):
        arr = np.ascontiguousarray(arr)
        arrays["in_" + name] = arr
        aps[name] = nc.dram_tensor("in_" + name, arr.shape, mybir.dt.from_np(arr.dtype), kind="ExternalInput").ap()
    out = nc.dram_tensor("out", (1, SEQ, D), F32, kind="ExternalOutput").ap()
    build(nc, aps, out)
    return run(nc, [arrays], core_ids=[0]).results[0]["out"]
```

```python
import math
from contextlib import ExitStack

import numpy as np

import concourse.bass as bass
from concourse import mybir

F32 = mybir.dt.float32
F32R = mybir.dt.float32r
ACT = mybir.ActivationFunctionType
ALU = mybir.AluOpType
AX = mybir.AxisListType

P = 128
D = 1024
KD = D // P
SEQ = 256
TOK = 2 * SEQ
DEPTH = 2
D_FF = 2816
JF = D_FF // P
CHUNKS = (8, 8, 6)
N_MOD = 9
MODT = N_MOD * KD
WB = 256
BT = WB // P
CONF_K = 31
PADC = CONF_K // 2
HEADS = 4
DH = 64
SCALE = DH ** -0.5
GRID_W = 64
WIN_ROWS, WIN_COLS = 8, 16
RPB_R, RPB_C = 2 * WIN_ROWS - 1, 2 * WIN_COLS - 1
ROWS = SEQ // GRID_W
MASKED = -1e30
ORDER = 2
PE_DIM = 33
FH = 64
LN_EPS = 1e-5
ALPHA = (2 * DEPTH) ** 0.25
TWO_PI = 2.0 * math.pi
PI_HI = 6.28125
PI_LO = TWO_PI - PI_HI
PI_IN = 3.1415925
ROUND = 1.5 * 2.0 ** 23
M_G = 22

VROW = {"b_mod": (0, 0), "b_in": (0, 72),
        "ln_g": (1, 0), "ln_b": (1, 24), "conf_w": (1, 48), "sc_w": (1, 110), "conf_b": (1, 116),
        "conf_g": (1, 118), "conf_be": (1, 120), "hy_bias": (1, 122),
        "hs_w": (2, 0), "hs_b": (2, 18), "b_out": (2, 24), "hy_b1": (2, 32), "hy_b2": (2, 33), "hy_f": (2, 34)}
NG = 3

WIN_ORDER = (0, 1, 2, 3, 16, 17, 18, 19, 20, 21, 4, 5, 6, 7, 8, 9, 10, 11, 12, 13, 14, 15)
N_WIN = len(WIN_ORDER)
N_SUB = 2 * DEPTH
MOD_IN = ((4, 4, 4), (4, 4, 4), (4, 0, 0), (0, 0, 0))
MOD_OUT = ((2, 2, 2), (2, 2, 2), (0, 0, 0), (0, 0, 0))
MOD_FIRST = 16


def plan():
    u, q = 0, MOD_FIRST
    at, modq, proj = {}, {}, set()

    def ffn(f):
        nonlocal u, q
        for c, n in enumerate(CHUNKS):
            at["in", f, c], modq["in", f, c] = u, q
            u += (n // 2) * 4
            q += (n // 2) * MOD_IN[f][c]
            at["out", f, c], modq["out", f, c] = u, q
            u += KD
            q += 2 * MOD_OUT[f][c]

    for l in range(DEPTH):
        ffn(2 * l)
        at["win", l] = u
        u += N_WIN
        at["gate", l] = u
        for m in range(KD):
            proj.add(u + 5 * m + 2)
        u += 5 * KD
        at["wout", l] = u
        u += KD
        ffn(2 * l + 1)
    assert q == DEPTH * MODT
    return at, modq, proj, u


AT, MODQ, PROJ, UNITS = plan()

SETUP = (("m", 0), ("m", 1), ("m", 2), ("m", 3), ("r", 0), ("x",), ("v",), ("t", 0), ("f", 0, 1), ("m", 4), ("f", 0, 2),
         ("m", 5), ("m", 6), ("f", 0, 3), ("m", 7), ("r", 1), ("f", 0, 4), ("t", 1), ("m", 8), ("f", 0, 5), ("m", 9),
         ("f", 0, 6), ("m", 10), ("f", 1, 1), ("m", 11), ("r", 2), ("f", 1, 2), ("t", 2), ("m", 12), ("m", 13),
         ("f", 1, 3), ("m", 14), ("m", 15), ("r", 3), ("f", 1, 4), ("t", 3))
FIRST_SLOTS = 8
N_CONST, N_VEC = 5, 19


LAST = AT["in", N_SUB - 1, 0]


def landed(u):
    return 16 * (u // 2 + 1) + 48 * sum(1 for x in PROJ if x % 2 == u % 2 and x <= u)


def body_in(nmod):
    mains = [("a", 0, 0), ("g", 0, 1), ("a", 1, 2), ("g", 1, 3)]
    return [x for i, w in enumerate(mains) for x in ([("m", i, i)] if nmod else []) + [w]]


def body_out(nmod):
    mains = [("o", i, i) for i in range(4)]
    return [("m", 0, 0)] + mains[:2] + [("m", 1, 1)] + mains[2:] if nmod else mains


def mod_last(f, kind, c):
    later = [(k, cc) for cc in range(len(CHUNKS)) for k in ("in", "out") if (MOD_IN if k == "in" else MOD_OUT)[f][cc]]
    return bool(later) and later[-1] == (kind, c)


def modbase(f, kind, c):
    n = MOD_FIRST // 4
    for ff in range(N_SUB):
        for cc, j in enumerate(CHUNKS):
            if (ff, "in", cc) == (f, kind, c):
                return n
            n += (j // 2) if MOD_IN[ff][cc] else 0
            if (ff, "out", cc) == (f, kind, c):
                return n
            n += 2 if MOD_OUT[ff][cc] else 0


def streams(l):
    return 2 if l < DEPTH - 1 else 1


def blocks(l):
    return [(s, h, q) for s in range(streams(l)) for h in range(HEADS) for q in range(2)]


def branch_steps(l):
    other = [("c", 1), ("c", 2), ("s", 1), ("c", 3), ("c", 4), ("s", 2), ("b", 0), ("s", 3), ("b", 2)]
    for o in range(ORDER):
        other += [("h", o, i) for i in range(1, 7)]
    other += [("b", 3)]
    att = [("a", n) for n in range(len(blocks(l)) + 3)] + [("b", 1)]
    both = [x for i in range(max(len(other), len(att))) for part in (other, att) for x in part[i:i + 1]]
    order = [x[1] for x in both if x[0] == "b"]
    return [x + (1 + order.index(x[1]),) if x[0] == "b" else x for x in both]


def win_tokens(l, m):
    return TOK if l < DEPTH - 1 or 6 <= m < 10 else SEQ


def build(nc, a, out):
    ctx = ExitStack()
    with ctx:
        def sb(name, shape, dt=F32):
            return ctx.enter_context(nc.sbuf_tensor(name, shape, dt))

        def sem(name):
            return ctx.enter_context(nc.semaphore(name))

        X = sb("X", [P, KD, TOK])
        Y = sb("Y", [P, KD, TOK])
        with nc.sbuf_tensor("HWORK", [P, FIRST_SLOTS, KD, P], F32) as mfirst:
            pass
        Hh = sb("Hh", [P, KD, TOK], F32R)
        Hl = sb("Hl", [P, KD, TOK], F32R)
        with nc.sbuf_tensor("UWORK", [P, 2 * KD * TOK], F32) as Wk:
            pass
        Uh = sb("Uh", [P, KD, TOK], F32R)
        Ul = sb("Ul", [P, KD, TOK], F32R)
        with nc.sbuf_tensor("MWORK", [P, 2, KD, P], F32) as mraw:
            pass
        Bh = sb("Bh", [P, 4, BT, TOK], F32R)
        Bl = sb("Bl", [P, 4, BT, TOK], F32R)
        mwh = [Bh[:, 2 + s, :, :].rearrange("p i (k c) -> p (i k) c", c=P) for s in range(2)]
        mwl = [Bl[:, s, :, :].rearrange("p i (k c) -> p (i k) c", c=P) for s in range(2)]
        raw = [sb(f"raw{s}", [P, KD, P]) for s in range(2)]
        def raw_of(u):
            i = (u - LAST) % 4
            return raw[u % 2] if u < LAST or i >= 2 else mraw[:, i, :, :]

        wh = [sb(f"wh{s}", [P, KD, P], F32R) for s in range(2)]
        wl = [sb(f"wl{s}", [P, KD, P], F32R) for s in range(2)]
        spec = sb("spec", [P, DEPTH, 2, 2, ORDER, WB])
        dft = sb("dft", [P, 4, 2, SEQ])
        mats = sb("mats", [P, 4, P])
        flip = sb("flip", [P, P])
        vec = sb("vec", [P, DEPTH, NG, P])
        bmod2 = sb("bmod2", [P, DEPTH * MODT, 2])
        modv = sb("modv", [P, DEPTH * MODT, 2])
        S4 = sb("S4", [P, KD, 4], F32R)
        modrow = sb("modrow", [4, 4, P])
        sel = sb("sel", [4, 2])
        gate = sb("gate", [P, KD, 2])
        small = sb("small", [P, 64])
        E = sb("E", [P, 5248])

        var = E[:, 0:P]
        rstd = E[:, P:2 * P]
        rows_of = E[:, 512:1536].rearrange("p (v t) -> p v t", v=2)
        mean_all = E[:, 1536:2048]
        tt = [E[:, 2048:2560], E[:, 2560:3072]]
        sq = [E[:, 3072:3584], E[:, 3584:4096]]
        acc1 = E[:, 4096:4608]
        acc2 = E[:, 4608:5120]
        Yf = Y[:].rearrange("p k t -> p (k t)")
        qk = Wk[:, 0:2048].rearrange("p (i t) -> p i t", i=4)
        vtok = Wk[:, 2048:3072].rearrange("p (i c) -> p i c", i=4)
        btab = Wk[:, 3072:5120].rearrange("p (q h r c) -> p q h r c", q=2, h=HEADS, r=ROWS)
        hvc = Wk[:, 5120:8192].rearrange("p (i t) -> p i t", i=6)
        rtab = Wk[:, 6144:8192].rearrange("p (q h r c) -> p q h r c", q=2, h=HEADS, r=ROWS)
        hvpad = Yf[:, 0:3096].rearrange("p (i s t) -> p i s t", i=6, s=2)
        cpad = E[:, 0:1144].rearrange("p (i s t) -> p i s t", i=2, s=2)
        cacc = E[:, 1144:2168].rearrange("p (i t) -> p i t", i=2)
        scpad = E[:, 2168:3200].rearrange("p (i s t) -> p i s t", i=2, s=2)
        sbb = E[:, 3200:4224].rearrange("p (i t) -> p i t", i=2)
        tmpa = E[:, 4224:5248].rearrange("p (i t) -> p i t", i=2)
        cmean, cvar = E[:, 0:512], E[:, 512:1024]
        ysp = E[:, 0:2048].rearrange("p (r f n) -> p r f n", r=2, f=2)
        uT = E[:, 2048:3072].rearrange("p (i n) -> p i n", i=2)
        hprod = [E[:, 3072 + 512 * i:3584 + 512 * i] for i in range(2)]
        sbuf_s = [Yf[:, 512 * i:512 * i + 512] for i in range(2)]
        sbuf_p = [Yf[:, 1024 + 512 * i:1536 + 512 * i] for i in range(2)]
        sbuf_pT = [Yf[:, 2048 + 512 * i:2560 + 512 * i].rearrange("p (k q) -> p k q", k=4) for i in range(2)]
        obuf = Yf[:, 3072:4096].rearrange("p (i t) -> p i t", i=2)
        csq = obuf
        xrow = Yf.rearrange("p (t n) -> p t n", t=4)
        vrow = Wk[:, 0:768].rearrange("p (l g c) -> p l g c", l=DEPTH, g=NG)
        crow = Wk[0:16, 768:896]
        decay = Wk[:, 1024:2048].rearrange("p (t r c) -> p t r c", t=2, r=2)
        zT = Wk[0:PE_DIM, 2048:2304]
        fw1 = Wk[0:PE_DIM, 2304:2304 + 2 * FH].rearrange("p (l c) -> p l c", l=2)
        fw2 = Wk[0:FH, 2432:2432 + 2 * FH].rearrange("p (l c) -> p l c", l=2)
        fw3 = Wk[0:FH, 2560:4608].rearrange("p (l c) -> p l c", l=2)
        farg = Wk[0:FH, 4608:4864]
        fk = Wk[0:FH, 4864:5120]
        fh = Wk[0:FH, 5120:5376]
        filt = E[:, 0:1024].rearrange("p (o r c) -> p o r c", o=ORDER, r=2)
        hp = Wk[:, 5376:6400].rearrange("p (t o c) -> p t o c", t=2, o=ORDER)
        hm = Wk[:, 6400:7424].rearrange("p (t o c) -> p t o c", t=2, o=ORDER)
        hsq = E[:, 2048:4096].rearrange("p (r t n) -> p r t n", r=2, t=2)
        fn = E[:, 4096:4608]
        cs = small[:, 0:16]
        nmax = small[:, 16:18]
        psumr = small[:, 18:20]
        prec = small[:, 20:22]

        ident, invD, invB, ones = (mats[:, i, :] for i in range(4))

        bank = [ctx.enter_context(nc.psum_tensor(f"bank{i}", [P, 512], F32)) for i in range(8)]

        def col(l, name, i=0, rows=slice(0, P)):
            g, r = VROW[name]
            return vec[rows, l, g, r + i:r + i + 1]

        s_c = sem("s_c")
        s_const = sem("s_const")
        s_vec = sem("s_vec")
        s_xin = sem("s_xin")
        w_landed = [sem(f"w_landed{s}") for s in range(2)]
        hi_done = sem("hi_done")
        lo_done = sem("lo_done")
        w4_landed = [sem(f"w4_landed{s}") for s in range(4)]
        m_landed = [sem(f"m_landed{s}") for s in range(2)]
        mfirst_landed = [sem(f"mfirst_landed{s}") for s in range(FIRST_SLOTS)]
        mhi_done = sem("mhi_done")
        mlo_done = sem("mlo_done")
        munit_done = sem("munit_done")
        unit_done = sem("unit_done")
        zero_done = sem("zero_done")
        turned = sem("turned")
        cols_done = sem("cols_done")
        s4hi = sem("s4hi")
        s4lo = sem("s4lo")
        cols_fix = sem("cols_fix")
        x_turned = sem("x_turned")
        x_tile = sem("x_tile")
        sq_tile = sem("sq_tile")
        acc_step = sem("acc_step")
        stat_mm = sem("stat_mm")
        stat_cp = sem("stat_cp")
        stat_v = sem("stat_v")
        rows_zero = sem("rows_zero")
        stat_rows = sem("stat_rows")
        stat_all = sem("stat_all")
        mean_cp = sem("mean_cp")
        stat_sd = sem("stat_sd")
        t_sub = sem("t_sub")
        t_mul = sem("t_mul")
        h_full = sem("h_full")
        h_fullv = sem("h_fullv")
        h_hi = sem("h_hi")
        h_lo = sem("h_lo")
        mrow_done = sem("mrow_done")
        mcol_mm = sem("mcol_mm")
        mod_done = sem("mod_done")
        silu_done = sem("silu_done")
        prod_done = sem("prod_done")
        u_hi = sem("u_hi")
        u_lo = sem("u_lo")
        out_evac = sem("out_evac")
        resid = sem("resid")
        gate_rdy = sem("gate_rdy")
        f_mm = sem("f_mm")
        f_v = sem("f_v")
        f_a = sem("f_a")
        pads = sem("pads")
        s_rtab = sem("s_rtab")
        r_mask = sem("r_mask")
        flipped = sem("flipped")
        btab_cp = sem("btab_cp")
        win_evac = sem("win_evac")
        cglu = sem("cglu")
        ctap = sem("ctap")
        htap = sem("htap")
        stap = sem("stap")
        c_sq = sem("c_sq")
        c_mm = sem("c_mm")
        c_cp = sem("c_cp")
        c_v = sem("c_v")
        c_sd = sem("c_sd")
        c_silu = sem("c_silu")
        b_hi = sem("b_hi")
        b_lo = sem("b_lo")
        at_s = sem("at_s")
        at_v = sem("at_v")
        at_m = sem("at_m")
        at_e = sem("at_e")
        at_r = sem("at_r")
        at_n = sem("at_n")
        at_t = sem("at_t")
        at_tc = sem("at_tc")
        at_o = sem("at_o")
        at_oc = sem("at_oc")
        hy_t = sem("hy_t")
        hy_tc = sem("hy_tc")
        hy_f = sem("hy_f")
        hy_p = sem("hy_p")
        hy_i = sem("hy_i")
        hy_z = sem("hy_z")
        sig_done = sem("sig_done")
        mix_step = sem("mix_step")
        m_hi = sem("m_hi")
        m_lo = sem("m_lo")
        o_turn = sem("o_turn")
        o_copy = sem("o_copy")
        s_out = sem("s_out")

        NB0 = len([1 for s in range(2) for h in range(HEADS) for q in range(2)])

        def lnt(n):
            return TOK if n <= 8 else SEQ

        def ffn_tok(f):
            return TOK if f < 3 else SEQ

        NLN = 6 * DEPTH

        V_TILES = (0, 5)

        def hfull_at(n, k):
            return sum((KD - len(V_TILES)) * (lnt(x) // SEQ) for x in range(0, n, 2)) + \
                sum(lnt(n) // SEQ for x in range(k + 1) if x not in V_TILES)

        def spec_bank(l, i, f):
            return 4 + f if i == 0 or l == DEPTH - 1 else f

        KSUM, KSUM_X = KD - 2, KD - 1

        def acc_at(i):
            return KD + i * (2 * KSUM_X + KSUM)

        FS = 6
        FV = 2 * FS + 12 + 4 + 4
        FM = 2 + 4 + 1 + 4
        NHT = 18
        NST = 2 + 6 + 2
        NCV = 8
        AV0 = 24
        FREE = 2
        FREE_MIX = 4
        FREE_LO = 4

        def mix_at(l, d):
            return FREE_MIX + 56 * l + 7 * d

        block = ctx.enter_context(nc.Block())

        @block.sync
        def _(sp):
            def unit(u, it, per, srcs):
                back = 4 if u >= LAST else 2
                sp.wait_ge(lo_done, FREE_LO + 2 * (u + 1 - back) + it * (2 * per))
                sp.nop(nofuse=True)
                into = w4_landed[(u - LAST) % 4] if u >= LAST else w_landed[u % 2]
                for lo, n, src in srcs:
                    sp.dma_start(raw_of(u)[:, lo:lo + n, :], src).then_inc(into, 16)

            def mod_unit(q, it, step, i):
                n = q + i
                sp.wait_ge(mlo_done, n - 1 + it * step)
                sp.nop(nofuse=True)
                sp.dma_start(mraw[:, n % 2, :, :], mod_src(q, it, step, i)).then_inc(m_landed[n % 2], 16)

            def rows(w, c0):
                return w.rearrange("(k p) n -> p k n", p=P)[:, :, bass.ds(c0, P)]

            def mod_src(q, it, step, i):
                l = q // MODT
                return rows(a["w_mod"][l], (q % MODT + i) * P + it * step * P)

            def xload():
                for t in range(2):
                    sp.dma_start(xrow[:, t, :], a["x"][0, t * P:(t + 1) * P, :]).then_inc(s_xin, 16)
                    sp.dma_start(xrow[:, 2 + t, :], a["ctx"][0, t * P:(t + 1) * P, :]).then_inc(s_xin, 16)

            def vload(name, src):
                g, r = VROW[name]
                n, _, w = src.shape
                sp.dma_start(vrow[r:r + n, :, g, 0:w], src).then_inc(s_vec, 16)

            def vectors():
                sp.wait_ge(zero_done, 1)
                vload("b_mod", a["b_mod"].rearrange("l (k p) -> k l p", p=P))
                vload("b_in", a["b_in"].rearrange("l (k p) -> k l p", p=P))
                vload("ln_g", a["post_ln_g"].rearrange("l i (k p) -> (i k) l p", p=P))
                vload("ln_b", a["post_ln_b"].rearrange("l i (k p) -> (i k) l p", p=P))
                vload("conf_w", a["conf_dw_w"].rearrange("l i (k p) -> (i k) l p", p=P))
                vload("sc_w", a["sc_conv_w"].rearrange("l i (k p) -> (i k) l p", p=P))
                vload("conf_b", a["conf_dw_b"].rearrange("l (k p) -> k l p", p=P))
                vload("conf_g", a["conf_ln_g"].rearrange("l (k p) -> k l p", p=P))
                vload("conf_be", a["conf_ln_b"].rearrange("l (k p) -> k l p", p=P))
                vload("hy_bias", a["hy_bias"].rearrange("l i (k p) -> (i k) l p", p=P))
                vload("hs_w", a["hy_sconv_w"].rearrange("l i (k p) -> (i k) l p", p=P))
                vload("hs_b", a["hy_sconv_b"].rearrange("l (k p) -> k l p", p=P))
                vload("b_out", a["b_out"].rearrange("l (k p) -> k l p", p=P))
                vload("hy_b1", a["hy_b1"].rearrange("(o l) p -> o l p", o=1))
                vload("hy_b2", a["hy_b2"].rearrange("(o l) p -> o l p", o=1))
                vload("hy_f", a["hy_freq"].rearrange("l i p -> i l p"))
                sp.dma_start(fw1, a["hy_w1"].rearrange("l k c -> k l c")).then_inc(s_vec, 16)
                sp.dma_start(fw2, a["hy_w2"].rearrange("l k c -> k l c")).then_inc(s_vec, 16)
                sp.dma_start(fw3, a["hy_w3"].rearrange("l k c -> k l c")).then_inc(s_vec, 16)

            sp.dma_start(crow[0:8, :], a["c"].rearrange("b (k p) -> (b k) p", p=P)).then_inc(s_c, 16)
            sp.dma_start(crow[8:16, :], a["c_ctx"].rearrange("(k p) -> k p", p=P)).then_inc(s_c, 16)
            sp.dma_start(mats[:], a["k_mats"]).then_inc(s_c, 16)
            for q in range(MOD_FIRST):
                if q >= FIRST_SLOTS:
                    sp.wait_ge(mlo_done, q - FIRST_SLOTS + 1)
                sp.dma_start(mfirst[:, q % FIRST_SLOTS, :, :], rows(a["w_mod"][0], q * P))\
                    .then_inc(mfirst_landed[q % FIRST_SLOTS], 16)
                if q == 3:
                    xload()
                    vectors()

            def ffn(f):
                l, s = f // 2, f % 2
                if f == N_SUB - 1:
                    sp.wait_ge(unit_done, AT["wout", DEPTH - 1])
                if f in (1, 2):
                    sp.wait_ge(unit_done, AT["wout", 0])
                j0 = 0
                for c, n in enumerate(CHUNKS):
                    u0, q0 = AT["in", f, c], MODQ["in", f, c]
                    body = body_in(MOD_IN[f][c])
                    with sp.Fori(0, n // 2) as it:
                        for kind, x, i in body:
                            if kind == "m":
                                mod_unit(q0, it, 4, x)
                            else:
                                src = rows(a["ffn_w_in"][l, s],
                                           (D_FF if kind == "g" else 0) + (j0 + x) * P + it * 2 * P)
                                unit(u0 + i, it, 4, [(0, KD, src)])
                    u0, q0 = AT["out", f, c], MODQ["out", f, c]
                    body = body_out(MOD_OUT[f][c])
                    with sp.Fori(0, 2) as it:
                        for kind, x, i in body:
                            if kind == "m":
                                mod_unit(q0, it, 2, x)
                            else:
                                w = a["ffn_w_out"][l, s, j0 * P:(j0 + n) * P, :]
                                unit(u0 + i, it, 4, [(0, n, rows(w, x * P + it * 4 * P))])
                    j0 += n

            def mixer(l):
                def win_units(first, last):
                    for i in range(first, last):
                        unit(AT["win", l] + i, 0, 0, [(0, KD, rows(a["w_in"][l], WIN_ORDER[i] * P))])

                win_units(0, 2)
                sp.wait_ge(unit_done, AT["win", l])
                rpb = a["na_rpb"]
                for r in range(ROWS):
                    for h in range(HEADS):
                        off = ((l * HEADS + h) * RPB_R + WIN_ROWS - 1 - r) * RPB_C + WIN_COLS - 1 - (GRID_W - 1)
                        src = bass.AP(tensor=rpb.tensor, offset=rpb.offset + off,
                                      ap=[[1, GRID_W], [RPB_C, ROWS], [1, GRID_W]])
                        sp.dma_start(rtab[GRID_W * (r % 2):GRID_W * (r % 2 + 1), r // 2, h, :, :],
                                     src).then_inc(s_rtab, 16)
                win_units(2, N_WIN)
                u0 = AT["gate", l]
                with sp.Fori(0, KD // 2) as it:
                    for d in range(2):
                        for i, b in enumerate((0, 1, None, 2, 3)):
                            if b is None:
                                srcs = [(2 * n, BT, rows(a[w][l], d * P + it * 2 * P)) for n, w in
                                        enumerate(("conf_w_proj", "na_w_proj", "sc_w_proj", "hy_w_proj"))]
                            else:
                                srcs = [(0, KD, rows(a["w_in"][l], (M_G + KD * b + d) * P + it * 2 * P))]
                            unit(u0 + 5 * d + i, it, 10, srcs)
                u0 = AT["wout", l]
                with sp.Fori(0, KD // 4) as it:
                    for i in range(4):
                        unit(u0 + i, it, 4, [(0, KD, rows(a["w_out"][l], i * P + it * 4 * P))])

            for l in range(DEPTH):
                ffn(2 * l)
                mixer(l)
                ffn(2 * l + 1)
            for t in range(2):
                sp.wait_ge(o_copy, 2 * (t + 1))
                sp.dma_start(out[0, t * P:(t + 1) * P, :], xrow[:, t, :]).then_inc(s_out, 16)
            sp.wait_ge(s_out, 32)

        @block.gpsimd
        def _(pool):
            pool.memset(Wk[:, 0:NG * DEPTH * P], 0.0).then_inc(zero_done, 1)
            pool.wait_ge(zero_done, 1)

            pool.dma_start(zT, a["k_zT"]).then_inc(s_const, 16)
            pool.dma_start(sel[:], a["k_sel"]).then_inc(s_const, 16)
            pool.dma_start(decay, a["k_decay"]).then_inc(s_const, 16)
            pool.dma_start(dft[:], a["k_dft"]).then_inc(s_const, 16)
            pool.dma_start(flip[:], a["k_flip"]).then_inc(s_const, 16)

            n_acc = 0

            def sum_sq(n, with_x):
                nonlocal n_acc
                T = lnt(n)
                for k in range(KSUM_X if with_x else KSUM if n else KD):
                    src = sq[k % 2] if with_x or n == 0 else Y[:, k, :]
                    base = n_acc
                    if with_x:
                        pool.wait_ge(resid, 8 * (n // 2) + k + 1)
                        if k == 0:
                            pool.tensor_copy(acc1[:, 0:T], X[:, k, 0:T]).then_inc(acc_step, 1)
                        else:
                            pool.wait_ge(acc_step, base - 1)
                            pool.tensor_tensor(acc1[:, 0:T], acc1[:, 0:T], X[:, k, 0:T],
                                               ALU.add).then_inc(acc_step, 1)
                        n_acc += 1
                    pool.wait_ge(sq_tile, 8 * n + k + 1)
                    if k == 0:
                        pool.tensor_copy(acc2[:, 0:T], src[:, 0:T]).then_inc(acc_step, 1)
                    else:
                        pool.wait_ge(acc_step, base)
                        pool.tensor_tensor(acc2[:, 0:T], acc2[:, 0:T], src[:, 0:T],
                                           ALU.add).then_inc(acc_step, 1)
                    n_acc += 1

            def masks(l):
                pool.wait_ge(s_rtab, 16 * 16 * (l + 1))
                pool.wait_ge(t_sub, 8 * (6 * l + 2) + KD)
                k = 8 * l
                for q in range(2):
                    for half in range(2):
                        rows = slice(GRID_W * half, GRID_W * half + GRID_W)
                        v = rtab[rows, q, :, :, 0:GRID_W - WIN_COLS].rearrange("p h r c -> p (h r) c")
                        pool.affine_select(out=v, in_=v, compare_op=ALU.is_ge, fill=MASKED,
                                           base=WIN_COLS // 2 - (GRID_W - 1),
                                           pattern=[[0, HEADS * ROWS], [1, GRID_W - WIN_COLS]],
                                           channel_multiplier=1).then_inc(r_mask, 1)
                        pool.wait_ge(r_mask, k + 1)
                        v = rtab[rows, q, :, :, WIN_COLS:GRID_W].rearrange("p h r c -> p (h r) c")
                        pool.affine_select(out=v, in_=v, compare_op=ALU.is_ge, fill=MASKED,
                                           base=GRID_W - 1 + WIN_COLS // 2 - 1 - WIN_COLS,
                                           pattern=[[0, HEADS * ROWS], [-1, GRID_W - WIN_COLS]],
                                           channel_multiplier=-1).then_inc(r_mask, 1)
                        k += 2
                        pool.wait_ge(r_mask, k)

            def apply_mod(n):
                T = lnt(n)
                pool.wait_ge(mean_cp, n // 2 + 1)
                for k in range(KD):
                    pool.tensor_tensor(Y[:, k, 0:T], X[:, k, 0:T], mean_all[:, 0:T],
                                       ALU.subtract).then_inc(t_sub, 1)

            sum_sq(0, False)
            apply_mod(0)
            for l in range(DEPTH):
                for sub in range(3):
                    n = 6 * l + 2 * sub + 1
                    sum_sq(n, True)
                    if n < NLN - 1:
                        sum_sq(n + 1, False)
                        apply_mod(n + 1)
                    if sub == 0:
                        masks(l)

        @block.scalar
        def _(act):
            def hi(u, it=0, per=0):
                if u >= LAST:
                    act.wait_ge(w4_landed[(u - LAST) % 4], 16 * ((u - LAST) // 4 + 1) + it * (4 * per))
                else:
                    step = landed(u + per) - landed(u) if per else 0
                    act.wait_ge(w_landed[u % 2], landed(u) + it * step)
                if u >= 2:
                    act.wait_ge(unit_done, u - 1 + it * per)
                for h in range(2):
                    k = slice(h * KD // 2, (h + 1) * KD // 2)
                    nc.scalar.activation(wh[u % 2][:, k, :], raw_of(u)[:, k, :], ACT.Copy).then_inc(hi_done, 1)

            def nxt(u, it=0, per=0):
                if per or u + 2 < UNITS:
                    hi(u + 2, it, per)

            def mhi(q, it=0, step=0):
                act.wait_ge(m_landed[q % 2], 16 * ((q - MOD_FIRST) // 2 + 1) + it * (8 * step))
                act.wait_ge(munit_done, q - 1 + it * step)
                nc.scalar.activation(mwh[q % 2], mraw[:, q % 2, :, :], ACT.Copy).then_inc(mhi_done, 1)

            def mhi_first(q):
                act.wait_ge(mfirst_landed[q % FIRST_SLOTS], 16 * (q // FIRST_SLOTS + 1))
                if q >= 2:
                    act.wait_ge(munit_done, q - 1)
                nc.scalar.activation(mwh[q % 2], mfirst[:, q % FIRST_SLOTS, :, :], ACT.Copy)\
                    .then_inc(mhi_done, 1)

            def rows_out(q, n_prev, it, step, nm):
                act.wait_ge(munit_done, q + 1 + it * step)
                if n_prev:
                    act.wait_ge(mcol_mm, n_prev + it)
                nc.scalar.activation(modrow[:, 0:nm, :],
                                     bank[6][0:4, 0:nm * P].rearrange("p (i c) -> p i c", i=nm),
                                     ACT.Copy).then_inc(mrow_done, 1)

            act.wait_ge(lo_done, FREE_LO)
            act.wait_ge(turned, 1)
            nc.scalar.activation(cs, bank[2][:, 0:16], ACT.Silu).then_inc(cols_done, 1)
            act.wait_ge(cols_done, 1)
            for s in range(2):
                nc.scalar.activation(S4[:, :, 2 * s], cs[:, 8 * s:8 * s + 8], ACT.Copy).then_inc(s4hi, 1)
            mhi_first(0)
            mhi_first(1)

            def turn_x():
                for k in range(KD):
                    act.wait_ge(x_turned, k + 1)
                    nc.scalar.activation(X[:, k, :], bank[4 + k % 2][:], ACT.Copy, scale=ALPHA).then_inc(x_tile, 1)
                    act.wait_ge(x_tile, k + 1)
                    if k >= 2:
                        act.wait_ge(acc_step, k - 1)
                    nc.scalar.activation(sq[k % 2][:], X[:, k, :], ACT.Square).then_inc(sq_tile, 1)

            def filters(l, step):
                if step <= 2:
                    act.wait_ge(f_v, FV * l + FS * step)
                    nc.scalar.activation(fh, farg, ACT.Sin).then_inc(f_a, 1)
                elif step == 3:
                    act.wait_ge(acc_step, KD)
                    act.wait_ge(f_v, FV * l + 2 * FS + 12)
                    nc.scalar.activation(hsq[:, 0, :, :], hp.rearrange("p t o c -> p t (o c)"), ACT.Square)\
                        .then_inc(f_a, 1)
                    nc.scalar.activation(hsq[:, 1, :, :], hm.rearrange("p t o c -> p t (o c)"), ACT.Square)\
                        .then_inc(f_a, 1)
                elif step == 4:
                    act.wait_ge(f_v, FV * l + 2 * FS + 15)
                    nc.scalar.activation(fn, fn, ACT.Sqrt).then_inc(f_a, 1)

            for what, *x in SETUP:
                if what == "m" and x[0] + 2 < MOD_FIRST:
                    mhi_first(x[0] + 2)
                elif what == "r":
                    rows_out(4 * x[0] + 3, x[0], 0, 0, 4)
                elif what == "x":
                    turn_x()
                elif what == "v":
                    act.wait_ge(turned, 3)
                    for l in range(DEPTH):
                        nc.scalar.activation(vec[:, l, :, :],
                                             bank[l][:, 0:NG * P].rearrange("p (g c) -> p g c", g=NG),
                                             ACT.Copy).then_inc(cols_done, 1)
                elif what == "f":
                    filters(*x)
            hi(0)
            hi(1)
            for q in range(2):
                mhi(MOD_FIRST + q)

            n_x = KD
            n_acc = KD

            def stats(n):
                T = lnt(n)
                rows = slice(0, T // 4)
                act.wait_ge(stat_mm, 2 * n + 1)
                nc.scalar.activation(var[rows], bank[0][rows, 0:P], ACT.Square).then_inc(stat_cp, 1)
                if n in (0, 3, 9):
                    act.wait_ge(rows_zero, (0, 3, 9).index(n) + 1)
                for j in range(T // P):
                    i = nc.scalar.activation(rows_of[32 * j:32 * j + 1, 0, j * P:(j + 1) * P],
                                             bank[0][32 * j:32 * j + 1, 0:P], ACT.Copy)
                i.then_inc(stat_rows, 1)
                act.wait_ge(stat_v, 4 * n + 2)
                nc.scalar.activation(var[rows], var[rows], ACT.Sqrt).then_inc(stat_sd, 1)
                if n % 2 == 0:
                    act.wait_ge(stat_all, 2 * n + 1)
                    nc.scalar.activation(mean_all[:, 0:T], bank[2][:, 0:T], ACT.Copy).then_inc(mean_cp, 1)

            def apply_post(n):
                nonlocal n_x, n_acc
                T, l, i = lnt(n), n // 6, (n % 6) // 2
                for k in range(KD + 1):
                    if k < KD:
                        act.wait_ge(t_mul, 8 * n + k + 1)
                        nc.scalar.activation(X[:, k, 0:T], Y[:, k, 0:T], ACT.Identity,
                                             bias=col(l, "ln_b", 8 * i + k), scale=col(l, "ln_g", 8 * i + k))\
                            .then_inc(x_tile, 1)
                        n_x += 1
                    if k and n < NLN - 1:
                        act.wait_ge(x_tile, n_x - (k < KD))
                        nc.scalar.activation(Y[:, k - 1, 0:T], X[:, k - 1, 0:T], ACT.Square).then_inc(sq_tile, 1)
                n_acc += 2 * KSUM_X + KSUM

            def apply_mod(n):
                T, l, i = lnt(n), n // 6, (n % 6) // 2
                act.wait_ge(mod_done, modbase((0, 1, 1, 2, 3, 3)[n // 2], "in", 0))
                for k in range(KD):
                    if k in V_TILES:
                        act.wait_ge(h_fullv, len(V_TILES) * (n // 2) + V_TILES.index(k) + 1)
                    else:
                        act.wait_ge(t_mul, 8 * n + k + 1)
                        for s in range(T // SEQ):
                            t = slice(s * SEQ, (s + 1) * SEQ)
                            q = l * MODT + 24 * i + k
                            nc.scalar.activation(Y[:, k, t], Y[:, k, t], ACT.Identity,
                                                 bias=modv[:, q, s:s + 1], scale=modv[:, q + 8, s:s + 1])\
                                .then_inc(h_full, 1)
                        act.wait_ge(h_full, hfull_at(n, k))
                    nc.scalar.activation(Hh[:, k, 0:T], Y[:, k, 0:T], ACT.Copy).then_inc(h_hi, 1)

            def mod_step(q, it, step, x, nbody, nm, ahead):
                if ahead:
                    mhi(q + x + 2, it, step)
                if x == nm - 1:
                    rows_out(q + x, nbody, it, step, nm)

            def hidden(f, c, x, u, it):
                T = ffn_tok(f)
                J = f * JF + sum(CHUNKS[:c]) + x
                nc.scalar.activation(tt[x][:, 0:T], bank[2 * x + 1][:, 0:T], ACT.Silu).then_inc(silu_done, 1)
                act.wait_ge(prod_done, FREE + J + 1 + it * 2)
                nc.scalar.activation(Uh[:, bass.ds(it * 2 + x, 1), 0:T].rearrange("p o t -> p (o t)"),
                                     sq[x][:, 0:T], ACT.Copy).then_inc(u_hi, 1)

            def tail(n, m):
                T = lnt(n)
                act.wait_ge(resid, 8 * (n // 2) + m + 1)
                if m >= 2:
                    act.wait_ge(acc_step, n_acc + 2 * (m - 1))
                nc.scalar.activation(sq[m % 2][:, 0:T], X[:, m, 0:T], ACT.Square).then_inc(sq_tile, 1)

            def out_tile(n, u0, m):
                if m == KD - 1:
                    tail(n, m)
                    nxt(u0 + m)
                    return
                nxt(u0 + m)
                if m:
                    tail(n, m - 1)
                if m == KD - 2:
                    tail(n, m)

            def ffn(f):
                l, s = f // 2, f % 2
                n = 6 * l + (1 if s == 0 else 5)
                for c, nj in enumerate(CHUNKS):
                    u0, q0, nm = AT["in", f, c], MODQ["in", f, c], MOD_IN[f][c]
                    nb_ = modbase(f, "in", c)

                    def in_body(it, ahead):
                        for kind, x, i in body_in(nm):
                            if kind == "m":
                                act.wait_ge(munit_done, q0 + x + 1 + it * 4)
                                mod_step(q0, it, 4, x, nb_, nm, ahead or x < 2)
                                continue
                            act.wait_ge(unit_done, u0 + i + 1 + it * 4)
                            nxt(u0 + i, it, 4)
                            if kind == "g":
                                hidden(f, c, x, u0 + i, it)

                    peel = mod_last(f, "in", c)
                    nc.scalar.activation(small[:, 40:41], small[:, 36:37], ACT.Silu)
                    with act.Fori(0, nj // 2 - peel) as it:
                        in_body(it, True)
                    if peel:
                        in_body(nj // 2 - 1, False)
                    u0, q0, nm = AT["out", f, c], MODQ["out", f, c], MOD_OUT[f][c]
                    nb_ = modbase(f, "out", c)

                    def out_body(it, last):
                        for kind, x, i in body_out(nm):
                            if kind == "m":
                                act.wait_ge(munit_done, q0 + x + 1 + it * 2)
                                mod_step(q0, it, 2, x, nb_, nm, not (last and it == 1))
                                continue
                            act.wait_ge(unit_done, u0 + i + 1 + it * 4)
                            if last:
                                out_tile(n, u0, 4 * it + x)
                            else:
                                nxt(u0 + i, it, 4)

                    if c < len(CHUNKS) - 1:
                        with act.Fori(0, 2) as it:
                            out_body(it, False)
                    else:
                        for it in range(2):
                            out_body(it, True)

            def branch_hi(l, b, src, S):
                nc.scalar.activation(Bh[:, b, :, 0:S * SEQ], src[:, :, 0:S * SEQ], ACT.Copy).then_inc(b_hi, 1)

            def mixer(l):
                S = streams(l)
                T = S * SEQ
                u0 = AT["win", l]
                for i, m in enumerate(WIN_ORDER):
                    u = u0 + i
                    act.wait_ge(unit_done, u + 1)
                    nxt(u)
                    b = col(l, "b_in", m)
                    src = bank[i % 4]
                    if i == 0:
                        act.wait_ge(pads, 6 * (l + 1))
                    if m in (0, 1):
                        o, f, v = tmpa[:, m, 0:T], ACT.Identity, src[:, 0:T]
                    elif m in (2, 3):
                        o, f, v = cacc[:, m - 2, 0:T], ACT.Sigmoid, src[:, 0:T]
                    elif m >= 16:
                        o, f, v = hvpad[:, m - 16, 0:S, 1:SEQ + 1], ACT.Identity, \
                            src[:, 0:T].rearrange("p (s t) -> p s t", s=S)
                    elif m < 8:
                        TT = win_tokens(l, m)
                        o, f, v = qk[:, m - 4, 0:TT], ACT.Identity, src[:, 0:TT]
                    elif m < 10:
                        o, f, v, b = vtok[:, :, (m - 8) * P:(m - 7) * P], ACT.Copy, \
                            src[:, :].rearrange("p (t c) -> p t c", t=4), 0.0
                    elif m < 12:
                        o, f, v = sbb[:, m - 10, 0:T], ACT.Identity, src[:, 0:T]
                    elif m < 14:
                        if m == 12:
                            act.wait_ge(cglu, 2 * (l + 1))
                        o, f, v = tmpa[:, m - 12, 0:T], ACT.Identity, src[:, 0:T]
                    else:
                        o, f, v = scpad[:, m - 14, 0:S, 1:SEQ + 1], ACT.Identity, \
                            src[:, 0:T].rearrange("p (s t) -> p s t", s=S)
                    nc.scalar.activation(o, v, f, bias=b).then_inc(win_evac, 1)
                    if i == 4:
                        for q in range(2):
                            for h2 in range(2):
                                act.wait_ge(flipped, 4 * l + 2 * q + h2 + 1)
                                nc.scalar.activation(
                                    btab[:, q, 2 * h2:2 * h2 + 2, :, :].rearrange("p h r c -> p (h r c)"),
                                    bank[4 + 2 * q + h2][:], ACT.Copy).then_inc(btab_cp, 1)

                def conformer(step):
                    if step == 1:
                        act.wait_ge(htap, NHT * (l + 1))
                        act.wait_ge(ctap, 2 * CONF_K * (l + 1))
                        nc.scalar.activation(csq[:, :, 0:T], cacc[:, :, 0:T], ACT.Square).then_inc(c_sq, 1)
                        act.wait_ge(c_mm, 2 * l + 1)
                        nc.scalar.activation(cmean[:, 0:T], bank[0][:, 0:T], ACT.Copy).then_inc(c_cp, 1)
                        nc.scalar.activation(cvar[:, 0:T], bank[0][:, 0:T], ACT.Square).then_inc(c_cp, 1)
                    elif step == 2:
                        act.wait_ge(c_v, 8 * l + 2)
                        nc.scalar.activation(cvar[:, 0:T], cvar[:, 0:T], ACT.Sqrt).then_inc(c_sd, 1)
                    elif step == 4:
                        for i in range(BT):
                            act.wait_ge(c_v, 8 * l + 6 + 2 * i)
                            nc.scalar.activation(cacc[:, i, 0:T], cacc[:, i, 0:T], ACT.Silu,
                                                 bias=col(l, "conf_be", i), scale=col(l, "conf_g", i))\
                                .then_inc(c_silu, 1)
                        act.wait_ge(c_silu, 2 * (l + 1))

                bl = blocks(l)
                nb = len(bl)
                g0 = NB0 * l

                def attention(n):
                    if n < nb:
                        K = TOK if bl[n][0] == 0 else SEQ
                        act.wait_ge(at_m, g0 + n + 1)
                        if n >= 2:
                            act.wait_ge(at_t, g0 + n - 1)
                        nc.scalar.activation(sbuf_p[n % 2][:, 0:K], sbuf_s[n % 2][:, 0:K], ACT.Exp,
                                             bias=nmax[:, n % 2:n % 2 + 1],
                                             accum_out=psumr[:, n % 2:n % 2 + 1]).then_inc(at_e, 1)
                    m = n - 2
                    if 0 <= m < nb:
                        kt = 4 if bl[m][0] == 0 else 2
                        act.wait_ge(at_t, g0 + m + 1)
                        if m >= 2:
                            act.wait_ge(at_o, g0 + m - 1)
                        nc.scalar.activation(sbuf_pT[m % 2][:, 0:kt, :],
                                             bank[6][:, 0:kt * P].rearrange("p (k q) -> p k q", k=kt),
                                             ACT.Copy).then_inc(at_tc, 1)
                    m = n - 3
                    if 0 <= m < nb:
                        s, h, q = bl[m]
                        rr = slice(DH * (h % 2), DH * (h % 2) + DH)
                        act.wait_ge(at_o, g0 + m + 1)
                        nc.scalar.activation(obuf[rr, h // 2, s * SEQ + q * P:s * SEQ + (q + 1) * P],
                                             bank[7][rr, 0:P], ACT.Identity,
                                             bias=col(l, "b_in", 8 + h // 2, rr)).then_inc(at_oc, 1)

                def hyena(o, step):
                    if step == 1:
                        if o == 0:
                            act.wait_ge(b_lo, 4 * l + 2)
                        for i in range(2):
                            act.wait_ge(hy_t, 2 * (ORDER * l + o) + i + 1)
                            nc.scalar.activation(uT[:, i, 0:S * WB], bank[i][:, 0:S * WB], ACT.Copy)\
                                .then_inc(hy_tc, 1)

                for what, *x in branch_steps(l):
                    if what == "c":
                        conformer(*x)
                    elif what == "h":
                        hyena(*x)
                    elif what == "a":
                        attention(*x)
                    elif what == "s":
                        continue
                    elif x[0] == 0:
                        branch_hi(l, 0, cacc, S)
                    elif x[0] == 2:
                        act.wait_ge(stap, NST * (l + 1))
                        branch_hi(l, 2, tmpa, S)
                    elif x[0] == 1:
                        act.wait_ge(at_oc, g0 + nb)
                        branch_hi(l, 1, obuf, S)
                    else:
                        act.wait_ge(hy_z, 4 * ORDER * (l + 1))
                        branch_hi(l, 3, hvc[:, 0:BT, :], S)
                u0 = AT["gate", l]
                nc.scalar.activation(small[:, 40:41], small[:, 36:37], ACT.Sigmoid)
                with act.Fori(0, KD // 2) as it:
                    for d in range(2):
                        for i, b in enumerate((0, 1, None, 2, 3)):
                            u = u0 + 5 * d + i
                            act.wait_ge(unit_done, u + 1 + it * 10)
                            nxt(u, it, 10)
                            if b is None:
                                continue
                            act.wait_ge(mix_step, mix_at(l, d) + (-3, -1, 1, 2)[b] + it * 14)
                            nc.scalar.activation(
                                tt[b % 2][:, 0:T], bank[4 + b][:, 0:T], ACT.Sigmoid,
                                bias=vec[:, l, 0, bass.ds(it * 2 + VROW["b_in"][1] + M_G + KD * b + d, 1)])\
                                .then_inc(sig_done, 1)
                        act.wait_ge(mix_step, mix_at(l, d) + 7 + it * 14)
                        nc.scalar.activation(Uh[:, bass.ds(it * 2 + d, 1), 0:T].rearrange("p o t -> p (o t)"),
                                             acc1[:, 0:T], ACT.Copy).then_inc(m_hi, 1)
                u0 = AT["wout", l]
                for m in range(KD):
                    act.wait_ge(unit_done, u0 + m + 1)
                    out_tile(6 * l + 3, u0, m)

            stats(0)
            apply_mod(0)
            for l in range(DEPTH):
                for sub in range(3):
                    n = 6 * l + 2 * sub + 1
                    if sub == 1:
                        mixer(l)
                    else:
                        ffn(2 * l + sub // 2)
                    if n in (3, 5):
                        for i in range(2):
                            mhi(MODQ["in", n // 2, 0] + i)
                    stats(n)
                    apply_post(n)
                    if n < NLN - 1:
                        stats(n + 1)
                        apply_mod(n + 1)
            for i in range(4):
                act.wait_ge(o_turn, i + 1)
                nc.scalar.activation(xrow[:, i // 2, (i % 2) * 512:(i % 2 + 1) * 512], bank[4 + i][:],
                                     ACT.Copy).then_inc(o_copy, 1)

        @block.vector
        def _(dve):
            V = nc.vector

            def lo(u, it=0, per=0):
                for h in range(2):
                    k = slice(h * KD // 2, (h + 1) * KD // 2)
                    dve.wait_ge(hi_done, 2 * u + 1 + h + it * (2 * per))
                    V.tensor_tensor(wl[u % 2][:, k, :], raw_of(u)[:, k, :], wh[u % 2][:, k, :].bitcast(F32),
                                    ALU.subtract).then_inc(lo_done, 1)

            def mlo(q, it=0, step=0):
                dve.wait_ge(mhi_done, q + 1 + it * step)
                V.tensor_tensor(mwl[q % 2], mraw[:, q % 2, :, :], mwh[q % 2].bitcast(F32),
                                ALU.subtract).then_inc(mlo_done, 1)

            def mlo_first(q):
                dve.wait_ge(mhi_done, q + 1)
                V.tensor_tensor(mwl[q % 2], mfirst[:, q % FIRST_SLOTS, :, :], mwh[q % 2].bitcast(F32),
                                ALU.subtract).then_inc(mlo_done, 1)

            def nxt(u, it=0, per=0):
                if per or u + 2 < UNITS:
                    lo(u + 2, it, per)

            def mod_cols(q0, it, step, nbody, nm):
                dve.wait_ge(mcol_mm, nbody + 1 + it)
                V.tensor_tensor(modv[:, bass.ds(it * step + q0, nm), :],
                                bank[7][:, 0:2 * nm].rearrange("p (i s) -> p i s", s=2),
                                bmod2[:, bass.ds(it * step + q0, nm), :], ALU.add).then_inc(mod_done, 1)

            V.memset(gate[:], 0.0).then_inc(gate_rdy, 1)
            V.memset(small[:, 32:33], 0.0).then_inc(prod_done, FREE)
            V.memset(small[:, 33:34], 0.0).then_inc(out_evac, FREE)
            V.memset(small[:, 34:35], 0.0).then_inc(mix_step, FREE_MIX)
            V.memset(small[:, 35:36], 0.0).then_inc(sig_done, FREE_MIX)
            V.memset(small[:, 36:37], 0.0).then_inc(lo_done, FREE_LO)
            dve.wait_ge(s4hi, 2)
            for s in range(2):
                V.tensor_tensor(S4[:, :, 2 * s + 1], cs[:, 8 * s:8 * s + 8], S4[:, :, 2 * s].bitcast(F32),
                                ALU.subtract).then_inc(s4lo, 1)
            mlo_first(0)
            mlo_first(1)
            def columns():
                dve.wait_ge(cols_done, 3)
                nfix = 0
                for l in range(DEPTH):
                    for s in range(2):
                        V.tensor_copy(bmod2[:, l * MODT:(l + 1) * MODT, s], vec[:, l, 0, 0:MODT]).then_inc(cols_fix, 1)
                        nfix += 1
                dve.wait_ge(cols_fix, nfix)
                for l in range(DEPTH):
                    v = bmod2[:, l * MODT:(l + 1) * MODT, :].rearrange("p (i k) s -> p i (k s)", i=3)
                    V.tensor_scalar(v[:, :, 16:32], v[:, :, 16:32], 1.0, None, ALU.add).then_inc(cols_fix, 1)
                    for r in (0, 24):
                        w = vec[:, l, 1, r:r + (24 if l < DEPTH - 1 else 16)]
                        V.tensor_scalar(w, w, ALPHA, None, ALU.mult).then_inc(cols_fix, 1)
                    nfix += 3
                dve.wait_ge(cols_fix, nfix)

            def sine_arg(l, i):
                b = col(l, ("hy_b1", "hy_b2")[i], 0, slice(0, FH))
                fr = col(l, "hy_f", i, slice(0, FH))
                dve.wait_ge(f_mm, FM * l + i + 1)
                c = FV * l + FS * i
                V.tensor_scalar(farg, bank[i][0:FH, 0:SEQ], b, fr, ALU.add, ALU.mult).then_inc(f_v, 1)
                dve.wait_ge(f_v, c + 1)
                V.tensor_scalar(fk, farg, 1.0 / TWO_PI, ROUND, ALU.mult, ALU.add).then_inc(f_v, 1)
                dve.wait_ge(f_v, c + 2)
                V.tensor_scalar(fk, fk, ROUND, -PI_HI, ALU.subtract, ALU.mult).then_inc(f_v, 1)
                dve.wait_ge(f_v, c + 3)
                V.tensor_tensor(farg, farg, fk, ALU.add).then_inc(f_v, 1)
                dve.wait_ge(f_v, c + 4)
                V.scalar_tensor_tensor(out=farg, in0=fk, scalar=PI_LO / PI_HI, in1=farg, op0=ALU.mult,
                                       op1=ALU.add).then_inc(f_v, 1)
                dve.wait_ge(f_v, c + 5)
                V.tensor_scalar(farg, farg, PI_IN, -PI_IN, ALU.min, ALU.max).then_inc(f_v, 1)

            def filters(l, step):
                c = FV * l + 2 * FS
                if step <= 2:
                    sine_arg(l, step - 1)
                elif step == 3:
                    for t in range(2):
                        for o in range(ORDER):
                            dve.wait_ge(f_mm, FM * l + 2 + 2 * t + o + 1)
                            dve.wait_ge(f_v, c)
                            V.tensor_tensor(filt[:, o, :, :], bank[2 + o][:].rearrange("p (r c) -> p r c", r=2),
                                            decay[:, t, :, :], ALU.mult).then_inc(f_v, 1)
                            c += 1
                            dve.wait_ge(f_v, c)
                            V.tensor_tensor(hp[:, t, o, :], filt[:, o, 0, :], filt[:, o, 1, :],
                                            ALU.add).then_inc(f_v, 1)
                            V.tensor_tensor(hm[:, t, o, :], filt[:, o, 0, :], filt[:, o, 1, :],
                                            ALU.subtract).then_inc(f_v, 1)
                            c += 2
                elif step == 4:
                    c += 12
                    dve.wait_ge(f_a, 5 * l + 4)
                    V.tensor_tensor(hsq[:, 0, :, :], hsq[:, 0, :, :], hsq[:, 1, :, :], ALU.add).then_inc(f_v, 1)
                    dve.wait_ge(f_v, c + 1)
                    V.tensor_tensor(hsq[:, 0, 0, :], hsq[:, 0, 0, :], hsq[:, 0, 1, :], ALU.add).then_inc(f_v, 1)
                    dve.wait_ge(f_mm, FM * l + 7)
                    V.tensor_scalar(fn, bank[1][:], 0.5, 1e-6, ALU.mult, ALU.add).then_inc(f_v, 1)
                    dve.wait_ge(f_a, 5 * (l + 1))
                    V.reciprocal(fn, fn).then_inc(f_v, 1)
                    dve.wait_ge(f_v, c + 4)
                else:
                    i = step - 5
                    for f in range(2):
                        dve.wait_ge(f_mm, FM * l + 8 + 2 * i + f)
                        V.tensor_tensor(spec[:, l, i, f, :, :].rearrange("p o c -> p (o c)"),
                                        bank[spec_bank(l, i, f)][:], fn, ALU.mult).then_inc(f_v, 1)

            for what, *x in SETUP:
                if what == "m" and x[0] + 2 < MOD_FIRST:
                    mlo_first(x[0] + 2)
                elif what == "v":
                    columns()
                elif what == "t":
                    mod_cols(4 * x[0], 0, 0, x[0], 4)
                elif what == "f":
                    filters(*x)
            lo(0)
            lo(1)
            for q in range(2):
                mlo(MOD_FIRST + q)

            def stats(n):
                part = slice(0, lnt(n) // 4)
                eps = LN_EPS if n % 2 else LN_EPS * ALPHA * ALPHA
                if n in (0, 3, 9):
                    if n:
                        dve.wait_ge(resid, 8 * (n // 2) + 1)
                    V.memset(rows_of, 0.0).then_inc(rows_zero, 1)
                    dve.wait_ge(rows_zero, (0, 3, 9).index(n) + 1)
                dve.wait_ge(stat_mm, 2 * n + 2)
                dve.wait_ge(stat_cp, n + 1)
                V.tensor_tensor(var[part], bank[1][part, 0:P], var[part], ALU.subtract).then_inc(stat_v, 1)
                dve.wait_ge(stat_v, 4 * n + 1)
                V.tensor_scalar(var[part], var[part], 0.0, eps, ALU.max, ALU.add).then_inc(stat_v, 1)
                dve.wait_ge(stat_sd, n + 1)
                V.reciprocal(rstd[part], var[part]).then_inc(stat_v, 1)
                dve.wait_ge(stat_v, 4 * n + 3)
                js = [(slice(32 * j, 32 * j + 1), slice(j * P, (j + 1) * P)) for j in range(lnt(n) // P)]
                for p, t in js:
                    i = V.tensor_copy(rows_of[p, 1, t], rstd[p])
                i.then_inc(stat_v, 1)

            def times_rstd(n, k):
                T = lnt(n)
                dve.wait_ge(t_sub, 8 * n + k + 1)
                V.tensor_tensor(Y[:, k, 0:T], Y[:, k, 0:T], bank[3][:, 0:T], ALU.mult).then_inc(t_mul, 1)

            def apply_post(n):
                T = lnt(n)

                def less_mean(k):
                    V.tensor_tensor(Y[:, k, 0:T], X[:, k, 0:T], bank[2][:, 0:T], ALU.subtract).then_inc(t_sub, 1)

                dve.wait_ge(stat_all, 2 * n + 1)
                less_mean(0)
                less_mean(1)
                dve.wait_ge(stat_all, 2 * n + 2)
                for k in range(KD):
                    if k + 2 < KD:
                        less_mean(k + 2)
                    times_rstd(n, k)

            def apply_mod(n):
                T, l, i = lnt(n), n // 6, (n % 6) // 2

                def low(k):
                    dve.wait_ge(h_hi, 4 * n + k + 1)
                    V.tensor_tensor(Hl[:, k, 0:T], Y[:, k, 0:T], Hh[:, k, 0:T].bitcast(F32),
                                    ALU.subtract).then_inc(h_lo, 1)

                dve.wait_ge(stat_all, 2 * n + 2)
                dve.wait_ge(mod_done, modbase((0, 1, 1, 2, 3, 3)[n // 2], "in", 0))
                for k in range(KD):
                    times_rstd(n, k)
                    if k >= 3:
                        low(k - 3)
                    if k in V_TILES:
                        dve.wait_ge(t_mul, 8 * n + k + 1)
                        for s in range(T // SEQ):
                            t = slice(s * SEQ, (s + 1) * SEQ)
                            q = l * MODT + 24 * i + k
                            h = V.tensor_scalar(Y[:, k, t], Y[:, k, t], modv[:, q + 8, s:s + 1],
                                                modv[:, q, s:s + 1], ALU.mult, ALU.add)
                        h.then_inc(h_fullv, 1)
                    if n == 0 and k == 4:
                        filters(DEPTH - 1, 5)
                for k in range(KD - 3, KD):
                    low(k)
                if n == 0:
                    filters(DEPTH - 1, 6)

            def hidden(f, c, x, it):
                T = ffn_tok(f)
                J = f * JF + sum(CHUNKS[:c]) + x
                dve.wait_ge(silu_done, J + 1 + it * 2)
                V.tensor_tensor(sq[x][:, 0:T], tt[x][:, 0:T], bank[2 * x][:, 0:T],
                                ALU.mult).then_inc(prod_done, 1)
                dve.wait_ge(u_hi, J + 1 + it * 2)
                V.tensor_tensor(Ul[:, bass.ds(it * 2 + x, 1), 0:T].rearrange("p o t -> p (o t)"),
                                sq[x][:, 0:T],
                                Uh[:, bass.ds(it * 2 + x, 1), 0:T].rearrange("p o t -> p (o t)").bitcast(F32),
                                ALU.subtract).then_inc(u_lo, 1)

            def partial(f, c, x, u, it):
                T = ffn_tok(f)
                dve.wait_ge(unit_done, u + 1 + it * 4)
                y = Y[:, bass.ds(it * 4 + x, 1), 0:T].rearrange("p o t -> p (o t)")
                if c == 0:
                    V.tensor_copy(y, bank[4 + x % 2][:, 0:T]).then_inc(out_evac, 1)
                else:
                    V.tensor_tensor(y, bank[4 + x % 2][:, 0:T], y, ALU.add).then_inc(out_evac, 1)

            def n_evac(n):
                l, sub = n // 6, (n % 6) // 2
                return 56 * l + (16, 24, 48)[sub]

            def tail(n, m, u, y):
                T = lnt(n)
                l = n // 6
                dve.wait_ge(unit_done, u + 1)
                if y is None:
                    V.tensor_scalar(tt[m % 2][:, 0:T], bank[4 + m % 2][:, 0:T], col(l, "b_out", m), None,
                                    ALU.add).then_inc(out_evac, 1)
                else:
                    V.tensor_tensor(tt[m % 2][:, 0:T], bank[4 + m % 2][:, 0:T], y, ALU.add).then_inc(out_evac, 1)
                dve.wait_ge(out_evac, FREE + n_evac(n) + m + 1)
                for s in range(T // SEQ):
                    t = slice(s * SEQ, (s + 1) * SEQ)
                    i = V.scalar_tensor_tensor(out=X[:, m, t], in0=tt[m % 2][:, t], scalar=gate[:, m, s:s + 1],
                                               in1=X[:, m, t], op0=ALU.mult, op1=ALU.add)
                i.then_inc(resid, 1)

            def set_gate(n, mod_bodies):
                l, sub = n // 6, (n % 6) // 2
                q = l * MODT + 24 * sub + 16
                dve.wait_ge(mod_done, mod_bodies)
                if n > 1:
                    dve.wait_ge(resid, 8 * (n // 2))
                V.tensor_scalar(gate[:], modv[:, q:q + 8, :], 1.0 if sub == 1 else 0.5, None,
                                ALU.mult).then_inc(gate_rdy, 1)
                dve.wait_ge(gate_rdy, n // 2 + 2)

            def ffn(f):
                l, s = f // 2, f % 2
                n = 6 * l + (1 if s == 0 else 5)
                for c, nj in enumerate(CHUNKS):
                    u0, q0, nm = AT["in", f, c], MODQ["in", f, c], MOD_IN[f][c]
                    nb_ = modbase(f, "in", c)

                    def in_body(it, ahead):
                        for kind, x, i in body_in(nm):
                            if kind == "m":
                                if ahead or x < 2:
                                    mlo(q0 + x + 2, it, 4)
                                continue
                            nxt(u0 + i, it, 4)
                            if kind == "g":
                                hidden(f, c, x, it)
                        if nm:
                            mod_cols(q0, it, 4, nb_, nm)

                    peel = mod_last(f, "in", c)
                    with dve.Fori(0, nj // 2 - peel) as it:
                        in_body(it, True)
                    if peel:
                        in_body(nj // 2 - 1, False)
                    u0, q0, nm = AT["out", f, c], MODQ["out", f, c], MOD_OUT[f][c]
                    nb_ = modbase(f, "out", c)

                    def out_body(it, last):
                        for kind, x, i in body_out(nm):
                            if kind == "m":
                                if not (last and it == 1):
                                    mlo(q0 + x + 2, it, 2)
                                continue
                            if last:
                                m = 4 * it + x
                                if m < KD - 1:
                                    nxt(u0 + m)
                                tail(n, m, u0 + m, Y[:, m, 0:ffn_tok(f)])
                                if m == KD - 1:
                                    nxt(u0 + m)
                            else:
                                nxt(u0 + i, it, 4)
                                partial(f, c, x, u0 + i, it)
                        if nm:
                            mod_cols(q0, it, 2, nb_, nm)

                    if c < len(CHUNKS) - 1:
                        with dve.Fori(0, 2) as it:
                            out_body(it, False)
                    else:
                        set_gate(n, nb_)
                        for it in range(2):
                            out_body(it, True)

            def mixer(l):
                S = streams(l)
                T = S * SEQ
                n = 6 * l + 3
                ct, ht, st = 2 * CONF_K * l, NHT * l, NST * l
                nw = N_WIN * l
                dve.wait_ge(h_lo, 24 * l + 16)
                for v, w, L in ((cpad, PADC, 2 * PADC + SEQ), (scpad, 1, SEQ + 2), (hvpad, 1, SEQ + 2)):
                    V.memset(v[:, :, :, 0:w], 0.0).then_inc(pads, 1)
                    V.memset(v[:, :, :, L - w:L], 0.0).then_inc(pads, 1)
                dve.wait_ge(pads, 6 * (l + 1))

                def conf_tap(j):
                    nonlocal ct
                    for i in range(BT):
                        src = cpad[:, i, 0:S, j:j + SEQ]
                        dst = cacc[:, i, 0:T].rearrange("p (s t) -> p s t", s=S)
                        w = col(l, "conf_w", BT * j + i)
                        if j == 0:
                            dve.wait_ge(cglu, 2 * (l + 1))
                            V.tensor_scalar(dst, src, w, col(l, "conf_b", i), ALU.mult, ALU.add).then_inc(ctap, 1)
                        else:
                            dve.wait_ge(ctap, ct - 1)
                            V.scalar_tensor_tensor(out=dst, in0=src, scalar=w, in1=dst, op0=ALU.mult,
                                                   op1=ALU.add).then_inc(ctap, 1)
                        ct += 1

                def hy_short(i):
                    nonlocal ht
                    dst = hvc[:, i, 0:T].rearrange("p (s t) -> p s t", s=S)
                    dve.wait_ge(win_evac, nw + 5 + i)
                    for j in range(3):
                        src = hvpad[:, i, 0:S, j:j + SEQ]
                        w = col(l, "hs_w", 6 * j + i)
                        if j == 0:
                            V.tensor_scalar(dst, src, w, col(l, "hs_b", i), ALU.mult, ALU.add).then_inc(htap, 1)
                        else:
                            dve.wait_ge(htap, ht)
                            V.scalar_tensor_tensor(out=dst, in0=src, scalar=w, in1=dst, op0=ALU.mult,
                                                   op1=ALU.add).then_inc(htap, 1)
                        ht += 1

                u0 = AT["win", l]
                tap = 0
                for i, m in enumerate(WIN_ORDER):
                    nxt(u0 + i)
                    if m in (2, 3):
                        dve.wait_ge(win_evac, nw + i + 1)
                        V.tensor_tensor(cpad[:, m - 2, 0:S, PADC:PADC + SEQ],
                                        tmpa[:, m - 2, 0:T].rearrange("p (s t) -> p s t", s=S),
                                        cacc[:, m - 2, 0:T].rearrange("p (s t) -> p s t", s=S),
                                        ALU.mult).then_inc(cglu, 1)
                    for _ in range(2):
                        if i >= 4 and tap < CONF_K:
                            conf_tap(tap)
                            tap += 1
                    if i == 5:
                        dve.wait_ge(btab_cp, 4 * (l + 1))
                    if 5 <= i < 11:
                        hy_short(i - 5)
                while tap < CONF_K:
                    conf_tap(tap)
                    tap += 1

                def short_conv(step):
                    nonlocal st
                    if step == 1:
                        dve.wait_ge(win_evac, nw + N_WIN)
                    if step < 3:
                        i = step - 1
                        v = scpad[:, i, 0:S, 1:SEQ + 1]
                        V.tensor_tensor(v, v, tmpa[:, i, 0:T].rearrange("p (s t) -> p s t", s=S),
                                        ALU.mult).then_inc(stap, 1)
                        st += 1
                        dst = tmpa[:, i, 0:T].rearrange("p (s t) -> p s t", s=S)
                        for j in range(3):
                            src = scpad[:, i, 0:S, j:j + SEQ]
                            w = col(l, "sc_w", BT * j + i)
                            dve.wait_ge(stap, st)
                            if j == 0:
                                V.tensor_scalar(dst, src, w, None, ALU.mult).then_inc(stap, 1)
                            else:
                                V.scalar_tensor_tensor(out=dst, in0=src, scalar=w, in1=dst, op0=ALU.mult,
                                                       op1=ALU.add).then_inc(stap, 1)
                            st += 1
                        return
                    for i in range(BT):
                        dve.wait_ge(stap, st)
                        V.tensor_tensor(tmpa[:, i, 0:T], tmpa[:, i, 0:T], sbb[:, i, 0:T], ALU.mult).then_inc(stap, 1)
                        st += 1

                def branch_lo(b, src, k):
                    dve.wait_ge(b_hi, 4 * l + k)
                    V.tensor_tensor(Bl[:, b, :, 0:T], src[:, :, 0:T], Bh[:, b, :, 0:T].bitcast(F32),
                                    ALU.subtract).then_inc(b_lo, 1)


                c0 = NCV * l

                def conformer(step):
                    if step == 2:
                        dve.wait_ge(c_mm, 2 * l + 2)
                        dve.wait_ge(c_cp, 2 * l + 2)
                        V.tensor_tensor(cvar[:, 0:T], bank[1][:, 0:T], cvar[:, 0:T], ALU.subtract).then_inc(c_v, 1)
                        dve.wait_ge(c_v, c0 + 1)
                        V.tensor_scalar(cvar[:, 0:T], cvar[:, 0:T], 0.0, LN_EPS, ALU.max, ALU.add).then_inc(c_v, 1)
                    elif step == 3:
                        dve.wait_ge(c_sd, l + 1)
                        V.reciprocal(cvar[:, 0:T], cvar[:, 0:T]).then_inc(c_v, 1)
                        dve.wait_ge(c_v, c0 + 3)
                        V.tensor_tensor(cmean[:, 0:T], cmean[:, 0:T], cvar[:, 0:T], ALU.mult).then_inc(c_v, 1)
                    elif step == 4:
                        dve.wait_ge(c_v, c0 + 4)
                        for i in range(BT):
                            V.tensor_tensor(cacc[:, i, 0:T], cacc[:, i, 0:T], cvar[:, 0:T],
                                            ALU.mult).then_inc(c_v, 1)
                            dve.wait_ge(c_v, c0 + 5 + 2 * i)
                            V.tensor_tensor(cacc[:, i, 0:T], cacc[:, i, 0:T], cmean[:, 0:T],
                                            ALU.subtract).then_inc(c_v, 1)

                bl = blocks(l)
                nb = len(bl)
                g0 = NB0 * l

                def score_steps(n):
                    return AV0 * l + sum(2 if b[0] == 0 else 1 for b in bl[:n + 1])

                def attention(n):
                    if n < nb:
                        s, h, q = bl[n]
                        r = n % 2
                        dve.wait_ge(at_s, g0 + n + 1)
                        if n >= 2:
                            dve.wait_ge(at_e, g0 + n - 1)
                        if s == 0:
                            V.scalar_tensor_tensor(out=sbuf_s[r][:, 0:SEQ], in0=bank[4 + r][:, 0:SEQ], scalar=SCALE,
                                                   in1=btab[:, q, h, :, :].rearrange("p r c -> p (r c)"),
                                                   op0=ALU.mult, op1=ALU.add).then_inc(at_v, 1)
                            V.tensor_scalar(sbuf_s[r][:, SEQ:TOK], bank[4 + r][:, SEQ:TOK], SCALE, None,
                                            ALU.mult).then_inc(at_v, 1)
                            K = TOK
                        else:
                            V.tensor_scalar(sbuf_s[r][:, 0:SEQ], bank[4 + r][:, 0:SEQ], SCALE, None,
                                            ALU.mult).then_inc(at_v, 1)
                            K = SEQ
                        dve.wait_ge(at_v, score_steps(n))
                        V.tensor_reduce(out=nmax[:, r:r + 1], in_=sbuf_s[r][:, 0:K], axis=AX.X, op=ALU.max,
                                        negate=True).then_inc(at_m, 1)
                    m = n - 1
                    if 0 <= m < nb:
                        r = m % 2
                        K = TOK if bl[m][0] == 0 else SEQ
                        dve.wait_ge(at_e, g0 + m + 1)
                        V.reciprocal(prec[:, r:r + 1], psumr[:, r:r + 1]).then_inc(at_r, 1)
                        dve.wait_ge(at_r, g0 + m + 1)
                        V.tensor_scalar(sbuf_p[r][:, 0:K], sbuf_p[r][:, 0:K], prec[:, r:r + 1], None,
                                        ALU.mult).then_inc(at_n, 1)

                def hyena(o, step):
                    N = S * WB
                    e = ORDER * l + o

                    def v3(x):
                        return x[:, 0:N].rearrange("p (s c) -> p s c", s=S)

                    if step in (3, 4):
                        f = step - 3
                        pc = 12 * e + 6 * f
                        kr = spec[:, l, 0, f, o, :].unsqueeze(1).to_broadcast([P, S, WB])
                        ks = spec[:, l, 1, f, o, :].unsqueeze(1).to_broadcast([P, S, WB])
                        dve.wait_ge(hy_f, 4 * e + 2 * f + 2)
                        for out_, x0, k0, x1, k1, op in ((0, f, kr, 2 + f, ks, ALU.subtract),
                                                         (1, f, ks, 2 + f, kr, ALU.add)):
                            if pc:
                                dve.wait_ge(hy_p, pc)
                            V.tensor_tensor(v3(hprod[0]), v3(bank[x0][:, :]), k0, ALU.mult).then_inc(hy_p, 1)
                            V.tensor_tensor(v3(hprod[1]), v3(bank[x1][:, :]), k1, ALU.mult).then_inc(hy_p, 1)
                            pc += 2
                            dve.wait_ge(hy_p, pc)
                            V.tensor_tensor(ysp[:, out_, f, 0:N], hprod[0][:, 0:N], hprod[1][:, 0:N],
                                            op).then_inc(hy_p, 1)
                            pc += 1
                    elif step == 6:
                        zc = 4 * e
                        for i in range(BT):
                            dve.wait_ge(hy_i, 2 * e + i + 1)
                            V.scalar_tensor_tensor(out=hvc[:, i, 0:T], in0=hvc[:, i, 0:T],
                                                   scalar=col(l, "hy_bias", BT * o + i), in1=bank[i][:, 0:T],
                                                   op0=ALU.mult, op1=ALU.add).then_inc(hy_z, 1)
                            zc += 1
                            dve.wait_ge(hy_z, zc)
                            V.tensor_tensor(hvc[:, i, 0:T], hvc[:, i, 0:T], hvc[:, BT * (1 + o) + i, 0:T],
                                            ALU.mult).then_inc(hy_z, 1)
                            zc += 1

                dve.wait_ge(htap, NHT * (l + 1))
                for what, *x in branch_steps(l):
                    if what == "c":
                        conformer(*x)
                    elif what == "h":
                        hyena(*x)
                    elif what == "a":
                        attention(*x)
                    elif what == "s":
                        short_conv(*x)
                    else:
                        branch_lo(x[0], {0: cacc, 1: obuf, 2: tmpa, 3: hvc[:, 0:BT, :]}[x[0]], x[1])
                u0 = AT["gate", l]
                with dve.Fori(0, KD // 2) as it:
                    for d in range(2):
                        base = mix_at(l, d)
                        for i, b in enumerate((0, 1, None, 2, 3)):
                            u = u0 + 5 * d + i
                            nxt(u, it, 10)
                            for b in {2: (0, 1), 3: (2,), 4: (3,)}.get(i, ()):
                                dve.wait_ge(sig_done, FREE_MIX + 32 * l + 4 * d + b + 1 + it * 8)
                                if b == 0:
                                    dve.wait_ge(unit_done, u0 + 5 * d + 3 + it * 10)
                                    V.tensor_tensor(acc1[:, 0:T], tt[0][:, 0:T], bank[0][:, 0:T],
                                                    ALU.mult).then_inc(mix_step, 1)
                                    continue
                                dve.wait_ge(mix_step, base + 2 * b - 1 + it * 14)
                                V.tensor_tensor(acc2[:, 0:T], tt[b % 2][:, 0:T], bank[b][:, 0:T],
                                                ALU.mult).then_inc(mix_step, 1)
                                dve.wait_ge(mix_step, base + 2 * b + it * 14)
                                V.tensor_tensor(acc1[:, 0:T], acc1[:, 0:T], acc2[:, 0:T],
                                                ALU.add).then_inc(mix_step, 1)
                        dve.wait_ge(m_hi, 8 * l + d + 1 + it * 2)
                        V.tensor_tensor(Ul[:, bass.ds(it * 2 + d, 1), 0:T].rearrange("p o t -> p (o t)"),
                                        acc1[:, 0:T],
                                        Uh[:, bass.ds(it * 2 + d, 1), 0:T].rearrange("p o t -> p (o t)").bitcast(F32),
                                        ALU.subtract).then_inc(m_lo, 1)
                set_gate(n, modbase(2 * l + 1, "in", 0))
                u0 = AT["wout", l]
                for m in range(KD):
                    if m < KD - 1:
                        nxt(u0 + m)
                    tail(n, m, u0 + m, None)
                    if m == KD - 1:
                        nxt(u0 + m)

            stats(0)
            apply_mod(0)
            for l in range(DEPTH):
                for sub in range(3):
                    n = 6 * l + 2 * sub + 1
                    if sub == 1:
                        mixer(l)
                    else:
                        ffn(2 * l + sub // 2)
                    if n in (3, 5):
                        for i in range(2):
                            mlo(MODQ["in", n // 2, 0] + i)
                    stats(n)
                    apply_post(n)
                    if n < NLN - 1:
                        stats(n + 1)
                        apply_mod(n + 1)

        @block.tensor
        def _(pe):
            T_ = nc.tensor

            def split3(o, k, s, xh, xl, first, last):
                T_.matmul(o, wh[s][:, k, :], xh, start=first, stop=False)
                T_.matmul(o, wh[s][:, k, :], xl, start=False, stop=False)
                return T_.matmul(o, wl[s][:, k, :], xh, start=False, stop=last)

            def split_in(u, k, it=0, per=0):
                if k in (0, KD // 2):
                    pe.wait_ge(lo_done, FREE_LO + 2 * u + 1 + k // (KD // 2) + it * (2 * per))

            def mod_unit(q, x, it=0, step=0):
                pe.wait_ge(mlo_done, q + 1 + it * step)
                o = bank[6][0:4, x * P:(x + 1) * P]
                for k in range(KD):
                    T_.matmul(o, S4[:, k, :], mwh[q % 2][:, k, :], start=(k == 0), stop=False)
                    i = T_.matmul(o, S4[:, k, :], mwl[q % 2][:, k, :], start=False, stop=(k == KD - 1))
                i.then_inc(munit_done, 1)

            def mod_turn(nbody, nm, it=0):
                pe.wait_ge(mrow_done, nbody + 1 + it)
                if nbody:
                    pe.wait_ge(mod_done, nbody + it)
                for x in range(nm):
                    i = T_.matmul(bank[7][:, 2 * x:2 * x + 2], modrow[:, x, :], sel[:], start=True, stop=True)
                i.then_inc(mcol_mm, 1)

            pe.wait_ge(s_c, 48)
            T_.transpose(bank[2][:, 0:16], crow, ident[0:16, 0:16]).then_inc(turned, 1)
            pe.wait_ge(s4hi, 2)
            pe.wait_ge(s4lo, 2)

            def turn_x():
                pe.wait_ge(s_xin, 64)
                for k in range(KD):
                    if k >= 2:
                        pe.wait_ge(x_tile, k - 1)
                    for t in range(4):
                        i = T_.transpose(bank[4 + k % 2][:, t * P:(t + 1) * P], xrow[:, t, k * P:(k + 1) * P], ident)
                    i.then_inc(x_turned, 1)

            def turn_vectors():
                pe.wait_ge(s_vec, 16 * N_VEC)
                pe.wait_ge(s_const, 16 * N_CONST)
                for l in range(DEPTH):
                    for g in range(NG):
                        i = T_.transpose(bank[l][:, g * P:(g + 1) * P], vrow[:, l, g, :], ident)
                    i.then_inc(turned, 1)

            def filters(l, step):
                if step == 1:
                    pe.wait_ge(cols_fix, 10)
                    if l:
                        pe.wait_ge(f_v, FV * l)
                    T_.matmul(bank[0][0:FH, 0:SEQ], fw1[:, l, :], zT, start=True, stop=True).then_inc(f_mm, 1)
                elif step == 2:
                    pe.wait_ge(f_a, 5 * l + 1)
                    T_.matmul(bank[1][0:FH, 0:SEQ], fw2[:, l, :], fh, start=True, stop=True).then_inc(f_mm, 1)
                elif step == 3:
                    pe.wait_ge(f_a, 5 * l + 2)
                    for t in range(2):
                        for o in range(ORDER):
                            if t:
                                pe.wait_ge(f_v, FV * l + 2 * FS + 3 * o + 1)
                            T_.matmul(bank[2 + o][:], fh[:, t * P:(t + 1) * P], fw3[:, l, o * 512:(o + 1) * 512],
                                      start=True, stop=True).then_inc(f_mm, 1)
                elif step == 4:
                    pe.wait_ge(f_v, FV * l + 2 * FS + 14)
                    T_.matmul(bank[1][:], ones, hsq[:, 0, 0, :], start=True, stop=True).then_inc(f_mm, 1)
                else:
                    i = step - 5
                    pe.wait_ge(f_v, FV * l + 2 * FS + 15)
                    if i and l == DEPTH - 1:
                        pe.wait_ge(f_v, FV * l + FV - 2)
                    for f in range(2):
                        for t in range(2):
                            m = T_.matmul(bank[spec_bank(l, i, f)][:], dft[:, i, t, f * P:(f + 1) * P],
                                          (hp, hm)[i][:, t, :, :].rearrange("p o c -> p (o c)"),
                                          start=(t == 0), stop=(t == 1))
                        m.then_inc(f_mm, 1)

            for what, *x in SETUP:
                if what == "m":
                    mod_unit(x[0], x[0] % 4)
                elif what == "t":
                    mod_turn(x[0], 4)
                elif what == "x":
                    turn_x()
                elif what == "v":
                    turn_vectors()
                elif what == "f":
                    filters(*x)

            def mean_of(b, x, T, first, last):
                for j in range(T // P):
                    m = T_.matmul(bank[b][32 * j:32 * j + 32, 0:P], invD[:, 0:32], x[:, j * P:(j + 1) * P],
                                  start=first, stop=last)
                return m

            def to_all(n):
                T = lnt(n)
                pe.wait_ge(stat_rows, n + 1)
                T_.matmul(bank[2][:, 0:T], ones, rows_of[:, 0, 0:T], start=True, stop=True).then_inc(stat_all, 1)
                pe.wait_ge(stat_v, 4 * n + 4)
                T_.matmul(bank[3][:, 0:T], ones, rows_of[:, 1, 0:T], start=True, stop=True).then_inc(stat_all, 1)

            def stats_direct(n):
                T = lnt(n)
                if n == 0:
                    pe.wait_ge(f_v, FV * DEPTH - 5)
                for k in range(KD):
                    pe.wait_ge(x_tile, 8 * (n // 2) + k + 1)
                    m = mean_of(0, X[:, k, :], T, k == 0, k == KD - 1)
                m.then_inc(stat_mm, 1)
                if n:
                    for k in range(KSUM, KD):
                        pe.wait_ge(sq_tile, 8 * n + k + 1)
                        mean_of(1, Y[:, k, :], T, k == KSUM, False)
                pe.wait_ge(acc_step, acc_at(n // 2))
                mean_of(1, acc2, T, n == 0, True).then_inc(stat_mm, 1)
                to_all(n)

            def stats_sums(n):
                T = lnt(n)
                pe.wait_ge(acc_step, acc_at(n // 2) + 2 * KSUM_X - 1)
                mean_of(0, acc1, T, True, False)
                pe.wait_ge(resid, 8 * (n // 2) + KD)
                mean_of(0, X[:, KSUM_X, :], T, False, True).then_inc(stat_mm, 1)
                pe.wait_ge(acc_step, acc_at(n // 2) + 2 * KSUM_X)
                mean_of(1, acc2, T, True, False)
                pe.wait_ge(sq_tile, 8 * n + KD)
                mean_of(1, sq[KSUM_X % 2], T, False, True).then_inc(stat_mm, 1)
                to_all(n)

            def ffn(f):
                T = ffn_tok(f)
                l, s = f // 2, f % 2
                n = 6 * l + (0 if s == 0 else 4)
                for c, nj in enumerate(CHUNKS):
                    J0 = f * JF + sum(CHUNKS[:c])
                    u0, q0, nm = AT["in", f, c], MODQ["in", f, c], MOD_IN[f][c]
                    body = body_in(nm)
                    nb_ = modbase(f, "in", c)
                    with pe.Fori(0, nj // 2) as it:
                        first_main = True
                        for kind, x, i in body:
                            u = u0 + i
                            if kind == "m":
                                mod_unit(q0 + x, x, it, 4)
                                continue
                            if kind == "a":
                                pe.wait_ge(prod_done, FREE + J0 + x - 1 + it * 2)
                            o = bank[2 * x + (kind == "g")][:, 0:T]
                            for k in range(KD):
                                split_in(u, k, it, 4)
                                if c == 0 and first_main:
                                    pe.wait_ge(h_lo, 4 * n + k + 1)
                                m = split3(o, k, u % 2, Hh[:, k, 0:T], Hl[:, k, 0:T], k == 0, k == KD - 1)
                            first_main = False
                            m.then_inc(unit_done, 1)
                        if nm:
                            mod_turn(nb_, nm, it)
                    u0, q0, nm = AT["out", f, c], MODQ["out", f, c], MOD_OUT[f][c]
                    body = body_out(nm)
                    nb_ = modbase(f, "out", c)
                    ev = n_evac_pe(f, c)

                    with pe.Fori(0, 2) as it:
                        for kind, x, i in body:
                            u = u0 + i
                            if kind == "m":
                                mod_unit(q0 + x, x, it, 2)
                                continue
                            pe.wait_ge(out_evac, FREE + ev + x - 1 + it * 4)
                            for k in range(nj):
                                split_in(u, k, it, 4)
                                if x == 0:
                                    pe.wait_ge(u_lo, J0 + k + 1)
                                m = split3(bank[4 + x % 2][:, 0:T], k, u % 2, Uh[:, k, 0:T], Ul[:, k, 0:T],
                                           k == 0, k == nj - 1)
                            m.then_inc(unit_done, 1)
                        if nm:
                            mod_turn(nb_, nm, it)

            def n_evac_pe(f, c):
                return 56 * (f // 2) + (32 if f % 2 else 0) + 8 * c

            def mixer(l):
                S = streams(l)
                T = S * SEQ
                n = 6 * l + 2
                u0 = AT["win", l]
                nw = N_WIN * l
                for i, m in enumerate(WIN_ORDER):
                    u = u0 + i
                    if i >= 4:
                        pe.wait_ge(win_evac, nw + i - 3)
                    TT = win_tokens(l, m)
                    if 8 <= m < 10:
                        split_in(u, KD // 2)
                        for t in range(4):
                            o = bank[i % 4][:, t * P:(t + 1) * P]
                            tk = slice(t * P, (t + 1) * P)
                            for k in range(KD):
                                T_.matmul(o, Hh[:, k, tk], wh[u % 2][:, k, :], start=(k == 0), stop=False)
                                T_.matmul(o, Hh[:, k, tk], wl[u % 2][:, k, :], start=False, stop=False)
                                mm = T_.matmul(o, Hl[:, k, tk], wh[u % 2][:, k, :], start=False, stop=(k == KD - 1))
                    else:
                        for k in range(KD):
                            split_in(u, k)
                            if i == 0:
                                pe.wait_ge(h_lo, 4 * n + k + 1)
                            mm = split3(bank[i % 4][:, 0:TT], k, u % 2, Hh[:, k, 0:TT], Hl[:, k, 0:TT], k == 0,
                                        k == KD - 1)
                    mm.then_inc(unit_done, 1)
                    if i == 2:
                        pe.wait_ge(r_mask, 8 * (l + 1))
                        for q in range(2):
                            for h2 in range(2):
                                T_.matmul(bank[4 + 2 * q + h2][:], flip[:],
                                          rtab[:, q, 2 * h2:2 * h2 + 2, :, :].rearrange("p h r c -> p (h r c)"),
                                          start=True, stop=True).then_inc(flipped, 1)
                def conformer(step):
                    if step == 1:
                        pe.wait_ge(ctap, 2 * CONF_K * (l + 1))
                        for i in range(BT):
                            mm = T_.matmul(bank[0][:, 0:T], invB, cacc[:, i, 0:T], start=(i == 0),
                                           stop=(i == BT - 1))
                        mm.then_inc(c_mm, 1)
                    elif step == 2:
                        pe.wait_ge(c_sq, l + 1)
                        for i in range(BT):
                            mm = T_.matmul(bank[1][:, 0:T], invB, csq[:, i, 0:T], start=(i == 0),
                                           stop=(i == BT - 1))
                        mm.then_inc(c_mm, 1)

                bl = blocks(l)
                nb = len(bl)
                g0 = NB0 * l

                def score_steps(n):
                    return AV0 * l + sum(2 if b[0] == 0 else 1 for b in bl[:n + 1])

                def attention(n):
                    if n < nb:
                        s, h, q = bl[n]
                        rr = slice(DH * (h % 2), DH * (h % 2) + DH)
                        qs = qk[rr, h // 2, s * SEQ + q * P:s * SEQ + (q + 1) * P]
                        if s == 0:
                            ks, K = qk[rr, 2 + h // 2, 0:TOK], TOK
                        else:
                            ks, K = qk[rr, 2 + h // 2, SEQ:TOK], SEQ
                        if n >= 2:
                            pe.wait_ge(at_v, score_steps(n - 2))
                        T_.matmul(bank[4 + n % 2][:, 0:K], qs, ks, start=True, stop=True).then_inc(at_s, 1)
                    m = n - 2
                    if 0 <= m < nb:
                        kt = 4 if bl[m][0] == 0 else 2
                        pe.wait_ge(at_n, g0 + m + 1)
                        if m:
                            pe.wait_ge(at_tc, g0 + m)
                        for k in range(kt):
                            mm = T_.transpose(bank[6][:, k * P:(k + 1) * P], sbuf_p[m % 2][:, k * P:(k + 1) * P], ident)
                        mm.then_inc(at_t, 1)
                    m = n - 3
                    if 0 <= m < nb:
                        s, h, q = bl[m]
                        kt = 4 if s == 0 else 2
                        rr = slice(DH * (h % 2), DH * (h % 2) + DH)
                        pe.wait_ge(at_tc, g0 + m + 1)
                        if m:
                            pe.wait_ge(at_oc, g0 + m)
                        for k in range(kt):
                            mm = T_.matmul(bank[7][rr, 0:P],
                                           vtok[:, 2 * s + k, h * DH:(h + 1) * DH], sbuf_pT[m % 2][:, k, :],
                                           start=(k == 0), stop=(k == kt - 1))
                        mm.then_inc(at_o, 1)

                def hyena(o, step):
                    N = S * WB
                    e = ORDER * l + o
                    if step == 1:
                        if o:
                            pe.wait_ge(hy_z, 4 * e)
                        else:
                            pe.wait_ge(htap, NHT * (l + 1))
                            pe.wait_ge(c_v, NCV * l + 1)
                        for t in range(2):
                            for s in range(S):
                                for i in range(BT):
                                    mm = T_.transpose(bank[t][:, s * WB + i * P:s * WB + (i + 1) * P],
                                                      hvc[:, i, s * SEQ + t * P:s * SEQ + (t + 1) * P], ident)
                            mm.then_inc(hy_t, 1)
                    elif step in (2, 3):
                        f = step - 2
                        pe.wait_ge(hy_tc, 2 * e + 2)
                        for r in range(2):
                            for t in range(2):
                                mm = T_.matmul(bank[2 * r + f][:, 0:N], dft[:, r, t, f * P:(f + 1) * P],
                                               uT[:, t, 0:N], start=(t == 0), stop=(t == 1))
                            mm.then_inc(hy_f, 1)
                    elif step == 5:
                        pe.wait_ge(hy_p, 12 * (e + 1))
                        for i in range(BT):
                            for s in range(S):
                                for f in range(2):
                                    for r in range(2):
                                        mm = T_.matmul(bank[i][:, s * SEQ:(s + 1) * SEQ],
                                                       ysp[:, r, f, s * WB + i * P:s * WB + (i + 1) * P],
                                                       dft[:, 2 + r, f, :], start=(f == 0 and r == 0),
                                                       stop=(f == 1 and r == 1))
                            mm.then_inc(hy_i, 1)

                pe.wait_ge(win_evac, N_WIN * (l + 1))
                pe.wait_ge(btab_cp, 4 * (l + 1))
                for what, *x in branch_steps(l):
                    if what == "c":
                        conformer(*x)
                    elif what == "h":
                        hyena(*x)
                    elif what == "a":
                        attention(*x)
                u0 = AT["gate", l]
                pe.wait_ge(at_oc, g0 + nb)

                def gate_unit(u, b, it, per):
                    for k in range(KD):
                        split_in(u, k, it, per)
                        mm = split3(bank[4 + b][:, 0:T], k, u % 2, Hh[:, k, 0:T], Hl[:, k, 0:T], k == 0, k == KD - 1)
                    mm.then_inc(unit_done, 1)

                with pe.Fori(0, KD // 2) as it:
                    for d in range(2):
                        for i, b in enumerate((0, 1, None, 2, 3)):
                            u = u0 + 5 * d + i
                            if b is not None:
                                pe.wait_ge(sig_done, FREE_MIX + 32 * l + 4 * d + b - 3 + it * 8)
                                gate_unit(u, b, it, 10)
                                continue
                            pe.wait_ge(b_lo, 4 * (l + 1))
                            pe.wait_ge(mix_step, mix_at(l, d) + it * 14)
                            for b4 in range(4):
                                for k in range(BT):
                                    split_in(u, 2 * b4 + k, it, 10)
                                    mm = split3(bank[b4][:, 0:T], 2 * b4 + k, u % 2, Bh[:, b4, k, 0:T],
                                                Bl[:, b4, k, 0:T], k == 0, k == BT - 1)
                            mm.then_inc(unit_done, 1)
                u0 = AT["wout", l]
                ev = 56 * l + 24
                for m in range(KD):
                    pe.wait_ge(out_evac, FREE + ev + m - 1)
                    for k in range(KD):
                        split_in(u0 + m, k)
                        if m == 0:
                            pe.wait_ge(m_lo, 8 * l + k + 1)
                        mm = split3(bank[4 + m % 2][:, 0:T], k, (u0 + m) % 2, Uh[:, k, 0:T], Ul[:, k, 0:T],
                                    k == 0, k == KD - 1)
                    mm.then_inc(unit_done, 1)

            stats_direct(0)
            filters(DEPTH - 1, 5)
            filters(DEPTH - 1, 6)
            for l in range(DEPTH):
                for sub in range(3):
                    n = 6 * l + 2 * sub + 1
                    if sub == 1:
                        mixer(l)
                    else:
                        ffn(2 * l + sub // 2)
                    stats_sums(n)
                    if n < NLN - 1:
                        stats_direct(n + 1)
            for i in range(4):
                t, half = i // 2, i % 2
                for k in range(4):
                    pe.wait_ge(x_tile, 8 * (NLN // 2) + 4 * half + k + 1)
                    mm = T_.transpose(bank[4 + i][:, k * P:(k + 1) * P], X[:, 4 * half + k, t * P:(t + 1) * P], ident)
                mm.then_inc(o_turn, 1)


def _tables():
    f32 = np.float32
    eye = np.eye(P, dtype=f32)
    mats = np.stack([eye, np.full((P, P), 1.0 / D, f32), np.full((P, P), 1.0 / WB, f32), np.ones((P, P), f32)], 1)
    sel = np.array([[1, 0], [1, 0], [0, 1], [0, 1]], f32)
    flip = np.zeros((P, P), f32)
    for p in range(P):
        flip[p, (p // GRID_W) * GRID_W + GRID_W - 1 - p % GRID_W] = 1.0
    t = np.arange(SEQ, dtype=np.float64)
    ang = np.outer(t, (t + 0.5) * 2 * np.pi / (2 * SEQ))
    dft = np.stack([np.cos(ang), np.sin(ang), np.cos(ang).T / SEQ, np.sin(ang).T / SEQ])
    dft = dft.reshape(4, 2, P, SEQ).transpose(2, 0, 1, 3).astype(f32)
    tf = np.arange(SEQ, dtype=f32)
    t_norm = tf / f32(SEQ - 1)
    deltas = np.linspace(math.log(1e-2) / 1.5, math.log(1e-2) / 0.3, WB, dtype=f32)
    dec = np.exp(-t_norm[:, None] * np.abs(deltas)[None, :]).astype(f32)
    back = dec.copy()
    back[0] = 0.0
    decay = np.stack([dec, back], 1).reshape(2, P, 2, WB).transpose(1, 0, 2, 3)
    bands = np.linspace(1e-4, 15, 16, dtype=f32)
    a = (f32(2.0 * math.pi / SEQ) * tf[:, None]) * bands[None, :]
    zT = np.concatenate([t_norm[:, None], np.cos(a), -np.sin(a)], -1).astype(f32).T
    return {"k_mats": mats, "k_sel": sel, "k_flip": flip, "k_dft": dft, "k_decay": decay, "k_zT": zT}


_INS = ("x", "c", "ctx", "c_ctx", "w_mod", "b_mod", "post_ln_g", "post_ln_b", "ffn_w_in", "ffn_w_out", "w_in", "b_in",
        "conf_dw_w", "conf_dw_b", "conf_ln_g", "conf_ln_b", "conf_w_proj", "na_rpb", "na_w_proj", "sc_conv_w",
        "sc_w_proj", "hy_sconv_w", "hy_sconv_b", "hy_w1", "hy_b1", "hy_w2", "hy_b2", "hy_freq", "hy_w3", "hy_bias",
        "hy_w_proj", "w_out", "b_out")


def kernel(**inputs):
    import concourse.bacc as bacc
    from concourse.bass_utils import run_bass_kernel_spmd as run

    nc = bacc.Bacc("TRN2", target_bir_lowering=False, num_devices=1)
    arrays, aps = {}, {}
    for name, arr in [(n, inputs[n]) for n in _INS] + list(_tables().items()):
        arr = np.ascontiguousarray(arr)
        arrays["in_" + name] = arr
        aps[name] = nc.dram_tensor("in_" + name, arr.shape, mybir.dt.from_np(arr.dtype), kind="ExternalInput").ap()
    out = nc.dram_tensor("out", (1, SEQ, D), F32, kind="ExternalOutput").ap()
    build(nc, aps, out)
    return run(nc, [arrays], core_ids=[0]).results[0]["out"]
```
